# Optimizing a Trainium2 kernel written in Bass

```python
import math
import jax, jax.numpy as jnp
from jax import lax
import numpy as np

D_MODEL = 1024
BATCH = 1
SEQ = 1024
DEPTH = 1
DEC_BATCH = 8
DEC_SEQ = 8
PAST_LEN = 2048
PAGE_SIZE = 128

D_SSM = D_MODEL // 2
SSM_GROUP = 16
N_SSM_GROUPS = D_SSM // SSM_GROUP
SSM_STATE = 64
D_ATT = D_MODEL - D_SSM
HEAD_DIM = 64
N_HEADS = D_ATT // HEAD_DIM
N_KV_HEADS = 4
Q_PER_KV = N_HEADS // N_KV_HEADS
N_IDX_HEADS = 4
IDX_DIM = 64
TOPK_KEYS = 256
Q_BLOCK = 128
N_EXPERTS = 64
TOP_K_EXPERTS = 6
D_EXPERT = 256
ROUTED_SCALE = 2.5
MOE_BLOCK = 128
ALPHA = (2 * DEPTH) ** 0.25
BETA = (8 * DEPTH) ** -0.25
LN_EPS = 1e-5
DT_MIN = 1e-3
DT_MAX = 1e-1
IN_SIZES = (D_SSM, N_HEADS * HEAD_DIM, N_KV_HEADS * HEAD_DIM, N_KV_HEADS * HEAD_DIM,
            N_IDX_HEADS * IDX_DIM, IDX_DIM, N_IDX_HEADS)

kernel_name = 'hymba_s5_dsa_moe_decode_step'

def _layer_norm(x, g, b):
    xf = x.astype(jnp.float32)
    mu = jnp.mean(xf, -1, keepdims=True)
    var = jnp.mean(jnp.square(xf - mu), -1, keepdims=True)
    return ((xf - mu) * lax.rsqrt(var + LN_EPS)).astype(x.dtype) * g + b

def _rms_norm(x, g):
    xf = x.astype(jnp.float32)
    return (xf * lax.rsqrt(jnp.mean(jnp.square(xf), -1, keepdims=True) + LN_EPS)).astype(x.dtype) * g

def _swiglu(x, w1, w3, w2):
    return (jax.nn.silu(x @ w1) * (x @ w3)) @ w2

def _input_projection(h, w_in):
    b, t, _ = h.shape
    cuts = np.cumsum(IN_SIZES)[:-1].tolist()
    u, q, k, v, qi, ki, wi = jnp.split(h @ w_in, cuts, axis=-1)
    return (u,
            q.reshape(b, t, N_HEADS, HEAD_DIM),
            k.reshape(b, t, N_KV_HEADS, HEAD_DIM),
            v.reshape(b, t, N_KV_HEADS, HEAD_DIM),
            qi.reshape(b, t, N_IDX_HEADS, IDX_DIM),
            ki,
            wi)

def _ssm_discretise(a_re, a_im, log_dt, b_re, b_im):
    f32 = jnp.float32
    ar, ai = a_re.astype(f32), a_im.astype(f32)
    dt = jnp.exp(log_dt.astype(f32))[:, None]
    mag = jnp.exp(dt * ar)
    abr, abi = mag * jnp.cos(dt * ai), mag * jnp.sin(dt * ai)
    den = ar * ar + ai * ai
    nr, ni = abr - 1.0, abi
    fr = (nr * ar + ni * ai) / den
    fi = (ni * ar - nr * ai) / den
    br, bi = b_re.astype(f32), b_im.astype(f32)
    bbr = fr[..., None] * br - fi[..., None] * bi
    bbi = fr[..., None] * bi + fi[..., None] * br
    return abr, abi, bbr, bbi

def _ssm_combine(e1, e2):
    a1r, a1i, b1r, b1i = e1
    a2r, a2i, b2r, b2i = e2
    return (a2r * a1r - a2i * a1i,
            a2r * a1i + a2i * a1r,
            a2r * b1r - a2i * b1i + b2r,
            a2r * b1i + a2i * b1r + b2i)

def _s5_group(u, h0_re, h0_im, abr, abi, bbr, bbi, c_re, c_im, d_skip, w_glu, b_glu):
    b, t, _ = u.shape
    f32 = jnp.float32
    uf = u.astype(f32).reshape(b, t, N_SSM_GROUPS, SSM_GROUP)
    bu_r = jnp.einsum('btgi,gpi->btgp', uf, bbr)
    bu_i = jnp.einsum('btgi,gpi->btgp', uf, bbi)
    a_r = jnp.broadcast_to(abr, bu_r.shape)
    a_i = jnp.broadcast_to(abi, bu_r.shape)
    pr, pi_, hr, hi = lax.associative_scan(_ssm_combine, (a_r, a_i, bu_r, bu_i), axis=1)
    if h0_re is not None:
        s_r = h0_re.astype(f32)[:, None]
        s_i = h0_im.astype(f32)[:, None]
        hr = hr + pr * s_r - pi_ * s_i
        hi = hi + pr * s_i + pi_ * s_r
    y = (jnp.einsum('btgp,gip->btgi', hr, c_re.astype(f32))
         - jnp.einsum('btgp,gip->btgi', hi, c_im.astype(f32)))
    y = (y + d_skip.astype(f32).reshape(N_SSM_GROUPS, SSM_GROUP) * uf).reshape(b, t, D_SSM)
    g = jax.nn.gelu(y.astype(u.dtype))
    out = g * jax.nn.sigmoid(g @ w_glu + b_glu)
    return out, hr[:, -1], hi[:, -1]

def _index_scores(qi, wi, ki):
    dots = jnp.einsum('bthd,bsd->bths', qi, ki).astype(jnp.float32) * IDX_DIM ** -0.5
    return jnp.einsum('bths,bth->bts', jax.nn.relu(dots), wi.astype(jnp.float32)) * N_IDX_HEADS ** -0.5

def _attend_selected(q, k_sel, v_sel, valid):
    b, t = q.shape[:2]
    qg = q.reshape(b, t, N_KV_HEADS, Q_PER_KV, HEAD_DIM)
    s = jnp.einsum('btngd,btknd->btngk', qg, k_sel).astype(jnp.float32) * HEAD_DIM ** -0.5
    s = jnp.where(valid[:, :, None, None, :], s, -jnp.inf)
    pr = jax.nn.softmax(s, axis=-1).astype(v_sel.dtype)
    o = jnp.einsum('btngk,btknd->btngd', pr, v_sel)
    return o.reshape(b, t, D_ATT)

def _dsa_prompt(q, k, v, qi, ki, wi):
    b, s_len = q.shape[:2]
    n_sel = min(TOPK_KEYS, s_len // 4)
    n_blocks = s_len // Q_BLOCK
    bidx = jnp.arange(b)[:, None, None]
    key_pos = jnp.arange(s_len)

    def block(i):
        t0 = i * Q_BLOCK
        qb = lax.dynamic_slice_in_dim(q, t0, Q_BLOCK, axis=1)
        qib = lax.dynamic_slice_in_dim(qi, t0, Q_BLOCK, axis=1)
        wib = lax.dynamic_slice_in_dim(wi, t0, Q_BLOCK, axis=1)
        tpos = t0 + jnp.arange(Q_BLOCK)
        sc = _index_scores(qib, wib, ki)
        sc = jnp.where((key_pos[None, :] <= tpos[:, None])[None], sc, -jnp.inf)
        _, idx = lax.top_k(sc, n_sel)
        valid = idx <= tpos[None, :, None]
        return _attend_selected(qb, k[bidx, idx], v[bidx, idx], valid)

    out = lax.map(block, jnp.arange(n_blocks))
    return jnp.transpose(out, (1, 0, 2, 3)).reshape(b, s_len, D_ATT)

def _dsa_sample(q, k, v, qi, ki, wi, cache_k, cache_v, cache_kidx, page_table):
    bd, t = q.shape[:2]
    n_pages = page_table.shape[1]
    past = n_pages * PAGE_SIZE
    n_keys = past + t
    n_sel = min(TOPK_KEYS, n_keys // 4)
    ki_past = cache_kidx[page_table].reshape(bd, past, IDX_DIM)
    ki_all = jnp.concatenate([ki_past, ki], axis=1)
    tpos = past + jnp.arange(t)
    sc = _index_scores(qi, wi, ki_all)
    sc = jnp.where((jnp.arange(n_keys)[None, :] <= tpos[:, None])[None], sc, -jnp.inf)
    _, idx = lax.top_k(sc, n_sel)
    valid = idx <= tpos[None, :, None]
    bidx = jnp.arange(bd)[:, None, None]
    pidx = jnp.minimum(idx, past - 1)
    phys = page_table[bidx, pidx // PAGE_SIZE]
    off = pidx % PAGE_SIZE
    nidx = jnp.clip(idx - past, 0, t - 1)
    in_past = (idx < past)[..., None, None]
    k_sel = jnp.where(in_past, cache_k[phys, off], k[bidx, nidx])
    v_sel = jnp.where(in_past, cache_v[phys, off], v[bidx, nidx])
    return _attend_selected(q, k_sel, v_sel, valid)

def _moe_ffn(h, w_router, b_router, w_e1, w_e3, w_e2, w_s1, w_s3, w_s2):
    n_tok, d = h.shape
    aff = jax.nn.sigmoid((h @ w_router).astype(jnp.float32))
    _, eidx = lax.top_k(aff + b_router.astype(jnp.float32), TOP_K_EXPERTS)
    gsel = jnp.take_along_axis(aff, eidx, axis=-1)
    gates = gsel / jnp.sum(gsel, -1, keepdims=True) * ROUTED_SCALE
    n_assign = n_tok * TOP_K_EXPERTS
    flat_e = eidx.reshape(-1)
    flat_t = jnp.repeat(jnp.arange(n_tok, dtype=jnp.int32), TOP_K_EXPERTS)
    flat_g = gates.reshape(-1)
    order = jnp.argsort(flat_e)
    se, st, sg = flat_e[order], flat_t[order], flat_g[order]
    counts = jnp.bincount(flat_e, length=N_EXPERTS)
    starts = jnp.cumsum(counts) - counts
    padded = (counts + MOE_BLOCK - 1) // MOE_BLOCK * MOE_BLOCK
    pends = jnp.cumsum(padded)
    pstarts = pends - padded
    dest = pstarts[se] + jnp.arange(n_assign) - starts[se]
    n_blocks = -(-n_assign // MOE_BLOCK) + N_EXPERTS
    n_slots = n_blocks * MOE_BLOCK
    slot_tok = jnp.full((n_slots,), n_tok, jnp.int32).at[dest].set(st)
    slot_gate = jnp.zeros((n_slots,), jnp.float32).at[dest].set(sg)
    block_e = jnp.minimum(jnp.searchsorted(pends, jnp.arange(n_blocks) * MOE_BLOCK, side='right'),
                          N_EXPERTS - 1)
    h_pad = jnp.concatenate([h, jnp.zeros((1, d), h.dtype)], axis=0)

    def expert_block(args):
        tok, e = args
        return _swiglu(h_pad[tok], w_e1[e], w_e3[e], w_e2[e])

    y = lax.map(expert_block, (slot_tok.reshape(n_blocks, MOE_BLOCK), block_e))
    y = y.reshape(n_slots, d) * slot_gate[:, None].astype(h.dtype)
    routed = jax.ops.segment_sum(y, slot_tok, num_segments=n_tok + 1)[:n_tok]
    return routed + _swiglu(h, w_s1, w_s3, w_s2)

def _decoder_layer(x, c, p, past=None):
    b, t, _ = x.shape
    mod = jax.nn.silu(c) @ p['w_ada'] + p['b_ada']
    sh1, sc1, g1, sh2, sc2, g2 = jnp.split(mod[:, None, :], 6, axis=-1)
    h = x * (1 + sc1) + sh1
    u, q, k, v, qi, ki, wi = _input_projection(h, p['w_in'])
    abr, abi, bbr, bbi = _ssm_discretise(p['ssm_a_re'], p['ssm_a_im'], p['ssm_log_dt'],
                                         p['ssm_b_re'], p['ssm_b_im'])
    if past is None:
        y_ssm, s_re, s_im = _s5_group(u, None, None, abr, abi, bbr, bbi, p['ssm_c_re'], p['ssm_c_im'],
                                      p['ssm_d'], p['w_glu'], p['b_glu'])
        y_att = _dsa_prompt(q, k, v, qi, ki, wi)
    else:
        y_ssm, s_re, s_im = _s5_group(u, past['ssm_re'], past['ssm_im'], abr, abi, bbr, bbi,
                                      p['ssm_c_re'], p['ssm_c_im'], p['ssm_d'], p['w_glu'], p['b_glu'])
        y_att = _dsa_sample(q, k, v, qi, ki, wi, past['k'], past['v'], past['kidx'], past['page_table'])
    mixed = jnp.concatenate([_rms_norm(y_ssm, p['g_ssm_out']), _rms_norm(y_att, p['g_att_out'])],
                            axis=-1) @ p['w_out']
    x = _layer_norm(ALPHA * x + g1 * mixed, p['ln1_g'], p['ln1_b'])
    h = x * (1 + sc2) + sh2
    ffn = _moe_ffn(h.reshape(b * t, D_MODEL), p['w_router'], p['b_router'], p['w_e1'], p['w_e3'],
                   p['w_e2'], p['w_s1'], p['w_s3'], p['w_s2']).reshape(b, t, D_MODEL)
    x = _layer_norm(ALPHA * x + g2 * ffn, p['ln2_g'], p['ln2_b'])
    return x, (k, v, ki, s_re, s_im)

def setup_inputs(seed: int = 0) -> dict:
    key = jax.random.key(seed)
    keys = list(jax.random.split(key, 64))
    f32 = jnp.float32

    def nrm(shape, scale=1.0):
        return jax.random.normal(keys.pop(), shape, f32) * scale

    n_pages = PAST_LEN // PAGE_SIZE
    n_pool = (DEC_BATCH * n_pages * 5) // 4
    L, D, G, P = DEPTH, D_MODEL, N_SSM_GROUPS, SSM_STATE
    inv = D ** -0.5
    x_prompt = nrm((BATCH, SEQ, D))
    x_sample = nrm((DEC_BATCH, DEC_SEQ, D))
    c_prompt = nrm((BATCH, D))
    c_sample = nrm((DEC_BATCH, D))
    cache_k = nrm((L, n_pool, PAGE_SIZE, N_KV_HEADS, HEAD_DIM))
    cache_v = nrm((L, n_pool, PAGE_SIZE, N_KV_HEADS, HEAD_DIM))
    cache_kidx = nrm((L, n_pool, PAGE_SIZE, IDX_DIM))
    state_ssm_re = nrm((L, DEC_BATCH, G, P), 0.3)
    state_ssm_im = nrm((L, DEC_BATCH, G, P), 0.3)
    page_table = jax.random.permutation(keys.pop(), n_pool)[:DEC_BATCH * n_pages].reshape(
        DEC_BATCH, n_pages).astype(jnp.int32)
    w_ada = nrm((L, D, 6 * D), 0.5 * inv)
    b_ada = nrm((L, 6 * D), 0.01)
    w_in = jnp.concatenate([nrm((L, D, D_SSM), inv),
                            nrm((L, D, N_HEADS * HEAD_DIM), inv),
                            nrm((L, D, N_KV_HEADS * HEAD_DIM), inv),
                            nrm((L, D, N_KV_HEADS * HEAD_DIM), inv * BETA),
                            nrm((L, D, N_IDX_HEADS * IDX_DIM), inv),
                            nrm((L, D, IDX_DIM), inv),
                            nrm((L, D, N_IDX_HEADS), inv)], axis=-1)
    ssm_a_re = -0.5 + nrm((L, G, P), 0.01)
    ssm_a_im = jnp.pi * jnp.arange(P, dtype=f32) + nrm((L, G, P), 0.01)
    ssm_log_dt = jax.random.uniform(keys.pop(), (L, G), f32, math.log(DT_MIN), math.log(DT_MAX))
    ssm_b_re = nrm((L, G, P, SSM_GROUP), (2 * SSM_GROUP) ** -0.5)
    ssm_b_im = nrm((L, G, P, SSM_GROUP), (2 * SSM_GROUP) ** -0.5)
    ssm_c_re = nrm((L, G, SSM_GROUP, P), (2 * P) ** -0.5)
    ssm_c_im = nrm((L, G, SSM_GROUP, P), (2 * P) ** -0.5)
    ssm_d = nrm((L, D_SSM))
    w_glu = nrm((L, D_SSM, D_SSM), D_SSM ** -0.5)
    b_glu = nrm((L, D_SSM), 0.01)
    g_ssm_out = 1.0 + nrm((L, D_SSM), 0.01)
    g_att_out = 1.0 + nrm((L, D_ATT), 0.01)
    w_out = nrm((L, D, D), inv * BETA)
    ln1_g = 1.0 + nrm((L, D), 0.01)
    ln1_b = nrm((L, D), 0.01)
    w_router = nrm((L, D, N_EXPERTS), inv)
    b_router = nrm((L, N_EXPERTS), 0.01)
    w_e1 = nrm((L, N_EXPERTS, D, D_EXPERT), inv)
    w_e3 = nrm((L, N_EXPERTS, D, D_EXPERT), inv)
    w_e2 = nrm((L, N_EXPERTS, D_EXPERT, D), D_EXPERT ** -0.5 * BETA)
    w_s1 = nrm((L, D, D_EXPERT), inv)
    w_s3 = nrm((L, D, D_EXPERT), inv)
    w_s2 = nrm((L, D_EXPERT, D), D_EXPERT ** -0.5 * BETA)
    ln2_g = 1.0 + nrm((L, D), 0.01)
    ln2_b = nrm((L, D), 0.01)
    return {'x_prompt': x_prompt, 'x_sample': x_sample, 'c_prompt': c_prompt, 'c_sample': c_sample,
            'cache_k': cache_k, 'cache_v': cache_v, 'cache_kidx': cache_kidx,
            'state_ssm_re': state_ssm_re, 'state_ssm_im': state_ssm_im, 'page_table': page_table,
            'w_ada': w_ada, 'b_ada': b_ada, 'w_in': w_in,
            'ssm_a_re': ssm_a_re, 'ssm_a_im': ssm_a_im, 'ssm_log_dt': ssm_log_dt,
            'ssm_b_re': ssm_b_re, 'ssm_b_im': ssm_b_im, 'ssm_c_re': ssm_c_re, 'ssm_c_im': ssm_c_im,
            'ssm_d': ssm_d, 'w_glu': w_glu, 'b_glu': b_glu, 'g_ssm_out': g_ssm_out, 'g_att_out': g_att_out,
            'w_out': w_out, 'ln1_g': ln1_g, 'ln1_b': ln1_b, 'w_router': w_router, 'b_router': b_router,
            'w_e1': w_e1, 'w_e3': w_e3, 'w_e2': w_e2, 'w_s1': w_s1, 'w_s3': w_s3, 'w_s2': w_s2,
            'ln2_g': ln2_g, 'ln2_b': ln2_b}

def reference(x_prompt, x_sample, c_prompt, c_sample, cache_k, cache_v, cache_kidx, state_ssm_re,
              state_ssm_im, page_table, w_ada, b_ada, w_in, ssm_a_re, ssm_a_im, ssm_log_dt, ssm_b_re,
              ssm_b_im, ssm_c_re, ssm_c_im, ssm_d, w_glu, b_glu, g_ssm_out, g_att_out, w_out, ln1_g,
              ln1_b, w_router, b_router, w_e1, w_e3, w_e2, w_s1, w_s3, w_s2, ln2_g, ln2_b):
    weights = {'w_ada': w_ada, 'b_ada': b_ada, 'w_in': w_in, 'ssm_a_re': ssm_a_re, 'ssm_a_im': ssm_a_im,
               'ssm_log_dt': ssm_log_dt, 'ssm_b_re': ssm_b_re, 'ssm_b_im': ssm_b_im,
               'ssm_c_re': ssm_c_re, 'ssm_c_im': ssm_c_im, 'ssm_d': ssm_d, 'w_glu': w_glu,
               'b_glu': b_glu, 'g_ssm_out': g_ssm_out, 'g_att_out': g_att_out, 'w_out': w_out,
               'ln1_g': ln1_g, 'ln1_b': ln1_b, 'w_router': w_router, 'b_router': b_router,
               'w_e1': w_e1, 'w_e3': w_e3, 'w_e2': w_e2, 'w_s1': w_s1, 'w_s3': w_s3, 'w_s2': w_s2,
               'ln2_g': ln2_g, 'ln2_b': ln2_b}
    xp, xs = x_prompt, x_sample
    new_p = [[], [], [], [], []]
    new_s = [[], [], [], [], []]
    for l in range(DEPTH):
        p = {name: arr[l] for name, arr in weights.items()}
        xp, st_p = _decoder_layer(xp, c_prompt, p)
        past = {'k': cache_k[l], 'v': cache_v[l], 'kidx': cache_kidx[l],
                'ssm_re': state_ssm_re[l], 'ssm_im': state_ssm_im[l], 'page_table': page_table}
        xs, st_s = _decoder_layer(xs, c_sample, p, past)
        for lst, a in zip(new_p, st_p):
            lst.append(a)
        for lst, a in zip(new_s, st_s):
            lst.append(a)
    k_p, v_p, ki_p, re_p, im_p = [jnp.stack(a, axis=0) for a in new_p]
    k_s, v_s, ki_s, re_s, im_s = [jnp.stack(a, axis=0) for a in new_s]
    return (xp, xs, k_p, v_p, ki_p, re_p, im_p, k_s, v_s, ki_s, re_s, im_s)


_drawn_inputs = setup_inputs


def setup_inputs(seed=0):
    import zlib

    import numpy as np

    out = dict(_drawn_inputs(seed))
    spreads = {}
    factors = {'ssm_a_re': 3.742,
     'b_glu': 8.0,
     'g_ssm_out': 8.0,
     'g_att_out': 8.0,
     'ln1_g': 3.538,
     'ln1_b': 3.432,
     'ln2_g': 5.486,
     'ln2_b': 5.902}
    for name, (base, spread) in spreads.items():
        noise = np.random.default_rng([zlib.crc32(name.encode()), seed]).standard_normal(out[name].shape)
        drawn = base * np.exp(spread * noise) if base else spread * noise
        out[name] = __import__('jax').numpy.asarray(drawn.astype(out[name].dtype))
    for name, factor in factors.items():
        out[name] = (out[name] * factor).astype(out[name].dtype)
    return out
```

```python
from contextlib import ExitStack

import numpy as np
import concourse.bass as bass
from concourse import mybir
from concourse.alu_op_type import AluOpType as ALU

ACT = mybir.ActivationFunctionType
F32 = mybir.dt.float32
BF16 = mybir.dt.bfloat16
I32 = mybir.dt.int32
U16 = mybir.dt.uint16
AX = mybir.AxisListType.X

P = 128
D = 1024
KD = D // P
SEQ = 1024
NB, NT = 8, 8
NS = NB * NT
TOK = SEQ + NS
TILES = SEQ // P
D_SSM = 512
GROUPS, GCH, STATES = 32, 16, 64
PAIRS = GROUPS // 2
LC = 8
CH = SEQ // LC
CHS = CH + NB
HEADS, KVH, HD = 8, 4, 64
IH, IDX = 4, 64
TOPK = 256
PAST, PAGE = 2048, 128
PAGES = PAST // PAGE
KEYS = PAST + NT
EXPERTS, TOPE, FE = 64, 6, 256
ROUTED_SCALE = 2.5
ALPHA = 2 ** 0.25
EPS = 1e-5
C_U, C_Q, C_K, C_V, C_QI, C_KI, C_WI, C_END = 0, 512, 1024, 1280, 1536, 1792, 1856, 1860
SH1, SC1, G1, SH2, SC2, G2 = (i * D for i in range(6))
BLK = 128
NBLK = TOK * TOPE // BLK + EXPERTS
SLOTS = NBLK * BLK
ROWS = (TILES + 1) * P
TRASH = ROWS
NEG = -1e30


HELD = []


def new_sem(nc, name):
    HELD.append(nc.alloc_semaphore(name))
    return HELD[-1]


def clear_sems(nc):
    nc.clear_and_free_semaphores(list(HELD))
    nc.all_engine_barrier()
    HELD.clear()


class Chain:

    def __init__(self, sem):
        self.sem, self.n = sem, 0

    def did(self, ins):
        self.n += 1
        ins.then_inc(self.sem, 1)
        return self.n


def make_constants(nc, cst):
    with ExitStack() as ctx:
        made = new_sem(nc, "constants_made")
        block = ctx.enter_context(nc.Block())

        @block.gpsimd
        def _(pool):
            nc.gpsimd.memset(cst["ident"][:], 0.0).then_inc(made, 1)
            nc.gpsimd.memset(cst["ones"][:], 1.0).then_inc(made, 1)
            nc.gpsimd.memset(cst["before"][:], 1.0).then_inc(made, 1)
            pool.wait_ge(made, 3)
            nc.gpsimd.affine_select(out=cst["ident"][:], in_=cst["ident"][:], pattern=[[-1, P]],
                                    compare_op=ALU.not_equal, fill=1.0, base=0,
                                    channel_multiplier=1).then_inc(made, 1)
            nc.gpsimd.affine_select(out=cst["before"][:], in_=cst["before"][:], pattern=[[1, P]],
                                    compare_op=ALU.is_gt, fill=0.0, base=0,
                                    channel_multiplier=-1).then_inc(made, 1)
            pool.wait_ge(made, 5)


def ada_phase(nc, cst, psum, a, scr, modT):
    NR = 1 + NB
    NCOL = 6 * D // 512
    RING = 3
    with ExitStack() as ctx:
        def sb(name, shape, dt=F32):
            return ctx.enter_context(nc.sbuf_tensor(name, shape, dt))

        def sem(name):
            return new_sem(nc, name)

        c_rows = sb("c_rows", [NR, D])
        c_sig = sb("c_sig", [NR, D])
        cT = sb("cT", [P, KD, NR])
        wa = sb("wa", [P, RING, KD, 512])
        bada = sb("bada", [NR, 6 * D])
        mod = sb("mod", [NR, 6 * D])
        c_in, silu_done, cT_ps, cT_sb = sem("c_in"), sem("silu_done"), sem("cT_ps"), sem("cT_sb")
        w_in = [sem(f"wa_in{i}") for i in range(RING)]
        b_in, mod_ps, mod_sb = sem("b_in"), sem("mod_ps"), sem("mod_sb")
        mT_ps, mT_sb, mod_out = sem("mT_ps"), sem("mT_sb"), sem("mod_out")
        block = ctx.enter_context(nc.Block())

        @block.sync
        def _(sp):
            sp.dma_start(c_rows[0:1], a["c_prompt"]).then_inc(c_in, 16)
            sp.dma_start(c_rows[1:NR], a["c_sample"]).then_inc(c_in, 16)
            for n in range(NCOL):
                if n >= RING:
                    sp.wait_ge(mod_ps, n - RING + 1)
                sp.dma_start(wa[:, n % RING],
                             a["w_ada"][0].rearrange("(p k) n -> p k n", k=KD)[:, :, n * 512:(n + 1) * 512]
                             ).then_inc(w_in[n % RING], 16)
                if n == 0:
                    sp.dma_start(bada[:], a["b_ada"][0].partition_broadcast(NR)).then_inc(b_in, 16)
            sp.wait_ge(mod_sb, NCOL)
            sp.dma_start(scr["mod"], mod[:]).then_inc(mod_out, 16)
            sp.wait_ge(mod_out, 16)

        @block.scalar
        def _(act):
            act.wait_ge(c_in, 32)
            nc.scalar.activation(c_sig[:], c_rows[:], ACT.Sigmoid).then_inc(silu_done, 1)

        @block.vector
        def _(dve):
            dve.wait_ge(silu_done, 1)
            nc.vector.tensor_tensor(c_sig[:], c_sig[:], c_rows[:], ALU.mult).then_inc(silu_done, 1)
            dve.wait_ge(cT_ps, 1)
            nc.vector.tensor_copy(cT[:], psum[:, 0, 0:KD * NR].rearrange("p (k r) -> p k r", k=KD)
                                  ).then_inc(cT_sb, 1)
            dve.wait_ge(b_in, 16)
            for n in range(NCOL):
                dve.wait_ge(mod_ps, n + 1)
                cols = slice(n * 512, (n + 1) * 512)
                nc.vector.tensor_tensor(mod[:, cols], psum[0:NR, 1 + n % 4, :], bada[:, cols], ALU.add
                                        ).then_inc(mod_sb, 1)
            dve.wait_ge(mT_ps, 1)
            nc.vector.tensor_copy(modT[:, 0], psum[:, 5, 0:KD * NR].rearrange("p (k r) -> p k r", k=KD))
            nc.vector.tensor_scalar(modT[:, 1], psum[:, 6, 0:KD * NR].rearrange("p (k r) -> p k r", k=KD),
                                    1.0, None, ALU.add).then_inc(mT_sb, 1)

        @block.tensor
        def _(pe):
            pe.wait_ge(silu_done, 2)
            for k in range(KD):
                mm = pe.transpose(psum[:, 0, k * NR:(k + 1) * NR], c_sig[:, k:D:KD],
                                  cst["ident"][0:NR, 0:NR])
            mm.then_inc(cT_ps, 1)
            pe.wait_ge(cT_sb, 1)
            for n in range(NCOL):
                pe.wait_ge(w_in[n % RING], 16 * (n // RING + 1))
                if n >= 4:
                    pe.wait_ge(mod_sb, n - 3)
                for k in range(KD):
                    mm = pe.matmul(psum[0:NR, 1 + n % 4, :], cT[:, k], wa[:, n % RING, k],
                                   start=(k == 0), stop=(k == KD - 1))
                mm.then_inc(mod_ps, 1)
            pe.wait_ge(mod_sb, NCOL)
            for part, bank in ((SH1, 5), (SC1, 6)):
                for k in range(KD):
                    mm = pe.transpose(psum[:, bank, k * NR:(k + 1) * NR],
                                      mod[:, part + k:part + D:KD], cst["ident"][0:NR, 0:NR])
            mm.then_inc(mT_ps, 1)


def project_phase(nc, cst, psum, a, o, modT, act_t):
    XR = 2
    with ExitStack() as ctx:
        def sb(name, shape, dt=F32):
            return ctx.enter_context(nc.sbuf_tensor(name, shape, dt))

        def sem(name):
            return new_sem(nc, name)

        w = sb("w", [P, KD, C_END])
        wq = sb("wq", [P, KD, 4, P])
        wkk = act_t["spare"][:, 0:KD * P].rearrange("p (k c) -> p k c", k=KD)
        krow = act_t["spare"][:, KD * P:KD * P + (TILES + 1) * KVH * HD].rearrange(
            "p (t c) -> p t c", t=TILES + 1)
        xt = sb("xt", [P, XR, D])
        hT = sb("hT", [P, KD, TOK])
        w_land = sem("w_land")
        x_land = [sem(f"x_land{i}") for i in range(XR)]
        wq_made = sem("wq_made")
        ps_full = sem("ps_full")
        dve_read, act_read = sem("dve_read"), sem("act_read")
        rows_out = sem("rows_out")
        hs_mid = sem("hs_mid")

        groups = []
        for t in range(TILES):
            groups += [("x", t, 0), ("x", t, 1)]
        groups += [("xs", 0, 0)]
        for s in range(LC):
            groups += [("u", s, 0)]
        groups += [("us", 0, 0)]
        cuts = [(0, 384), (384, 736), (736, TOK)]
        for name, n in (("q", 4), ("k", 2), ("qi", 2), ("ki", 1)):
            for b in range(n):
                for c in cuts:
                    groups.append((name, b, c))
        for t in range(TILES + 1):
            groups += [("v", t, 0), ("kiwi", t, 0), ("krow", t, 0)]
        last_even = max(g for g in range(len(groups)) if g % 2 == 0)
        X_GROUPS = 2 * TILES + 1

        def tokens(t):
            return (t * P, P) if t < TILES else (SEQ, NS)

        block = ctx.enter_context(nc.Block())

        @block.sync
        def _(sp):
            for t in range(TILES + 1):
                if t >= XR:
                    sp.wait_ge(ps_full, 2 * (t - XR) + 2)
                if t < TILES:
                    sp.dma_start(xt[:, t % XR], a["x_prompt"][0].rearrange("(c s) d -> s c d", s=LC)[t]
                                 ).then_inc(x_land[t % XR], 16)
                else:
                    sp.dma_start(xt[0:NS, t % XR], a["x_sample"].rearrange("b t d -> (b t) d")
                                 ).then_inc(x_land[t % XR], 16)
                if t == XR - 1:
                    sp.dma_start(w[:], a["w_in"][0].rearrange("(p k) n -> p k n", k=KD)).then_inc(w_land, 16)
            sp.wait_ge(dve_read, last_even // 2 + 1)
            sp.wait_ge(act_read, len(groups) // 2)
            v, kiwi = act_t["v"], act_t["kiwi"]
            outs = [(o["k_prompt"], krow, 256), (o["v_prompt"], v, 256), (o["ki_prompt"], kiwi, IDX)]
            for dst, src, n in outs:
                flat = dst.rearrange("l b s h d -> (l b s) (h d)") if n == 256 else \
                    dst.rearrange("l b s d -> (l b s) d")
                sp.dma_start(flat.rearrange("(t p) n -> p t n", p=P), src[:, 0:TILES, 0:n]
                             ).then_inc(rows_out, 16)
            outs = [(o["k_sample"], krow, 256), (o["v_sample"], v, 256), (o["ki_sample"], kiwi, IDX)]
            for dst, src, n in outs:
                flat = dst.rearrange("l b s h d -> (l b s) (h d)") if n == 256 else \
                    dst.rearrange("l b s d -> (l b s) d")
                sp.dma_start(flat, src[0:NS, TILES, 0:n]).then_inc(rows_out, 16)
            sp.wait_ge(rows_out, 96)

        def evacuate(eng, g):
            kind, i, c = groups[g]
            bank = psum[:, g % 8]
            done = dve_read if g % 2 == 0 else act_read
            copy = nc.vector.tensor_copy if g % 2 == 0 else nc.scalar.copy
            if kind == "x":
                for j in range(4):
                    k = 4 * c + j
                    out, src = hT[:, k, i:SEQ:LC], bank[:, j * P:(j + 1) * P]
                    if g % 2 == 0:
                        ins = nc.vector.tensor_scalar(out, src, modT[:, 1, k, 0:1], modT[:, 0, k, 0:1],
                                                      ALU.mult, ALU.add)
                    else:
                        ins = nc.scalar.activation(out, src, ACT.Identity, bias=modT[:, 0, k, 0:1],
                                                   scale=modT[:, 1, k, 0:1])
                return ins.then_inc(done, 1)
            if kind == "xs":
                out = hT[:, :, SEQ:TOK].rearrange("p k (b t) -> p k b t", b=NB)
                src = bank.rearrange("p (k b t) -> p k b t", k=KD, b=NB)
                shape = [P, KD, NB, NT]
                nc.vector.tensor_tensor(out, src, modT[:, 1, :, 1:].unsqueeze(3).broadcast_to(shape),
                                        ALU.mult).then_inc(hs_mid, 1)
                eng.wait_ge(hs_mid, 1)
                return nc.vector.tensor_tensor(out, out, modT[:, 0, :, 1:].unsqueeze(3).broadcast_to(shape),
                                               ALU.add).then_inc(done, 1)
            if kind == "u":
                out = act_t["u"][:, :, i, :]
                return copy(out, bank.rearrange("p (g j) -> p g j", g=GROUPS)).then_inc(done, 1)
            if kind == "us":
                return copy(act_t["us"][0:NS, :], bank[0:NS, :]).then_inc(done, 1)
            if kind in ("q", "k", "qi", "ki"):
                dst = act_t[kind + "T"]
                out = dst[:, i, c[0]:c[1]]
                return copy(out, bank[:, 0:c[1] - c[0]]).then_inc(done, 1)
            n = tokens(i)[1]
            dst, width = {"v": (act_t["v"], 256), "kiwi": (act_t["kiwi"], IDX + IH),
                          "krow": (krow, 256)}[kind]
            return copy(dst[0:n, i, :], bank[0:n, 0:width]).then_inc(done, 1)

        @block.vector
        def _(dve):
            for g in range(0, len(groups), 2):
                dve.wait_ge(ps_full, g + 1)
                evacuate(dve, g)
                if g == 2 * TILES + 2:
                    dve.wait_ge(w_land, 16)
                    nc.vector.tensor_copy(
                        wq[:].rearrange("p k (m a) (n d) -> p k m a n d", m=2, n=2)[:, :, 0],
                        w[:, :, C_Q:C_Q + 256].rearrange("p k (n a d) -> p k a n d", n=2, a=2))
                    nc.vector.tensor_copy(
                        wq[:].rearrange("p k (m a) (n d) -> p k m a n d", m=2, n=2)[:, :, 1],
                        w[:, :, C_Q + 256:C_K].rearrange("p k (n a d) -> p k a n d", n=2, a=2))
                    for half in range(2):
                        ins = nc.vector.tensor_copy(wkk[:, :, half * IDX:(half + 1) * IDX],
                                                    w[:, :, C_KI:C_WI])
                    ins.then_inc(wq_made, 1)

        @block.scalar
        def _(act):
            for g in range(1, len(groups), 2):
                act.wait_ge(ps_full, g + 1)
                evacuate(act, g)

        @block.tensor
        def _(pe):
            for g, (kind, i, c) in enumerate(groups):
                bank = psum[:, g % 8]
                if g >= 8:
                    if g % 2 == 0:
                        pe.wait_ge(dve_read, (g - 8) // 2 + 1)
                    else:
                        pe.wait_ge(act_read, (g - 8) // 2 + 1)
                if kind in ("x", "xs"):
                    t = i if kind == "x" else TILES
                    pe.wait_ge(x_land[t % XR], 16 * (t // XR + 1))
                    if kind == "x":
                        for j in range(4):
                            mm = pe.transpose(bank[:, j * P:(j + 1) * P], xt[:, t % XR, 4 * c + j:D:KD],
                                              cst["ident"][:])
                        mm.then_inc(ps_full, 1)
                    else:
                        for k in range(KD):
                            mm = pe.transpose(bank[:, k * NS:(k + 1) * NS], xt[0:NS, t % XR, k:D:KD],
                                              cst["ident"][0:NS, 0:NS])
                        mm.then_inc(ps_full, 1)
                    continue
                if g == X_GROUPS:
                    pe.wait_ge(dve_read, X_GROUPS // 2 + 1)
                    pe.wait_ge(act_read, X_GROUPS // 2)
                    pe.wait_ge(w_land, 16)
                if kind == "q" and i == 0 and c[0] == 0:
                    pe.wait_ge(wq_made, 1)
                if kind == "krow":
                    first, n = tokens(i)
                    if i == 0:
                        kg = max(j for j, x in enumerate(groups) if x[0] == "k")
                        pe.wait_ge(dve_read, kg // 2 + 1)
                        pe.wait_ge(act_read, (kg + 1) // 2)
                    for b in range(2):
                        mm = pe.transpose(bank[0:n, b * P:(b + 1) * P], act_t["kT"][:, b, first:first + n],
                                          cst["ident"][:])
                    mm.then_inc(ps_full, 1)
                    continue
                for k in range(KD):
                    flags = dict(start=(k == 0), stop=(k == KD - 1))
                    if kind == "u":
                        mm = pe.matmul(bank, hT[:, k, i:SEQ:LC], w[:, k, C_U:C_Q], **flags)
                    elif kind == "us":
                        mm = pe.matmul(bank[0:NS], hT[:, k, SEQ:TOK], w[:, k, C_U:C_Q], **flags)
                    elif kind in ("q", "k", "qi", "ki"):
                        lhs = {"q": lambda: wq[:, k, i, :], "k": lambda: w[:, k, C_K + i * P:C_K + (i + 1) * P],
                               "qi": lambda: w[:, k, C_QI + i * P:C_QI + (i + 1) * P],
                               "ki": lambda: wkk[:, k, :]}[kind]()
                        mm = pe.matmul(bank[:, 0:c[1] - c[0]], lhs, hT[:, k, c[0]:c[1]], **flags)
                    else:
                        first, n = tokens(i)
                        cols = (C_V, C_QI) if kind == "v" else (C_KI, C_END)
                        mm = pe.matmul(bank[0:n, 0:cols[1] - cols[0]], hT[:, k, first:first + n],
                                       w[:, k, cols[0]:cols[1]], **flags)
                mm.then_inc(ps_full, 1)


def ssm_tables_phase(nc, cst, psum, a, s):
    M = PAIRS
    with ExitStack() as ctx:
        def sb(name, shape, dt=F32):
            return ctx.enter_context(nc.sbuf_tensor(name, shape, dt))

        def sem(name):
            return new_sem(nc, name)

        ar, ai = sb("ar", [M, P]), sb("ai", [M, P])
        ldt, dt = sb("ldt", [M, 2]), sb("dt", [M, 2])
        mag, ang = sb("mag", [M, P]), sb("ang", [M, P])
        NQ = 2 * (LC + 1) + 5
        rows = sb("rows", [M, NQ, P])
        PR, PI, FR, FI, R8, C8, S8 = 0, LC + 1, 2 * LC + 2, 2 * LC + 3, 2 * LC + 4, 2 * LC + 5, 2 * LC + 6
        w1, w2, w3, w4 = (sb(f"w{i}", [M, P]) for i in range(1, 5))
        e1, e2, e3 = (sb(f"e{i}", [M, P]) for i in range(1, 4))
        ei = sb("ei", [M, P], I32)
        cf = sb("cf", [P, NQ, M])
        prev = sb("prev", [P, 2, M, LC + 1])
        b_raw = sb("b_raw", [P, 2, M, GCH])
        bbar = sb("bbar", [P, 2, M, GCH])
        wz = sb("wz", [P, 2, M, LC, GCH])
        tmp = s["spare"][:, 0:M * LC * GCH].rearrange("p (m s j) -> p m s j", m=M, s=LC)
        c_nat = sb("c_nat", [P, 2, 4, STATES])
        cT = sb("c_T", [P, 2, M, GCH])
        cb = sb("c_b", [P, 2, M, 2, GCH])
        dmat = sb("dmat", [P, GROUPS, GCH])
        kmat = sb("kmat", [P, GROUPS, GCH])
        shift = sb("shift", [P, P + (LC - 1) * GCH])
        rsq = sb("rsq", [P, 2, 2, M])
        rt = s["spare"][:, M * P:2 * M * P].rearrange("p (i m c) -> p i m c", i=2, m=M)
        in_land, d_land, c_land = sem("in_land"), sem("d_land"), sem("c_land")
        sin_in, sin_out = sem("sin_in"), sem("sin_out")
        rows_made, cf_ps, cf_read = sem("rows_made"), sem("cf_ps"), sem("cf_read")
        ct_ps, ct_read = sem("ct_ps"), sem("ct_read")
        wz_made, k_ps, k_made, shift_made, dmat_made = (sem(n) for n in ("wz_made", "k_ps", "k_made",
                                                                         "shift_made", "dmat_made"))
        t_ps, t_read, wt_ps, wt_read = sem("t_ps"), sem("t_read"), sem("wt_ps"), sem("wt_read")
        chain = Chain(sem("ssm_chain"))
        block = ctx.enter_context(nc.Block())

        @block.sync
        def _(sp):
            sp.dma_start(ar[:], a["ssm_a_re"][0].rearrange("(m g) p -> m (g p)", g=2)).then_inc(in_land, 16)
            sp.dma_start(ai[:], a["ssm_a_im"][0].rearrange("(m g) p -> m (g p)", g=2)).then_inc(in_land, 16)
            sp.dma_start(ldt[:], a["ssm_log_dt"][0].rearrange("(m g) -> m g", g=2)).then_inc(in_land, 16)
            for i, n in enumerate(("ssm_c_re", "ssm_c_im")):
                sp.dma_start(c_nat[:, i], a[n][0].rearrange("(q g) i p -> (g i) q p", g=8)).then_inc(c_land, 16)
            sp.dma_start(dmat[:].rearrange("p g i -> p (g i)"), a["ssm_d"][0].partition_broadcast(P)
                         ).then_inc(d_land, 16)
            for i, n in enumerate(("ssm_b_re", "ssm_b_im")):
                sp.dma_start(b_raw[:, i], a[n][0].rearrange("(m g) p j -> (g p) m j", g=2)
                             ).then_inc(in_land, 16)

        @block.gpsimd
        def _(pool):
            nc.gpsimd.memset(shift[:], 0.0).then_inc(shift_made, 1)
            pool.wait_ge(shift_made, 1)
            nc.gpsimd.affine_select(out=shift[:], in_=shift[:], pattern=[[-1, shift.shape[1]]],
                                    compare_op=ALU.not_equal, fill=1.0, base=0,
                                    channel_multiplier=1).then_inc(shift_made, 1)
            pool.wait_ge(d_land, 16)
            nc.gpsimd.affine_select(out=dmat[:], in_=dmat[:], pattern=[[0, GROUPS], [-1, GCH]],
                                    compare_op=ALU.is_equal, fill=0.0, base=-(LC - 1) * GCH,
                                    channel_multiplier=1).then_inc(dmat_made, 1)

        @block.scalar
        def _(act):
            act.wait_ge(sin_in, 1)
            nc.scalar.activation(w3[:], w1[:], ACT.Sin)
            nc.scalar.activation(w4[:], w2[:], ACT.Sin).then_inc(sin_out, 1)

        @block.vector
        def _(dve):
            def seq(ins):
                dve.wait_ge(chain.sem, chain.did(ins))

            def tt(out, x, y, op):
                seq(nc.vector.tensor_tensor(out, x, y, op))

            def ts(out, x, s1, s2, op0, op1=ALU.bypass):
                if s2 is None:
                    seq(nc.vector.tensor_scalar(out, x, s1, None, op0))
                else:
                    seq(nc.vector.tensor_scalar(out, x, s1, s2, op0, op1))

            def exp(out, x, n):
                magic, ln_hi = 12582912.0, 0.693145751953125
                ln_lo = float(np.log(2.0) - ln_hi)
                r, kk, acc, ki = e1[:, 0:n], e2[:, 0:n], e3[:, 0:n], ei[:, 0:n]
                ts(kk, x, float(1 / np.log(2.0)), magic, ALU.mult, ALU.add)
                ts(kk, kk, magic, -126.0, ALU.subtract, ALU.max)
                seq(nc.vector.scalar_tensor_tensor(r, kk, -ln_hi, x, ALU.mult, ALU.add))
                seq(nc.vector.scalar_tensor_tensor(r, kk, -ln_lo, r, ALU.mult, ALU.add))
                ts(acc, r, 1 / 40320.0, 1 / 5040.0, ALU.mult, ALU.add)
                for c in (720.0, 120.0, 24.0, 6.0, 2.0, 1.0, 1.0):
                    tt(acc, acc, r, ALU.mult)
                    ts(acc, acc, 1 / c, None, ALU.add)
                ts(ki, kk, 127.0, 8388608.0, ALU.add, ALU.mult)
                tt(out, acc, ki.bitcast(F32), ALU.mult)

            def cmul(orr, oi, xr, xi, yr, yi, t1):
                tt(orr, xr, yr, ALU.mult)
                tt(t1, xi, yi, ALU.mult)
                tt(orr, orr, t1, ALU.subtract)
                tt(oi, xr, yi, ALU.mult)
                tt(t1, xi, yr, ALU.mult)
                tt(oi, oi, t1, ALU.add)

            dve.wait_ge(in_land, 5 * 16)
            exp(dt[:], ldt[:], 2)
            dtb = dt[:].unsqueeze(2).broadcast_to([M, 2, STATES])
            tt(mag[:].rearrange("m (g p) -> m g p", g=2), ar[:].rearrange("m (g p) -> m g p", g=2), dtb, ALU.mult)
            tt(ang[:].rearrange("m (g p) -> m g p", g=2), ai[:].rearrange("m (g p) -> m g p", g=2), dtb, ALU.mult)
            turn = 2 * np.pi
            t_hi = 6.28125
            t_mid = float(np.float32(int((turn - t_hi) * 2 ** 20)) / 2 ** 20)
            t_lo = float(turn - t_hi - t_mid)
            pi_in = 3.1415925
            ts(w1[:], ang[:], 1 / turn, 12582912.0, ALU.mult, ALU.add)
            ts(w2[:], w1[:], 12582912.0, None, ALU.subtract)
            seq(nc.vector.scalar_tensor_tensor(w1[:], w2[:], -t_hi, ang[:], ALU.mult, ALU.add))
            seq(nc.vector.scalar_tensor_tensor(w1[:], w2[:], -t_mid, w1[:], ALU.mult, ALU.add))
            seq(nc.vector.scalar_tensor_tensor(w1[:], w2[:], -t_lo, w1[:], ALU.mult, ALU.add))
            ts(w1[:], w1[:], pi_in, -pi_in, ALU.min, ALU.max)
            ts(w2[:], w1[:], -1.0, None, ALU.mult)
            tt(w2[:], w2[:], w1[:], ALU.min)
            nc.vector.tensor_scalar(w2[:], w2[:], float(np.pi / 2), None, ALU.add).then_inc(sin_in, 1)
            ts(ang[:], mag[:], float(LC), None, ALU.mult)
            exp(rows[:, R8], ang[:], P)
            exp(ang[:], mag[:], P)
            dve.wait_ge(sin_out, 1)
            nc.vector.tensor_copy(rows[:, C8], w4[:])
            seq(nc.vector.tensor_copy(rows[:, S8], w3[:]))
            for _ in range(3):
                cmul(e1[:], e2[:], rows[:, C8], rows[:, S8], rows[:, C8], rows[:, S8], e3[:])
                nc.vector.tensor_copy(rows[:, C8], e1[:])
                seq(nc.vector.tensor_copy(rows[:, S8], e2[:]))
            nc.vector.memset(rows[:, PR], 1.0)
            nc.vector.memset(rows[:, PI], 0.0)
            tt(rows[:, PR + 1], ang[:], w4[:], ALU.mult)
            tt(rows[:, PI + 1], ang[:], w3[:], ALU.mult)
            for n in range(2, LC + 1):
                h = n // 2
                cmul(rows[:, PR + n], rows[:, PI + n], rows[:, PR + h], rows[:, PI + h],
                     rows[:, PR + n - h], rows[:, PI + n - h], e1[:])
            tt(e1[:], ar[:], ar[:], ALU.mult)
            tt(e2[:], ai[:], ai[:], ALU.mult)
            tt(e1[:], e1[:], e2[:], ALU.add)
            seq(nc.vector.reciprocal(e3[:], e1[:]))
            ts(w1[:], rows[:, PR + 1], -1.0, None, ALU.add)
            ni = rows[:, PI + 1]
            tt(e1[:], w1[:], ar[:], ALU.mult)
            tt(e2[:], ni, ai[:], ALU.mult)
            tt(e1[:], e1[:], e2[:], ALU.add)
            tt(rows[:, FR], e1[:], e3[:], ALU.mult)
            tt(e1[:], ni, ar[:], ALU.mult)
            tt(e2[:], w1[:], ai[:], ALU.mult)
            tt(e1[:], e1[:], e2[:], ALU.subtract)
            nc.vector.tensor_tensor(rows[:, FI], e1[:], e3[:], ALU.mult).then_inc(rows_made, 1)
            dve.wait_ge(ct_ps, 1)
            nc.vector.tensor_copy(cT[:, 0], psum[:, 1, 0:M * GCH].rearrange("p (m i) -> p m i", m=M))
            nc.vector.tensor_scalar(cT[:, 1], psum[:, 2, 0:M * GCH].rearrange("p (m i) -> p m i", m=M),
                                    -1.0, None, ALU.mult)
            seq(nc.vector.memset(cb[:], 0.0))
            for g in range(2):
                half = slice(g * 64, g * 64 + 64)
                seq(nc.vector.tensor_copy(cb[half, :, :, g], cT[half]))
            dve.wait_ge(cf_ps, 1)
            seq(nc.vector.tensor_copy(cf[:].rearrange("p q m -> p (q m)"), psum[:, 0, 0:NQ * M]))
            for n in range(LC + 1):
                nc.vector.tensor_copy(prev[:, 0, :, LC - n], cf[:, PR + n])
                last = nc.vector.tensor_copy(prev[:, 1, :, LC - n], cf[:, PI + n])
            seq(last)
            wide = [P, M, GCH]
            cmul(bbar[:, 0], bbar[:, 1], cf[:, FR].unsqueeze(2).broadcast_to(wide),
                 cf[:, FI].unsqueeze(2).broadcast_to(wide), b_raw[:, 0], b_raw[:, 1], tmp[:, :, 0, :])
            full = [P, M, LC, GCH]
            cmul(wz[:, 0], wz[:, 1], prev[:, 0, :, 1:].unsqueeze(3).broadcast_to(full),
                 prev[:, 1, :, 1:].unsqueeze(3).broadcast_to(full),
                 bbar[:, 0].unsqueeze(2).broadcast_to(full), bbar[:, 1].unsqueeze(2).broadcast_to(full), tmp)
            nc.vector.tensor_copy(s["r8"][:], cf[:, R8]).then_inc(wz_made, 1)
            nc.vector.tensor_copy(s["a8"][:, 0], cf[:, PR + LC])
            seq(nc.vector.tensor_copy(s["a8"][:, 1], cf[:, PI + LC]))
            fwd = [cf[:, PR + 1:PR + LC + 1].rearrange("p t m -> p m t").unsqueeze(3).broadcast_to(full),
                   cf[:, PI + 1:PI + LC + 1].rearrange("p t m -> p m t").unsqueeze(3).broadcast_to(full)]
            cc = [cT[:, i].unsqueeze(2).broadcast_to(full) for i in range(2)]
            tt(s["ca"][:, 0], fwd[0], cc[0], ALU.mult)
            tt(tmp[:], fwd[1], cc[1], ALU.mult)
            tt(s["ca"][:, 0], s["ca"][:, 0], tmp[:], ALU.add)
            tt(s["ca"][:, 1], fwd[0], cc[1], ALU.mult)
            tt(tmp[:], fwd[1], cc[0], ALU.mult)
            tt(s["ca"][:, 1], s["ca"][:, 1], tmp[:], ALU.subtract)
            dve.wait_ge(k_ps, 1)
            dve.wait_ge(dmat_made, 1)
            nc.vector.tensor_tensor(kmat[:].rearrange("p g i -> p (g i)"), psum[:, 3, :],
                                    dmat[:].rearrange("p g i -> p (g i)"), ALU.add).then_inc(k_made, 1)
            rot = s["rot"]
            nc.vector.memset(rot[:, 0, :, 0], 1.0)
            nc.vector.memset(rot[:, 1, :, 0], 0.0)
            nc.vector.tensor_copy(rsq[:, 0, 0], cf[:, C8])
            seq(nc.vector.tensor_copy(rsq[:, 0, 1], cf[:, S8]))
            n, cur = 1, 0
            while n < CH:
                nar = [P, M, n]
                er, ei_ = (rsq[:, cur, i].unsqueeze(2).broadcast_to(nar) for i in range(2))
                cmul(rot[:, 0, :, n:2 * n], rot[:, 1, :, n:2 * n], rot[:, 0, :, 0:n], rot[:, 1, :, 0:n],
                     er, ei_, rt[:, 0, :, 0:n])
                n *= 2
                if n < CH:
                    cmul(rsq[:, 1 - cur, 0], rsq[:, 1 - cur, 1], rsq[:, cur, 0], rsq[:, cur, 1],
                         rsq[:, cur, 0], rsq[:, cur, 1], rt[:, 1, :, 0])
                    cur = 1 - cur
            for i in range(2):
                for q in range(4):
                    dve.wait_ge(wt_ps, 4 * i + q + 1)
                    last = nc.vector.tensor_copy(s["wT"][:, i, 4 * q:4 * q + 4],
                                                 psum[:, 4 + q, :].rearrange("p (m x) -> p m x", m=4))
                    last.then_inc(wt_read, 1)
            for t in range(LC):
                dve.wait_ge(t_ps, t + 1)
                nc.vector.tensor_copy(s["toep"][:, :, t], psum[:, t % 4, :].rearrange("p (g i) -> p g i", i=GCH)
                                      ).then_inc(t_read, 1)

        @block.tensor
        def _(pe):
            ident = cst["ident"]
            pe.wait_ge(c_land, 32)
            for i in range(2):
                for q in range(4):
                    for g in range(2):
                        sel = ident[:].rearrange("p (m g i) -> p m g i", g=2, i=GCH)[:, :, g]
                        mm = pe.matmul(psum[64 * g:64 * g + 64, 1 + i, q * 64:(q + 1) * 64].rearrange(
                            "p (m i) -> p m i", m=4), c_nat[:, i, q], sel, start=True, stop=True)
            mm.then_inc(ct_ps, 1)
            pe.wait_ge(rows_made, 1)
            for q in range(NQ):
                mm = pe.transpose(psum[:, 0, q * M:(q + 1) * M], rows[:, q], ident[0:M, 0:M])
            mm.then_inc(cf_ps, 1)
            pe.wait_ge(wz_made, 1)
            for m in range(M):
                for i in range(2):
                    mm = pe.matmul(psum[:, 3, m * 32:(m + 1) * 32],
                                   wz[:, i, m].rearrange("p s j -> p (s j)"),
                                   cb[:, i, m].rearrange("p g i -> p (g i)"), start=(i == 0), stop=(i == 1))
            mm.then_inc(k_ps, 1)
            for i in range(2):
                for q in range(4):
                    if i:
                        pe.wait_ge(wt_read, q + 1)
                    for m in range(4):
                        mm = pe.transpose(psum[:, 4 + q, m * P:(m + 1) * P],
                                          wz[:, i, 4 * q + m].rearrange("p s j -> p (s j)"), ident[:])
                    mm.then_inc(wt_ps, 1)
            pe.wait_ge(k_made, 1)
            pe.wait_ge(shift_made, 2)
            for t in range(LC):
                if t >= 4:
                    pe.wait_ge(t_read, t - 3)
                off = GCH * (LC - 1 - t)
                mm = pe.matmul(psum[:, t % 4, :], shift[:, off:off + P], kmat[:].rearrange("p g i -> p (g i)"),
                               start=True, stop=True)
                mm.then_inc(t_ps, 1)


def ssm_input_phase(nc, cst, psum, t, s):
    with ExitStack() as ctx:
        def sb(name, shape, dt=F32):
            return ctx.enter_context(nc.sbuf_tensor(name, shape, dt))

        def sem(name):
            return new_sem(nc, name)

        us_b = sb("us_b", [NB, NT, D_SSM])
        us_g = sb("us_g", [NB, GROUPS, NT, GCH])
        us_land, us_made, ps_full, dve_read, act_read = (sem(n) for n in (
            "us_land", "us_made", "uc_ps", "uc_dve_read", "uc_act_read"))
        block = ctx.enter_context(nc.Block())
        uc = s["uc"]

        @block.sync
        def _(sp):
            for b in range(NB):
                sp.dma_start(us_b[b:b + 1], t["us"][b * NT:(b + 1) * NT]).then_inc(us_land, 16)

        @block.vector
        def _(dve):
            dve.wait_ge(us_land, 16 * NB)
            nc.vector.tensor_copy(us_g[:], us_b[:].rearrange("b s (g j) -> b g s j", j=GCH)).then_inc(us_made, 1)
            for q in range(0, 8, 2):
                dve.wait_ge(ps_full, q + 1)
                nc.vector.tensor_copy(uc[:, 4 * q:4 * q + 4, 0:CH],
                                      psum[:, q, :].rearrange("p (g c) -> p g c", g=4)).then_inc(dve_read, 1)
            dve.wait_ge(ps_full, 9)
            nc.vector.tensor_copy(uc[:, :, CH:CHS], psum[:, 0, 0:GROUPS * NB].rearrange(
                "p (g c) -> p g c", g=GROUPS)).then_inc(dve_read, 1)

        @block.scalar
        def _(act):
            for q in range(1, 8, 2):
                act.wait_ge(ps_full, q + 1)
                nc.scalar.copy(uc[:, 4 * q:4 * q + 4, 0:CH],
                               psum[:, q, :].rearrange("p (g c) -> p g c", g=4)).then_inc(act_read, 1)

        @block.tensor
        def _(pe):
            for q in range(8):
                for g in range(4):
                    mm = pe.transpose(psum[:, q, g * P:(g + 1) * P],
                                      t["u"][:, 4 * q + g].rearrange("p s j -> p (s j)"), cst["ident"][:])
                mm.then_inc(ps_full, 1)
            pe.wait_ge(us_made, 1)
            pe.wait_ge(dve_read, 1)
            for g in range(GROUPS):
                mm = pe.transpose(psum[:, 0, g * NB:(g + 1) * NB], us_g[:, g].rearrange("p s j -> p (s j)"),
                                  cst["ident"][0:NB, 0:NB])
            mm.then_inc(ps_full, 1)


def ssm_scan_phase(nc, cst, psum, a, o, scr, t, s):
    M, QM = PAIRS, 4
    with ExitStack() as ctx:
        def sb(name, shape, dt=F32):
            return ctx.enter_context(nc.sbuf_tensor(name, shape, dt))

        def sem(name):
            return new_sem(nc, name)

        hx = sb("hx", [P, 2, M, 1 + CH + NB])
        g_sb = sb("g_sb", [P, 2, M, CHS])
        q1, q2 = sb("q1", [P, QM, CH]), sb("q2", [P, QM, CH])
        sr, si = sb("sr", [P, QM, CH]), sb("si", [P, QM, CH])
        decay = sb("decay", [P, M, CH])
        h0 = sb("h0", [P, 2, P])
        hf = sb("hf", [P, 2, NB, M])
        hf_t = sb("hf_t", [P, 2, P])
        hp_t = sb("hp_t", [M, 2, P])
        ys = s["rot"][0:NB].rearrange("p i m c -> p (i m c)").rearrange("p (t x) -> p t x", t=NT)
        h0_land, h0_ps, h0_put, g_ps, g_read = (sem(n) for n in ("h0_land", "h0_ps", "h0_put", "g_ps", "g_read"))
        states_made, y_ps, y_dve, y_act = (sem(n) for n in ("states_made", "y_ps", "y_dve", "y_act"))
        ys_ps, ys_read, fin_ps, fin_read, fin_out = (sem(n) for n in ("ys_ps", "ys_read", "fin_ps", "fin_read",
                                                                      "fin_out"))
        chain = Chain(sem("scan_chain"))
        block = ctx.enter_context(nc.Block())
        y = t["u"][:].rearrange("p g s j -> p (g s j)").rearrange("p (t x) -> p t x", t=LC)

        @block.sync
        def _(sp):
            for i, n in enumerate(("state_ssm_re", "state_ssm_im")):
                sp.dma_start(h0[:, i], a[n][0].rearrange("b (m g) p -> (b m) (g p)", g=2)).then_inc(h0_land, 16)
            sp.wait_ge(fin_read, 1)
            for i, n in enumerate(("re", "im")):
                sp.dma_start(o[n + "_prompt"][0, 0].rearrange("(m g) p -> m (g p)", g=2), hp_t[:, i]
                             ).then_inc(fin_out, 16)
                sp.dma_start(o[n + "_sample"][0].rearrange("b (m g) p -> (b m) (g p)", g=2), hf_t[:, i]
                             ).then_inc(fin_out, 16)
            sp.wait_ge(ys_read, 8)
            sp.dma_start(scr["ys"].rearrange("(b t) c -> b t c", t=NT), ys).then_inc(fin_out, 16)
            sp.wait_ge(fin_out, 80)

        @block.vector
        def _(dve):
            def seq(ins):
                dve.wait_ge(chain.sem, chain.did(ins))

            def tt(out, x, z, op):
                seq(nc.vector.tensor_tensor(out, x, z, op))

            nc.vector.tensor_copy(decay[:], s["r8"][:].unsqueeze(2).broadcast_to([P, M, CH]))
            seq(nc.vector.memset(hx[:, :, :, 0], 0.0))
            seq(nc.vector.memset(decay[:, :, 0:1], 0.0))
            dve.wait_ge(h0_ps, 1)
            for i in range(2):
                last = nc.vector.tensor_copy(hx[:, i, :, 1 + CH:], psum[:, i, 0:P].rearrange(
                    "p (b m) -> p m b", b=NB))
            last.then_inc(h0_put, 1)
            rot = s["rot"]
            for q in range(M // QM):
                ms = slice(q * QM, (q + 1) * QM)
                for m in range(q * QM, (q + 1) * QM):
                    for i in range(2):
                        n = 2 * m + i
                        dve.wait_ge(g_ps, n + 1)
                        ins = nc.vector.tensor_copy(g_sb[:, i, m], psum[:, 2 + n % 6, 0:CHS])
                        ins.then_inc(g_read, 1)
                dve.wait_ge(g_read, 2 * (q + 1) * QM)
                gr, gi = g_sb[:, 0, ms, 0:CH], g_sb[:, 1, ms, 0:CH]
                cr, ci = rot[:, 0, ms], rot[:, 1, ms]
                tt(sr[:], gr, cr, ALU.mult)
                tt(q1[:], gi, ci, ALU.mult)
                tt(sr[:], sr[:], q1[:], ALU.add)
                tt(si[:], gi, cr, ALU.mult)
                tt(q2[:], gr, ci, ALU.mult)
                tt(si[:], si[:], q2[:], ALU.subtract)
                flat = "p m c -> p (m c)"
                dec = decay[:, ms].rearrange(flat)
                seq(nc.vector.tensor_tensor_scan(q1[:].rearrange(flat), dec, sr[:].rearrange(flat), 0.0,
                                                 ALU.mult, ALU.add))
                seq(nc.vector.tensor_tensor_scan(q2[:].rearrange(flat), dec, si[:].rearrange(flat), 0.0,
                                                 ALU.mult, ALU.add))
                hr, hi = hx[:, 0, ms, 1:1 + CH], hx[:, 1, ms, 1:1 + CH]
                tt(hr, q1[:], cr, ALU.mult)
                tt(sr[:], q2[:], ci, ALU.mult)
                tt(hr, hr, sr[:], ALU.subtract)
                tt(hi, q1[:], ci, ALU.mult)
                tt(si[:], q2[:], cr, ALU.mult)
                nc.vector.tensor_tensor(hi, hi, si[:], ALU.add).then_inc(states_made, 1)
            b0 = [h0_ for h0_ in (hx[:, 0, :, 1 + CH:].rearrange("p m b -> p b m"),
                                  hx[:, 1, :, 1 + CH:].rearrange("p m b -> p b m"))]
            a8 = [s["a8"][:, i].unsqueeze(1).broadcast_to([P, NB, M]) for i in range(2)]
            tmp = q1[:].rearrange("p m c -> p (m c)")[:, 0:P].rearrange("p (b m) -> p b m", b=NB)
            dve.wait_ge(states_made, 4)
            dve.wait_ge(h0_put, 1)
            gs = [g_sb[:, i, :, CH:].rearrange("p m b -> p b m") for i in range(2)]
            tt(hf[:, 0], b0[0], a8[0], ALU.mult)
            tt(tmp, b0[1], a8[1], ALU.mult)
            tt(hf[:, 0], hf[:, 0], tmp, ALU.subtract)
            tt(hf[:, 0], hf[:, 0], gs[0], ALU.add)
            tt(hf[:, 1], b0[0], a8[1], ALU.mult)
            tt(tmp, b0[1], a8[0], ALU.mult)
            tt(hf[:, 1], hf[:, 1], tmp, ALU.add)
            nc.vector.tensor_tensor(hf[:, 1], hf[:, 1], gs[1], ALU.add).then_inc(states_made, 1)
            for q in range(0, 8, 2):
                dve.wait_ge(y_ps, q + 1)
                out = y.rearrange("p t (m g i) -> p g m t i", g=2, i=GCH)[:, q % 2, 4 * (q // 2):4 * (q // 2) + 4]
                nc.vector.tensor_copy(out, psum[:, 2 + q % 4, :].rearrange("p (g t i) -> p g t i", g=4, t=LC)
                                      ).then_inc(y_dve, 1)
            for q in range(8):
                dve.wait_ge(ys_ps, q + 1)
                out = ys.rearrange("p t (m g i) -> p g m t i", g=2, i=GCH)[:, q % 2, 4 * (q // 2):4 * (q // 2) + 4]
                nc.vector.tensor_copy(out, psum[0:NB, 6 + q % 2, :].rearrange("p (g t i) -> p g t i", g=4, t=LC)
                                      ).then_inc(ys_read, 1)
            dve.wait_ge(fin_ps, 1)
            nc.vector.tensor_copy(hp_t[:], psum[0:M, 0, 0:2 * P].rearrange("p (i x) -> p i x", i=2))
            nc.vector.tensor_copy(hf_t[:], psum[:, 1, 0:2 * P].rearrange("p (i x) -> p i x", i=2)
                                  ).then_inc(fin_read, 1)

        @block.scalar
        def _(act):
            for q in range(1, 8, 2):
                act.wait_ge(y_ps, q + 1)
                for j in range(4):
                    out = y.rearrange("p t (m g i) -> p g m t i", g=2, i=GCH)[:, 1, 4 * (q // 2) + j]
                    last = nc.scalar.copy(out, psum[:, 2 + q % 4, j * P:(j + 1) * P].rearrange(
                        "p (t i) -> p t i", t=LC))
                last.then_inc(y_act, 1)

        @block.tensor
        def _(pe):
            uc = s["uc"]
            pe.wait_ge(h0_land, 32)
            for i in range(2):
                mm = pe.transpose(psum[:, i, 0:P], h0[:, i], cst["ident"][:])
            mm.then_inc(h0_ps, 1)
            for m in range(M):
                for i in range(2):
                    n = 2 * m + i
                    if n >= 6:
                        pe.wait_ge(g_read, n - 5)
                    for g in range(2):
                        mm = pe.matmul(psum[64 * g:64 * g + 64, 2 + n % 6, 0:CHS],
                                       s["wT"][:, i, m, 64 * g:64 * g + 64], uc[:, 2 * m + g],
                                       start=True, stop=True)
                    mm.then_inc(g_ps, 1)
            pe.wait_ge(g_read, 2 * M)
            for q in range(8):
                pe.wait_ge(states_made, q // 2 + 1)
                if q >= 4:
                    if q % 2 == 0:
                        pe.wait_ge(y_dve, (q - 4) // 2 + 1)
                    else:
                        pe.wait_ge(y_act, (q - 4) // 2 + 1)
                rows = slice(64 * (q % 2), 64 * (q % 2) + 64)
                for j in range(4):
                    m = 4 * (q // 2) + j
                    g = 2 * m + q % 2
                    out = psum[:, 2 + q % 4, j * P:(j + 1) * P]
                    pe.matmul(out, uc[:, g, 0:CH], s["toep"][:, g].rearrange("p t i -> p (t i)"),
                              start=True, stop=False)
                    pe.matmul(out, hx[rows, 0, m, 0:CH], s["ca"][rows, 0, m].rearrange("p t i -> p (t i)"),
                              start=False, stop=False)
                    mm = pe.matmul(out, hx[rows, 1, m, 0:CH], s["ca"][rows, 1, m].rearrange("p t i -> p (t i)"),
                                   start=False, stop=True)
                mm.then_inc(y_ps, 1)
            pe.wait_ge(h0_put, 1)
            for q in range(8):
                if q >= 2:
                    pe.wait_ge(ys_read, q - 1)
                rows = slice(64 * (q % 2), 64 * (q % 2) + 64)
                for j in range(4):
                    m = 4 * (q // 2) + j
                    g = 2 * m + q % 2
                    out = psum[0:NB, 6 + q % 2, j * P:(j + 1) * P]
                    pe.matmul(out, uc[:, g, CH:CHS], s["toep"][:, g].rearrange("p t i -> p (t i)"),
                              start=True, stop=False)
                    pe.matmul(out, hx[rows, 0, m, 1 + CH:], s["ca"][rows, 0, m].rearrange("p t i -> p (t i)"),
                              start=False, stop=False)
                    mm = pe.matmul(out, hx[rows, 1, m, 1 + CH:], s["ca"][rows, 1, m].rearrange("p t i -> p (t i)"),
                                   start=False, stop=True)
                mm.then_inc(ys_ps, 1)
            pe.wait_ge(states_made, 5)
            for i in range(2):
                pe.transpose(psum[0:M, 0, i * P:(i + 1) * P], hx[:, i, :, CH], cst["ident"][:])
                mm = pe.transpose(psum[:, 1, i * P:(i + 1) * P], hf[:, i].rearrange("p b m -> p (b m)"),
                                  cst["ident"][:])
            mm.then_inc(fin_ps, 1)


def score_off(i):
    return P * i * (i + 1) // 2


def index_phase(nc, cst, psum, a, t, x):
    NCUT = PAGES * PAGE // 512
    with ExitStack() as ctx:
        def sb(name, shape, dt=F32):
            return ctx.enter_context(nc.sbuf_tensor(name, shape, dt))

        def sem(name):
            return new_sem(nc, name)

        KR = 3
        psc, ssc, gidx = x["psc"], x["ssc"], x["gidx"]
        relu = sb("relu", [P, 4, 512])
        wis = sb("wis", [P, TILES, IH])
        pt = sb("pt", [P, NB], I32)
        sub = sb("sub", [P, 1], I32)
        subf = sb("subf", [P, 1])
        kx = sb("kx", [P, KR, PAGES, IDX])
        kxT = sb("kxT", [P, 2, PAGES // 2, P])
        qib = sb("qib", [P, IH, NS])
        qi2 = sb("qi2", [P, NB, IH, NT])
        wT = sb("wT", [IH, NS])
        expand = sb("expand", [IH, IH * NT])
        same_t = sb("same_t", [IH * NT, NB, NT])
        rowi = sb("rowi", [P, NT], I32)
        coli = sb("coli", [P, NT], I32)
        wm = sb("wm", [IH * NT, NS])
        w8 = sb("w8", [IH * NT, NB, NS])
        rs = sb("rs", [IH * NT, 2, 512])
        tail = sb("tail", [NS, NT])
        pt_land, sub_made, idx_made, qib_land = (sem(n) for n in ("pt_land", "sub_made", "idx_made", "qib_land"))
        kx_land = [sem(f"kx_land{i}") for i in range(KR)]
        wis_made, d_ps, r_made, r_used = (sem(n) for n in ("wis_made", "d_ps", "r_made", "r_used"))
        masked, tab_made = sem("masked"), sem("tab_made")
        small_ps, w_put, kxT_ps, kxT_read = (sem(n) for n in ("small_ps", "w_put", "kxT_ps", "kxT_read"))
        sd_ps, sr_made, ws_ps = sem("sd_ps"), sem("sr_made"), sem("ws_ps")
        chain = Chain(sem("index_chain"))
        groups = [(i, c, min(c + 512, (i + 1) * P), h) for i in range(TILES)
                  for c in range(0, (i + 1) * P, 512) for h in range(IH)]
        block = ctx.enter_context(nc.Block())

        @block.sync
        def _(sp):
            for r in range(8):
                sp.dma_start(pt[r:P:8], a["page_table"].rearrange("b j -> j b"),
                             allow_slow_non_contiguous=True).then_inc(pt_land, 16)
            for h in range(IH):
                for half in range(2):
                    sp.dma_start(qib[64 * half:64 * half + 64, h],
                                 t["qiT"][64 * (h % 2):64 * (h % 2) + 64, h // 2, SEQ:TOK]).then_inc(qib_land, 16)

        @block.gpsimd
        def _(pool):
            nc.gpsimd.iota(sub[:], pattern=[[0, 1]], base=0, channel_multiplier=1).then_inc(sub_made, 1)
            nc.gpsimd.iota(rowi[:], pattern=[[0, NT]], base=0, channel_multiplier=1)
            nc.gpsimd.iota(coli[:], pattern=[[1, NT]], base=0, channel_multiplier=0).then_inc(sub_made, 1)
            nc.gpsimd.memset(expand[:], 1.0).then_inc(tab_made, 1)
            nc.gpsimd.memset(same_t[:], 0.0).then_inc(tab_made, 1)
            nc.gpsimd.memset(w8[:], 0.0).then_inc(tab_made, 1)
            pool.wait_ge(tab_made, 3)
            nc.gpsimd.affine_select(out=expand[:].rearrange("q (h t) -> q h t", h=IH),
                                    in_=expand[:].rearrange("q (h t) -> q h t", h=IH),
                                    pattern=[[-1, IH], [0, NT]], compare_op=ALU.is_equal, fill=0.0, base=0,
                                    channel_multiplier=1).then_inc(tab_made, 1)
            for h in range(IH):
                pool.wait_ge(tab_made, 4 + h)
                nc.gpsimd.affine_select(out=same_t[:], in_=same_t[:], pattern=[[0, NB], [-1, NT]],
                                        compare_op=ALU.not_equal, fill=1.0, base=-NT * h,
                                        channel_multiplier=1).then_inc(tab_made, 1)
            pool.wait_ge(idx_made, 1)
            for b in range(NB):
                if b >= KR:
                    pool.wait_ge(kxT_ps, 2 * (b - KR) + 2)
                nc.gpsimd.indirect_dma_start(
                    out=kx[:, b % KR].rearrange("p k d -> p (k d)"), out_offset=None,
                    in_=a["cache_kidx"][0].rearrange("n (r k) d -> (n r) (k d)", r=8),
                    in_offset=bass.IndirectOffsetOnAxis(ap=gidx[:, b:b + 1], axis=0)).then_inc(kx_land[b % KR], 16)
            for i in range(TILES):
                pool.wait_ge(r_used, sum(1 for g in groups if g[0] <= i))
                diag = psc[:, score_off(i) + i * P:score_off(i) + (i + 1) * P]
                nc.gpsimd.affine_select(out=diag, in_=diag, pattern=[[-1, P]], compare_op=ALU.is_ge,
                                        fill=-3e38, base=0, channel_multiplier=1).then_inc(masked, 1)
            pool.wait_ge(masked, TILES)

        @block.scalar
        def _(act):
            for n, (i, c0, c1, h) in enumerate(groups):
                act.wait_ge(d_ps, n + 1)
                if n >= 4:
                    act.wait_ge(r_used, n - 3)
                nc.scalar.activation(relu[:, n % 4, 0:c1 - c0], psum[:, n % 4, 0:c1 - c0], ACT.Relu
                                     ).then_inc(r_made, 1)
            for n in range(5 * NB):
                w = 512 if n % 5 < 4 else NT
                act.wait_ge(sd_ps, n + 1)
                if n >= 2:
                    act.wait_ge(ws_ps, n - 1)
                nc.scalar.activation(rs[:, n % 2, 0:w], psum[0:IH * NT, 5 + n % 2, 0:w], ACT.Relu
                                     ).then_inc(sr_made, 1)

        @block.vector
        def _(dve):
            def seq(ins):
                dve.wait_ge(chain.sem, chain.did(ins))

            dve.wait_ge(sub_made, 2)
            dve.wait_ge(pt_land, 16 * 8)
            seq(nc.vector.tensor_scalar(sub[:], sub[:], 7, None, ALU.bitwise_and))
            seq(nc.vector.tensor_copy(subf[:], sub[:]))
            nc.vector.tensor_scalar(gidx[:], pt[:], 8.0, subf[:], ALU.mult, ALU.add).then_inc(idx_made, 1)
            seq(nc.vector.tensor_scalar(rowi[:], rowi[:], 7, None, ALU.bitwise_and))
            seq(nc.vector.tensor_tensor(tail[:], rowi[0:NS], coli[0:NS], ALU.is_ge))
            seq(nc.vector.tensor_scalar(tail[:], tail[:], -1.0, 3e38, ALU.add, ALU.mult))
            scale = float(IDX) ** -0.5 * float(IH) ** -0.5
            nc.vector.tensor_scalar(wis[:], t["kiwi"][:, 0:TILES, IDX:], scale, None, ALU.mult
                                    ).then_inc(wis_made, 1)
            dve.wait_ge(qib_land, 16 * 8)
            nc.vector.tensor_copy(qi2[:].rearrange("p b h t -> p h b t"),
                                  qib[:].rearrange("p h (b t) -> p h b t", b=NB)).then_inc(w_put, 1)
            dve.wait_ge(small_ps, 1)
            nc.vector.tensor_copy(wT[:], psum[0:IH, 7, 0:NS]).then_inc(w_put, 1)
            dve.wait_ge(small_ps, 2)
            dve.wait_ge(tab_made, 8)
            seq(nc.vector.scalar_tensor_tensor(wm[:], psum[0:IH * NT, 7, 0:NS], scale,
                                               same_t[:].rearrange("q b t -> q (b t)"), ALU.mult, ALU.mult))
            for b in range(NB):
                last = nc.vector.tensor_copy(w8[:, b, b * NT:(b + 1) * NT], wm[:, b * NT:(b + 1) * NT])
            last.then_inc(w_put, 1)
            dve.wait_ge(wis_made, 1)
            for n, (i, c0, c1, h) in enumerate(groups):
                dve.wait_ge(r_made, n + 1)
                acc = psc[:, score_off(i) + c0:score_off(i) + c1]
                if h == 0:
                    ins = nc.vector.tensor_scalar(acc, relu[:, n % 4, 0:c1 - c0], wis[:, i, 0:1], None, ALU.mult)
                else:
                    dve.wait_ge(r_used, n)
                    ins = nc.vector.scalar_tensor_tensor(acc, relu[:, n % 4, 0:c1 - c0], wis[:, i, h:h + 1], acc,
                                                         ALU.mult, ALU.add)
                ins.then_inc(r_used, 1)
            for g in range(2 * NB):
                b, q = divmod(g, 2)
                dve.wait_ge(kxT_ps, g + 1)
                if b >= 2:
                    dve.wait_ge(sd_ps, 5 * (b - 2) + 4)
                nc.vector.tensor_copy(kxT[:, b % 2, 4 * q:4 * q + 4],
                                      psum[:, 7, :].rearrange("p (j k) -> p j k", j=4)).then_inc(kxT_read, 1)
            dve.wait_ge(ws_ps, 5 * NB)
            nat = ssc[:, 0:PAST].rearrange("r (k j e) -> r e j k", j=PAGES // 2, e=2)
            for c in range(4):
                e, q = divmod(c, 2)
                nc.vector.tensor_copy(nat[:, e, 4 * q:4 * q + 4],
                                      psum[0:NS, c, :].rearrange("r (j k) -> r j k", j=4))
            nc.vector.tensor_tensor(ssc[:, PAST:], psum[0:NS, 4, 0:NT], tail[:], ALU.add)

        @block.tensor
        def _(pe):
            pe.transpose(psum[0:IH, 7, 0:NS], t["kiwi"][0:NS, TILES, IDX:], cst["ident"][0:NS, 0:NS]
                         ).then_inc(small_ps, 1)
            pe.wait_ge(w_put, 2)
            pe.wait_ge(tab_made, 4)
            pe.matmul(psum[0:IH * NT, 7, 0:NS], expand[:], wT[:], start=True, stop=True).then_inc(small_ps, 1)
            for n, (i, c0, c1, h) in enumerate(groups):
                if n >= 4:
                    pe.wait_ge(r_made, n - 3)
                rows = slice(64 * (h % 2), 64 * (h % 2) + 64)
                pe.matmul(psum[:, n % 4, 0:c1 - c0], t["qiT"][rows, h // 2, i * P:(i + 1) * P],
                          t["kiT"][rows, 0, c0:c1], start=True, stop=True).then_inc(d_ps, 1)
            pe.wait_ge(r_made, len(groups))
            pe.wait_ge(w_put, 3)
            for b in range(NB):
                pe.wait_ge(kx_land[b % KR], 16 * (b // KR + 1))
                for q in range(2):
                    if 2 * b + q >= 1:
                        pe.wait_ge(kxT_read, 2 * b + q)
                    for j in range(4):
                        mm = pe.transpose(psum[:, 7, j * P:(j + 1) * P],
                                          kx[:, b % KR, 8 * q + 2 * j:8 * q + 2 * j + 2].rearrange("p k d -> p (k d)"),
                                          cst["ident"][:])
                    mm.then_inc(kxT_ps, 1)
                pe.wait_ge(kxT_read, 2 * b + 2)
                for c in range(6):
                    if c < 5:
                        n = 5 * b + c
                        if n >= 2:
                            pe.wait_ge(sr_made, n - 1)
                        e, q = divmod(c, 2)
                        rows = slice(64 * e, 64 * e + 64) if c < 4 else slice(0, 64)
                        rhs = kxT[rows, b % 2, 4 * q:4 * q + 4].rearrange("p j k -> p (j k)") if c < 4 else \
                            t["kiT"][rows, 0, SEQ + b * NT:SEQ + (b + 1) * NT]
                        w = 512 if c < 4 else NT
                        pe.matmul(psum[0:IH * NT, 5 + n % 2, 0:w], qi2[rows, b].rearrange("p h t -> p (h t)"),
                                  rhs, start=True, stop=True).then_inc(sd_ps, 1)
                    if c >= 1:
                        n = 5 * b + c - 1
                        w = 512 if c - 1 < 4 else NT
                        pe.wait_ge(sr_made, n + 1)
                        pe.matmul(psum[0:NS, c - 1, 0:w], w8[:, b], rs[:, n % 2, 0:w],
                                  start=(b == 0), stop=(b == NB - 1)).then_inc(ws_ps, 1)


def topk_phase(nc, cst, x):
    R = TILES - 2 + 1
    o2 = score_off(2)
    W = score_off(TILES) - o2
    with ExitStack() as ctx:
        def sb(name, shape, dt=F32):
            return ctx.enter_context(nc.sbuf_tensor(name, shape, dt))

        def sem(name):
            return new_sem(nc, name)

        WA = W + KEYS
        hi, lo = sb("hi", [P, WA], U16), sb("lo", [P, WA], U16)
        key = sb("key", [P, WA], I32)
        junk = sb("junk", [P, KEYS], BF16)
        thr, tlo, cand, cnt, kk, ge = (sb(n, [P, R]) for n in ("thr", "tlo", "cand", "cnt", "kk", "ge"))
        bit = sb("bit", [P, 1])
        one = sb("one", [P, 1])
        sel, eq, eh = (sb(n, [P, KEYS], BF16) for n in ("sel", "eq", "eh"))
        rank = sb("rank", [P, KEYS], U16)
        chain = Chain(sem("topk_chain"))
        sel0 = sem("sel0")
        block = ctx.enter_context(nc.Block())
        regions = [(P, score_off(i) - o2, (i + 1) * P) for i in range(2, TILES)] + [(NS, W, KEYS)]

        @block.gpsimd
        def _(pool):
            nc.gpsimd.memset(x["pbias"][:, 0:o2], 0.0).then_inc(sel0, 1)
            for i in range(2):
                diag = x["pbias"][:, score_off(i) + i * P:score_off(i) + (i + 1) * P]
                pool.wait_ge(sel0, 1)
                nc.gpsimd.affine_select(out=diag, in_=diag, pattern=[[-1, P]], compare_op=ALU.is_ge,
                                        fill=NEG, base=0, channel_multiplier=1).then_inc(sel0, 1)
            pool.wait_ge(sel0, 3)

        @block.vector
        def _(dve):
            def seq(ins):
                dve.wait_ge(chain.sem, chain.did(ins))

            nc.vector.memset(cnt[:], 0.0)
            nc.vector.memset(thr[:], 0.0)
            nc.vector.memset(tlo[:], 0.0)
            nc.vector.memset(one[:], 1.0)
            seq(nc.vector.memset(kk[:], float(TOPK)))
            for rows, src, first, n in ((P, x["psc"][:, o2:], 0, W), (NS, x["ssc"][:], W, KEYS)):
                kr = key[0:rows, first:first + n]
                si = src.bitcast(I32)
                seq(nc.vector.tensor_scalar(src, src, 0.0, None, ALU.add))
                seq(nc.vector.tensor_scalar(kr, si, 31, 0x7FFFFFFF, ALU.arith_shift_right, ALU.bitwise_and))
                seq(nc.vector.tensor_tensor(kr, kr, si, ALU.bitwise_xor))
                halves = kr.bitcast(U16).rearrange("p (n e) -> p n e", e=2)
                nc.vector.tensor_scalar(hi[0:rows, first:first + n], halves[:, :, 1], 0x8000, None,
                                        ALU.bitwise_xor)
                seq(nc.vector.tensor_copy(lo[0:rows, first:first + n], halves[:, :, 0]))

            def search(half, t):
                seq(nc.vector.memset(bit[:], 32768.0))
                start = chain.n
                PER = R + 4
                with dve.Fori(0, 16) as it:
                    base = start + it * PER
                    nc.vector.tensor_scalar(cand[:], t[:], bit[:], None, ALU.add).then_inc(chain.sem, 1)
                    dve.wait_ge(chain.sem, base + 1)
                    for r, (rows, first, n) in enumerate(regions):
                        nc.vector.tensor_scalar(junk[0:rows, 0:n], half[0:rows, first:first + n],
                                                cand[0:rows, r:r + 1], 0.0, ALU.is_ge, ALU.add,
                                                accum_out=cnt[0:rows, r:r + 1]).then_inc(chain.sem, 1)
                        dve.wait_ge(chain.sem, base + 2 + r)
                    nc.vector.tensor_tensor(ge[:], cnt[:], kk[:], ALU.is_ge).then_inc(chain.sem, 1)
                    dve.wait_ge(chain.sem, base + R + 2)
                    nc.vector.scalar_tensor_tensor(t[:], ge[:], bit[:], t[:], ALU.mult, ALU.add
                                                   ).then_inc(chain.sem, 1)
                    dve.wait_ge(chain.sem, base + R + 3)
                    nc.vector.tensor_scalar(bit[:], bit[:], 0.5, None, ALU.mult).then_inc(chain.sem, 1)
                    dve.wait_ge(chain.sem, base + R + 4)
                chain.n = start + 16 * PER
            search(hi, thr)
            for r, (rows, first, n) in enumerate(regions):
                h, l = hi[0:rows, first:first + n], lo[0:rows, first:first + n]
                seq(nc.vector.tensor_scalar(junk[0:rows, 0:n], h, thr[0:rows, r:r + 1], 0.0, ALU.is_gt, ALU.add,
                                            accum_out=cnt[0:rows, r:r + 1]))
                seq(nc.vector.scalar_tensor_tensor(l, h, thr[0:rows, r:r + 1], l, ALU.is_equal, ALU.mult))
            seq(nc.vector.tensor_tensor(kk[:], kk[:], cnt[:], ALU.subtract))
            search(lo, tlo)
            for r, (rows, first, n) in enumerate(regions):
                h, l = hi[0:rows, first:first + n], lo[0:rows, first:first + n]
                th, tl = thr[0:rows, r:r + 1], tlo[0:rows, r:r + 1]
                s_, e_, m_, k_ = sel[0:rows, 0:n], eq[0:rows, 0:n], eh[0:rows, 0:n], rank[0:rows, 0:n]
                nc.vector.tensor_scalar(s_, h, th, None, ALU.is_gt)
                seq(nc.vector.tensor_scalar(m_, h, th, None, ALU.is_equal))
                nc.vector.scalar_tensor_tensor(e_, l, tl, m_, ALU.is_equal, ALU.mult)
                seq(nc.vector.scalar_tensor_tensor(s_, l, tl, s_, ALU.is_gt, ALU.add,
                                                   accum_out=cnt[0:rows, r:r + 1]))
                seq(nc.vector.tensor_tensor_scan(k_, one[0:rows].broadcast_to([rows, n]), e_, 0.0,
                                                 ALU.mult, ALU.add))
                seq(nc.vector.tensor_scalar(ge[0:rows, r:r + 1], cnt[0:rows, r:r + 1], -1.0, float(TOPK),
                                            ALU.mult, ALU.add))
                seq(nc.vector.scalar_tensor_tensor(e_, k_, ge[0:rows, r:r + 1], e_, ALU.is_le, ALU.mult))
                seq(nc.vector.tensor_tensor(s_, s_, e_, ALU.add))
                out = x["pbias"][:, o2 + first:o2 + first + n] if r < R - 1 else x["sbias"][:]
                seq(nc.vector.tensor_scalar(out, s_, -1.0, -NEG, ALU.add, ALU.mult))


def head_place(h):
    m, r = divmod(h, 4)
    return 2 * m + r % 2, slice(64 * (r // 2), 64 * (r // 2) + 64), m


def prompt_attention_phase(nc, cst, psum, t, x, att):
    scale = float(HD) ** -0.5
    steps = [(i, h) for i in range(TILES) for h in range(HEADS)]
    parts = [(n, c, min(c + 4, i + 1)) for n, (i, h) in enumerate(steps) for c in range(0, i + 1, 4)]
    first_part = [min(g for g, p in enumerate(parts) if p[0] == n) for n in range(len(steps))] + [len(parts)]
    with ExitStack() as ctx:
        def sb(name, shape, dt=F32):
            return ctx.enter_context(nc.sbuf_tensor(name, shape, dt))

        def sem(name):
            return new_sem(nc, name)

        sm = sb("sm", [P, 2, SEQ])
        pT = sb("pT", [P, 2, TILES, P])
        mx, nmx = sb("mx", [P, HEADS * TILES]), sb("nmx", [P, HEADS * TILES])
        rsum, rinv = sb("rsum", [P, HEADS * TILES]), sb("rinv", [P, HEADS * TILES])
        s_ps, sm_made, max_made, p_made = (sem(n) for n in ("s_ps", "sm_made", "max_made", "p_made"))
        pt_ps, pt_act, pt_dve, o_ps, inv_made, o_read = (sem(n) for n in (
            "pt_ps", "pt_act", "pt_dve", "o_ps", "inv_made", "o_read"))
        block = ctx.enter_context(nc.Block())

        def read_part(eng, copy, g, done):
            n, c0, c1 = parts[g]
            eng.wait_ge(pt_ps, g + 1)
            if n >= 2:
                eng.wait_ge(o_ps, n - 1)
            copy(pT[:, n % 2, c0:c1], psum[:, 4 + g % 2, 0:(c1 - c0) * P].rearrange("p (c q) -> p c q", q=P)
                 ).then_inc(done, 1)

        @block.vector
        def _(dve):
            def largest(n):
                i, h = steps[n]
                w = (i + 1) * P
                dve.wait_ge(s_ps, n + 1)
                if n >= 2:
                    dve.wait_ge(pt_ps, first_part[n - 1])
                bank = 2 * (n % 2)
                nc.vector.tensor_tensor_reduce(
                    sm[:, n % 2, 0:w], psum[:, bank:bank + 2, :].rearrange("p a b -> p (a b)")[:, 0:w],
                    x["pbias"][:, score_off(i):score_off(i) + w], scale, -3e38, ALU.add, ALU.max,
                    mx[:, n:n + 1]).then_inc(sm_made, 1)
                dve.wait_ge(sm_made, n + 1)
                nc.vector.tensor_scalar(nmx[:, n:n + 1], mx[:, n:n + 1], -1.0, None, ALU.mult).then_inc(max_made, 1)

            def finish(i):
                cols = slice(i * HEADS, (i + 1) * HEADS)
                dve.wait_ge(p_made, (i + 1) * HEADS)
                nc.vector.reciprocal(rinv[:, cols], rsum[:, cols]).then_inc(inv_made, 1)
                dve.wait_ge(inv_made, i + 1)
                dve.wait_ge(o_ps, (i + 1) * HEADS)
                nc.vector.tensor_tensor(att[:, i].rearrange("p (h d) -> p h d", h=HEADS),
                                        psum[:, 6 + i % 2, :].rearrange("p (h d) -> p h d", h=HEADS),
                                        rinv[:, cols].unsqueeze(2).broadcast_to([P, HEADS, HD]), ALU.mult
                                        ).then_inc(o_read, 1)

            largest(0)
            for n in range(len(steps)):
                if n + 1 < len(steps):
                    largest(n + 1)
                for g in range(first_part[n], first_part[n + 1]):
                    if g % 2 == 1:
                        read_part(dve, nc.vector.tensor_copy, g, pt_dve)
                if n % HEADS == 1 and n > HEADS:
                    finish(n // HEADS - 1)
            finish(TILES - 1)

        @block.scalar
        def _(act):
            def exps(n):
                w = (steps[n][0] + 1) * P
                act.wait_ge(max_made, n + 1)
                nc.scalar.activation(sm[:, n % 2, 0:w], sm[:, n % 2, 0:w], ACT.Exp, bias=nmx[:, n:n + 1],
                                     accum_out=rsum[:, n:n + 1]).then_inc(p_made, 1)

            exps(0)
            for n in range(len(steps)):
                if n + 1 < len(steps):
                    exps(n + 1)
                for g in range(first_part[n], first_part[n + 1]):
                    if g % 2 == 0:
                        read_part(act, nc.scalar.copy, g, pt_act)

        @block.tensor
        def _(pe):
            def scores(n):
                i, h = steps[n]
                qb, rows, kb = head_place(h)
                if n >= 2:
                    pe.wait_ge(sm_made, n - 1)
                for c in range(0, (i + 1) * P, 512):
                    w = min(512, (i + 1) * P - c)
                    mm = pe.matmul(psum[:, 2 * (n % 2) + c // 512, 0:w], t["qT"][rows, qb, i * P:(i + 1) * P],
                                   t["kT"][rows, kb, c:c + w], start=True, stop=True)
                mm.then_inc(s_ps, 1)

            def transposes(n):
                pe.wait_ge(p_made, n + 1)
                for g in range(first_part[n], first_part[n + 1]):
                    _, c0, c1 = parts[g]
                    if g >= 2:
                        pe.wait_ge(pt_act if g % 2 == 0 else pt_dve, g // 2)
                    for c in range(c0, c1):
                        mm = pe.transpose(psum[:, 4 + g % 2, (c - c0) * P:(c - c0 + 1) * P],
                                          sm[:, n % 2, c * P:(c + 1) * P], cst["ident"][:])
                    mm.then_inc(pt_ps, 1)

            def values(n):
                i, h = steps[n]
                done = first_part[n + 1]
                pe.wait_ge(pt_act, (done + 1) // 2)
                if done >= 2:
                    pe.wait_ge(pt_dve, done // 2)
                if h == 0 and i >= 2:
                    pe.wait_ge(o_read, i - 1)
                for c in range(i + 1):
                    mm = pe.matmul(psum[:, 6 + i % 2, h * HD:(h + 1) * HD], pT[:, n % 2, c],
                                   t["v"][:, c, (h // 2) * HD:(h // 2 + 1) * HD], start=(c == 0), stop=(c == i))
                mm.then_inc(o_ps, 1)

            scores(0)
            for n in range(len(steps)):
                if n + 1 < len(steps):
                    scores(n + 1)
                transposes(n)
                if n >= 1:
                    values(n - 1)
            values(len(steps) - 1)


def sample_attention_phase(nc, cst, psum, a, scr, t, x):
    scale = float(HD) ** -0.5
    HT = HEADS * NT
    groups = []

    def add_k(b):
        groups.extend(("k", b, j) for j in range(PAGES // 2))

    add_k(0)
    for b in range(NB):
        if b + 1 < NB:
            add_k(b + 1)
        groups.extend(("p", b, j) for j in range(3))
    num = {g: n for n, g in enumerate(groups)}

    with ExitStack() as ctx:
        def sb(name, shape, dt=F32):
            return ctx.enter_context(nc.sbuf_tensor(name, shape, dt))

        def sem(name):
            return new_sem(nc, name)

        kc = sb("kc", [P, 2, PAGES, KVH * HD])
        vc = sb("vc", [P, 2, PAGES, KVH * HD])
        kcT = sb("kcT", [P, 2, PAGES, P])
        qbd = sb("qbd", [P, 2, NB, HT])
        rep = sb("rep", [NS, NB, HEADS, NT], BF16)
        pr = sb("pr", [HT, KEYS])
        prT = sb("prT", [P, PAGES + 1, HT])
        vn = sb("vn", [NT, NB, KVH * HD])
        own = sb("own", [HT, KVH])
        oe = sb("oe", [HT, KVH, HD])
        os_ = sb("os_sb", [HT, 2, HD])
        m2, m1, s2, s1 = sb("m2", [HT, 2]), sb("m1", [HT, 1]), sb("s2", [HT, 2]), sb("s1", [HT, 1])
        k_land = [sem(f"kc_land{i}") for i in range(2)]
        v_land = [sem(f"vc_land{i}") for i in range(2)]
        vn_land, setup, own_made = sem("vn_land"), sem("setup"), sem("own_made")
        s_ps, m_made, p_made, sum_made = (sem(n) for n in ("ss_ps", "sm2_made", "sp_made", "ssum_made"))
        tr_ps, tr_dve, tr_act, o_ps, o_read, o_made = (sem(n) for n in ("tr_ps", "tr_dve", "tr_act", "so_ps",
                                                                        "so_read", "so_made"))
        o_out = [sem(f"so_out{i}") for i in range(2)]
        chain = Chain(sem("sample_chain"))
        block = ctx.enter_context(nc.Block())

        @block.gpsimd
        def _(pool):
            nc.gpsimd.memset(own[:], 1.0).then_inc(own_made, 1)
            pool.wait_ge(own_made, 1)
            nc.gpsimd.affine_select(out=own[:], in_=own[:], pattern=[[-2 * NT, KVH]], compare_op=ALU.is_ge,
                                    fill=0.0, base=0, channel_multiplier=1).then_inc(own_made, 1)
            pool.wait_ge(own_made, 2)
            nc.gpsimd.affine_select(out=own[:], in_=own[:], pattern=[[2 * NT, KVH]], compare_op=ALU.is_ge,
                                    fill=0.0, base=2 * NT - 1, channel_multiplier=-1).then_inc(own_made, 1)
            for b in range(NB):
                if b >= 2:
                    pool.wait_ge(tr_ps, num[("k", b - 2, 7)] + 1)
                for dst, src, land in ((kc, "cache_k", k_land), (vc, "cache_v", v_land)):
                    if b >= 2 and src == "cache_v":
                        pool.wait_ge(o_ps, b - 1)
                    nc.gpsimd.indirect_dma_start(
                        out=dst[:, b % 2].rearrange("p k d -> p (k d)"), out_offset=None,
                        in_=a[src][0].rearrange("n (r k) h d -> (n r) (k h d)", r=8),
                        in_offset=bass.IndirectOffsetOnAxis(ap=x["gidx"][:, b:b + 1], axis=0)
                    ).then_inc(land[b % 2], 16)

        @block.sync
        def _(sp):
            for b in range(NB):
                sp.dma_start(vn[:, b], t["v"][b * NT:(b + 1) * NT, TILES]).then_inc(vn_land, 16)
            for b in range(NB):
                sp.wait_ge(o_made, b + 1)
                for h in range(HEADS):
                    sp.dma_start(scr["os"][b * NT:(b + 1) * NT, h * HD:(h + 1) * HD],
                                 os_[h * NT:(h + 1) * NT, b % 2]).then_inc(o_out[b % 2], 16)
            for i in range(2):
                sp.wait_ge(o_out[i], 16 * HEADS * NB // 2)

        def read_group(eng, copy, g, done):
            kind, b, j = groups[g]
            eng.wait_ge(tr_ps, g + 1)
            bank = psum[:, 5 + g % 2, :]
            if kind == "k":
                if b >= 1:
                    eng.wait_ge(s_ps, b)
                copy(kcT[:, :, 2 * j:2 * j + 2].rearrange("p m k q -> p k m q"),
                     bank.rearrange("p (k m q) -> p k m q", k=2, m=2)).then_inc(done, 1)
            else:
                if b >= 1:
                    eng.wait_ge(o_ps, b)
                if j < 2:
                    copy(prT[:, 8 * j:8 * j + 8], bank.rearrange("p (k r) -> p k r", k=8)).then_inc(done, 1)
                else:
                    copy(prT[0:NT, PAGES], bank[0:NT, 0:HT]).then_inc(done, 1)

        def groups_of(b):
            lo = num[("k", b + 1, 0)] if b + 1 < NB else num[("p", b, 0)]
            return range(lo, num[("p", b, 2)] + 1)

        @block.vector
        def _(dve):
            def seq(ins):
                dve.wait_ge(chain.sem, chain.did(ins))

            seq(nc.vector.memset(qbd[:], 0.0))
            for m in range(2):
                for half in range(2):
                    for c in range(2):
                        h = 4 * m + 2 * half + c
                        rows = slice(64 * half, 64 * half + 64)
                        nc.vector.tensor_copy(
                            qbd[rows, m, :, h * NT:(h + 1) * NT],
                            t["qT"][rows, 2 * m + c, SEQ:TOK].rearrange("p (b t) -> p b t", b=NB))
            nc.vector.tensor_copy(rep[:], cst["ident"][0:NS, 0:NS].rearrange("r (b t) -> r b t", b=NB)
                                  .unsqueeze(2).broadcast_to([NS, NB, HEADS, NT])).then_inc(setup, 1)
            for g in range(0, 8, 2):
                read_group(dve, nc.vector.tensor_copy, g, tr_dve)
            dve.wait_ge(own_made, 3)
            for b in range(NB):
                dve.wait_ge(s_ps, b + 1)
                nc.vector.tensor_reduce(m2[:, 0:1], psum[0:HT, 0:4, :].rearrange("p a b -> p (a b)"), AX, ALU.max)
                seq(nc.vector.tensor_reduce(m2[:, 1:2], psum[0:HT, 4, 0:NT], AX, ALU.max))
                if b >= 1:
                    dve.wait_ge(p_made, b)
                seq(nc.vector.tensor_reduce(m1[:], m2[:], AX, ALU.max))
                nc.vector.tensor_scalar(m1[:], m1[:], -scale, None, ALU.mult).then_inc(m_made, 1)
                for g in groups_of(b):
                    if g % 2 == 0:
                        read_group(dve, nc.vector.tensor_copy, g, tr_dve)
                dve.wait_ge(p_made, b + 1)
                seq(nc.vector.tensor_reduce(s1[:], s2[:], AX, ALU.add))
                nc.vector.reciprocal(s1[:], s1[:]).then_inc(sum_made, 1)
                dve.wait_ge(sum_made, b + 1)
                dve.wait_ge(o_ps, b + 1)
                nc.vector.tensor_tensor(oe[:], psum[0:HT, 7, 0:KVH * HD].rearrange("p (k d) -> p k d", k=KVH),
                                        own[:].unsqueeze(2).broadcast_to([HT, KVH, HD]), ALU.mult
                                        ).then_inc(o_read, 1)
                dve.wait_ge(o_read, b + 1)
                if b >= 2:
                    dve.wait_ge(o_out[b % 2], 16 * HEADS * (b // 2))
                seq(nc.vector.tensor_reduce(os_[:, b % 2], oe[:].rearrange("p k d -> p d k"), AX, ALU.add))
                nc.vector.tensor_scalar(os_[:, b % 2], os_[:, b % 2], s1[:], None, ALU.mult).then_inc(o_made, 1)

        @block.scalar
        def _(act):
            for g in range(1, 8, 2):
                read_group(act, nc.scalar.copy, g, tr_act)
            for b in range(NB):
                act.wait_ge(m_made, b + 1)
                if b >= 1:
                    act.wait_ge(tr_ps, num[("p", b - 1, 2)] + 1)
                    act.wait_ge(sum_made, b)
                nc.scalar.activation(pr[:, 0:PAST], psum[0:HT, 0:4, :].rearrange("p a b -> p (a b)"), ACT.Exp,
                                     bias=m1[:], scale=scale, accum_out=s2[:, 0:1])
                nc.scalar.activation(pr[:, PAST:], psum[0:HT, 4, 0:NT], ACT.Exp,
                                     bias=m1[:], scale=scale, accum_out=s2[:, 1:2]).then_inc(p_made, 1)
                for g in groups_of(b):
                    if g % 2 == 1:
                        read_group(act, nc.scalar.copy, g, tr_act)

        @block.tensor
        def _(pe):
            def transposes(g):
                kind, b, j = groups[g]
                if g >= 2:
                    pe.wait_ge(tr_dve if g % 2 == 0 else tr_act, g // 2)
                if kind == "k":
                    if j == 0:
                        pe.wait_ge(k_land[b % 2], 16 * (b // 2 + 1))
                    for k in range(2):
                        for m in range(2):
                            mm = pe.transpose(psum[:, 5 + g % 2, (2 * k + m) * P:(2 * k + m + 1) * P],
                                              kc[:, b % 2, 2 * j + k, m * P:(m + 1) * P], cst["ident"][:])
                else:
                    pe.wait_ge(p_made, b + 1)
                    if j < 2:
                        for k in range(8):
                            mm = pe.transpose(psum[:, 5 + g % 2, k * HT:(k + 1) * HT],
                                              pr[:, (8 * j + k) * P:(8 * j + k + 1) * P], cst["ident"][0:HT, 0:HT])
                    else:
                        mm = pe.transpose(psum[0:NT, 5 + g % 2, 0:HT], pr[:, PAST:], cst["ident"][0:HT, 0:HT])
                mm.then_inc(tr_ps, 1)

            def all_read(g):
                pe.wait_ge(tr_dve, g // 2 + 1)
                pe.wait_ge(tr_act, (g + 1) // 2)

            for g in range(8):
                transposes(g)
            pe.wait_ge(setup, 1)
            pe.wait_ge(vn_land, 16 * NB)
            for b in range(NB):
                all_read(num[("k", b, 7)])
                if b >= 1:
                    pe.wait_ge(p_made, b)
                bias = x["sbias"][:, 0:PAST].rearrange("r (p k) -> r k p", k=PAGES)
                for c in range(5):
                    w = 512 if c < 4 else NT
                    pe.matmul(psum[0:HT, c, 0:w], rep[:, b].rearrange("r h t -> r (h t)"),
                              bias[:, 4 * c:4 * c + 4] if c < 4 else x["sbias"][:, PAST:], start=True, stop=False)
                    for m in range(2):
                        rhs = kcT[:, m, 4 * c:4 * c + 4].rearrange("p k q -> p (k q)") if c < 4 else \
                            t["kT"][:, m, SEQ + b * NT:SEQ + (b + 1) * NT]
                        mm = pe.matmul(psum[0:HT, c, 0:w], qbd[:, m, b], rhs, start=False, stop=(m == 1))
                mm.then_inc(s_ps, 1)
                for g in groups_of(b):
                    transposes(g)
                all_read(num[("p", b, 2)])
                pe.wait_ge(v_land[b % 2], 16 * (b // 2 + 1))
                if b >= 1:
                    pe.wait_ge(o_read, b)
                for k in range(PAGES + 1):
                    lhs, rhs = (prT[:, k], vc[:, b % 2, k]) if k < PAGES else (prT[0:NT, k], vn[:, b])
                    mm = pe.matmul(psum[0:HT, 7, 0:KVH * HD], lhs, rhs, start=(k == 0), stop=(k == PAGES))
                mm.then_inc(o_ps, 1)


def mix_phase(nc, cst, psum, a, scr, t, att, mixT):
    NTL = TILES + 1
    KH = D_SSM // P
    with ExitStack() as ctx:
        def sb(name, shape, dt=F32):
            return ctx.enter_context(nc.sbuf_tensor(name, shape, dt))

        def sem(name):
            return new_sem(nc, name)

        yss = sb("yss", [NS, D_SSM])
        wg = sb("wg", [P, KH, D_SSM])
        bg = sb("bg", [P, D_SSM])
        gcol = sb("gcol", [P, 2, KH])
        gT = sb("gT", [P, 2, KH, P])
        zb = sb("zb", [P, 2, D_SSM])
        sq = sb("sq", [P, D_SSM])
        ss = sb("ss", [P, 2, NTL])
        rstd = sb("rstd", [P, 2, NTL])
        ys_land, os_land, wg_land = sem("ys_land"), sem("os_land"), sem("wg_land")
        ss_clear, gelu, gT_ps, gT_made, z_ps, z_made, sig, glu, sums, root, inv = (sem(n) for n in (
            "ss_clear", "gelu", "gT_ps", "gT_made", "z_ps", "z_made", "sig", "glu", "sums", "root", "inv"))
        scaled, m_ps, m_dve, m_act = (sem(n) for n in ("scaled", "m_ps", "m_dve", "m_act"))
        sq_done = sem("sq_done")
        block = ctx.enter_context(nc.Block())
        y = t["u"][:].rearrange("p g s j -> p (g s j)").rearrange("p (t x) -> p t x", t=LC)

        def ssm_rows(i):
            return y[:, i] if i < TILES else yss[:]

        def att_rows(i):
            return att[:, i] if i < TILES else att[0:NS, TILES]

        def rows_of(i):
            return P if i < TILES else NS

        def sum_squares(act, i):
            r = rows_of(i)
            act.wait_ge(glu, i + 1)
            act.wait_ge(sq_done, NTL + i)
            nc.scalar.activation(sq[0:r], ssm_rows(i), ACT.Square, accum_out=ss[0:r, 0, i:i + 1]
                                 ).then_inc(sq_done, 1)

        def transposed(g, eng):
            i, half = divmod(g, 2)
            r = rows_of(i)
            for k in range(KH):
                if i == TILES:
                    out = mixT[:, KH * half + k, SEQ:TOK]
                elif half == 0:
                    out = mixT[:, k, i:SEQ:LC]
                else:
                    out = mixT[:, KH + k, i * P:(i + 1) * P]
                src = psum[:, 4 + g % 4, k * P:k * P + r]
                if g % 2 == 0:
                    ins = nc.vector.tensor_scalar(out, src, gcol[:, half, k:k + 1], None, ALU.mult)
                else:
                    ins = nc.scalar.activation(out, src, ACT.Copy, scale=gcol[:, half, k:k + 1])
            ins.then_inc(m_dve if g % 2 == 0 else m_act, 1)

        @block.sync
        def _(sp):
            sp.dma_start(yss[:], scr["ys"]).then_inc(ys_land, 16)
            sp.dma_start(att[0:NS, TILES], scr["os"]).then_inc(os_land, 16)
            sp.dma_start(wg[:], a["w_glu"][0].rearrange("(p k) n -> p k n", k=KH)).then_inc(wg_land, 16)
            sp.dma_start(bg[:], a["b_glu"][0].partition_broadcast(P)).then_inc(wg_land, 16)
            sp.dma_start(gcol[:, 0], a["g_ssm_out"][0].rearrange("(p k) -> p k", k=KH)).then_inc(wg_land, 16)
            sp.dma_start(gcol[:, 1], a["g_att_out"][0].rearrange("(p k) -> p k", k=KH)).then_inc(wg_land, 16)

        @block.scalar
        def _(act):
            act.wait_ge(ys_land, 16)
            for i in range(NTL):
                nc.scalar.activation(ssm_rows(i), ssm_rows(i), ACT.Gelu_apprx_tanh).then_inc(gelu, 1)
            act.wait_ge(os_land, 16)
            act.wait_ge(ss_clear, 1)
            for i in range(NTL):
                r = rows_of(i)
                if i:
                    act.wait_ge(sq_done, i)
                nc.scalar.activation(sq[0:r], att_rows(i), ACT.Square, accum_out=ss[0:r, 1, i:i + 1]
                                     ).then_inc(sq_done, 1)
            for i in range(NTL):
                r = rows_of(i)
                act.wait_ge(z_made, i + 1)
                nc.scalar.activation(zb[0:r, i % 2], zb[0:r, i % 2], ACT.Sigmoid).then_inc(sig, 1)
                if i >= 1:
                    sum_squares(act, i - 1)
            sum_squares(act, NTL - 1)
            act.wait_ge(sums, 1)
            nc.scalar.activation(rstd[:], ss[:], ACT.Sqrt).then_inc(root, 1)
            for g in range(1, 2 * NTL, 2):
                act.wait_ge(m_ps, g + 1)
                transposed(g, act)

        @block.vector
        def _(dve):
            nc.vector.memset(ss[:], 1.0).then_inc(ss_clear, 1)
            dve.wait_ge(wg_land, 64)
            for i in range(NTL + 1):
                if i < NTL:
                    r = rows_of(i)
                    dve.wait_ge(gT_ps, i + 1)
                    if i >= 2:
                        dve.wait_ge(z_ps, i - 1)
                    nc.vector.tensor_copy(gT[:, i % 2, :, 0:r], psum[:, i % 2, :].rearrange(
                        "p (k q) -> p k q", k=KH)[:, :, 0:r]).then_inc(gT_made, 1)
                if i >= 1:
                    j, r = i - 1, rows_of(i - 1)
                    dve.wait_ge(z_ps, j + 1)
                    if j >= 2:
                        dve.wait_ge(glu, j - 1)
                    nc.vector.tensor_tensor(zb[0:r, j % 2], psum[0:r, 2 + j % 2, :], bg[0:r], ALU.add
                                            ).then_inc(z_made, 1)
                    dve.wait_ge(sig, j + 1)
                    nc.vector.tensor_tensor(ssm_rows(j), ssm_rows(j), zb[0:r, j % 2], ALU.mult).then_inc(glu, 1)
            dve.wait_ge(sq_done, 2 * NTL)
            nc.vector.tensor_scalar(ss[:], ss[:], 1.0 / D_SSM, EPS, ALU.mult, ALU.add).then_inc(sums, 1)
            dve.wait_ge(root, 1)
            nc.vector.reciprocal(rstd[:], rstd[:]).then_inc(inv, 1)
            dve.wait_ge(inv, 1)
            for i in range(NTL):
                r = rows_of(i)
                nc.vector.tensor_scalar(ssm_rows(i), ssm_rows(i), rstd[0:r, 0, i:i + 1], None, ALU.mult
                                        ).then_inc(scaled, 1)
                nc.vector.tensor_scalar(att_rows(i), att_rows(i), rstd[0:r, 1, i:i + 1], None, ALU.mult
                                        ).then_inc(scaled, 1)
            for g in range(0, 2 * NTL, 2):
                dve.wait_ge(m_ps, g + 1)
                transposed(g, dve)

        @block.tensor
        def _(pe):
            ident = cst["ident"]
            for i in range(NTL + 1):
                if i < NTL:
                    r = rows_of(i)
                    pe.wait_ge(gelu, i + 1)
                    if i >= 2:
                        pe.wait_ge(gT_made, i - 1)
                    for k in range(KH):
                        mm = pe.transpose(psum[:, i % 2, k * P:k * P + r], ssm_rows(i)[:, k:D_SSM:KH],
                                          ident[0:r, 0:r])
                    mm.then_inc(gT_ps, 1)
                if i >= 1:
                    j, r = i - 1, rows_of(i - 1)
                    pe.wait_ge(gT_made, j + 1)
                    pe.wait_ge(wg_land, 64)
                    if j >= 2:
                        pe.wait_ge(z_made, j - 1)
                    for k in range(KH):
                        mm = pe.matmul(psum[0:r, 2 + j % 2, :], gT[:, j % 2, k, 0:r], wg[:, k],
                                       start=(k == 0), stop=(k == KH - 1))
                    mm.then_inc(z_ps, 1)
            for g in range(2 * NTL):
                i, half = divmod(g, 2)
                r = rows_of(i)
                pe.wait_ge(scaled, g + 1)
                if g >= 4:
                    pe.wait_ge(m_dve if g % 2 == 0 else m_act, (g - 4) // 2 + 1)
                src = ssm_rows(i) if half == 0 else att_rows(i)
                for k in range(KH):
                    mm = pe.transpose(psum[:, 4 + g % 4, k * P:k * P + r], src[:, k:D_SSM:KH], ident[0:r, 0:r])
                mm.then_inc(m_ps, 1)


def load_rows(sp, dst, scr_mod, part, samples, land):
    if samples:
        for b in range(NB):
            sp.dma_start(dst[b * NT:(b + 1) * NT], scr_mod[1 + b, part:part + D].partition_broadcast(NT)
                         ).then_inc(land, 16)
    else:
        sp.dma_start(dst, scr_mod[0, part:part + D].partition_broadcast(P)).then_inc(land, 16)


def out_phase(nc, cst, psum, a, scr, mixT, aff):
    NTL = TILES + 1
    with ExitStack() as ctx:
        def sb(name, shape, dt=F32):
            return ctx.enter_context(nc.sbuf_tensor(name, shape, dt))

        def sem(name):
            return new_sem(nc, name)

        wo = sb("wo", [P, KD, D])
        wr = sb("wr", [P, KD, EXPERTS])
        xt = sb("xt2", [P, 2, D])
        g1, sc2, sh2 = (sb(n, [P, 2, D]) for n in ("g1", "sc2", "sh2"))
        lg, lb = sb("lg", [P, D]), sb("lb", [P, D])
        xr = sb("xr", [P, 2, D])
        x1 = sb("x1", [P, 2, D])
        h2 = sb("h2", [P, 2, D])
        sq = sb("sq2", [P, D])
        zero = sb("zero", [P, D])
        st = sb("st", [P, NTL, 4])
        wo_land, mod_land, sc_made, zero_made = (sem(n) for n in ("wo_land", "mod_land", "sc_made", "zero_made"))
        x_land = [sem(f"x2_land{i}") for i in range(2)]
        mixed_ps, mixed_read, x_made, sq_made, root, xhat, x1_made, h2_made = (sem(n) for n in (
            "mixed_ps", "mixed_read", "x_made", "sq_made", "root2", "xhat", "x1_made", "h2_made"))
        st_clear = sem("st_clear")
        hT_ps, hT_act, aff_ps, aff_made = (sem(n) for n in ("hT_ps", "hT_act", "aff_ps", "aff_made"))
        x1_out = [sem(f"x1_out{i}") for i in range(2)]
        h2_out = [sem(f"h2_out{i}") for i in range(2)]
        z_out = sem("z_out")
        chain = Chain(sem("out_chain"))
        block = ctx.enter_context(nc.Block())

        def rows_of(i):
            return P if i < TILES else NS

        def cols_of(i):
            return slice(i, SEQ, LC) if i < TILES else slice(SEQ, TOK)

        def scores(dve, i):
            r = rows_of(i)
            dve.wait_ge(aff_ps, i + 1)
            nc.vector.tensor_copy(aff[0:r, i], psum[0:r, 6 + i % 2, 0:EXPERTS]).then_inc(aff_made, 1)

        @block.sync
        def _(sp):
            for half in range(2):
                sp.dma_start(wo[:, 4 * half:4 * half + 4],
                             a["w_out"][0, half * D_SSM:(half + 1) * D_SSM].rearrange("(p k) n -> p k n", k=4)
                             ).then_inc(wo_land, 16)
            for s in range(2):
                for dst, part in ((g1, G1), (sc2, SC2), (sh2, SH2)):
                    load_rows(sp, dst[:, s], scr["mod"], part, s, mod_land)
            sp.dma_start(lg[:], a["ln1_g"][0].partition_broadcast(P)).then_inc(mod_land, 16)
            sp.dma_start(lb[:], a["ln1_b"][0].partition_broadcast(P)).then_inc(mod_land, 16)
            sp.dma_start(wr[:], a["w_router"][0].rearrange("(p k) e -> p k e", k=KD)).then_inc(mod_land, 16)
            for i in range(NTL):
                r = rows_of(i)
                if i >= 2:
                    sp.wait_ge(x_made, i - 1)
                src = a["x_prompt"][0].rearrange("(c s) d -> s c d", s=LC)[i] if i < TILES else \
                    a["x_sample"].rearrange("b t d -> (b t) d")
                sp.dma_start(xt[0:r, i % 2], src).then_inc(x_land[i % 2], 16)
            sp.wait_ge(zero_made, 1)
            for name in ("h2", "acc"):
                sp.dma_start(scr[name][SEQ + NS:TRASH], zero[0:NS]).then_inc(z_out, 16)
                sp.dma_start(scr[name][TRASH:], zero[:]).then_inc(z_out, 16)
            sp.wait_ge(z_out, 64)

        @block.gpsimd
        def _(pool):
            nc.gpsimd.memset(zero[:], 0.0).then_inc(zero_made, 1)
            pool.wait_ge(mod_land, 16 * (3 * (1 + NB) + 3))
            for i in range(NTL):
                r = rows_of(i)
                pool.wait_ge(xhat, i + 1)
                if i >= 2:
                    pool.wait_ge(x1_out[i % 2], 16 * (i // 2))
                    pool.wait_ge(h2_out[i % 2], 16 * (i // 2))
                    pool.wait_ge(h2_made, i - 1)
                nc.gpsimd.tensor_tensor(x1[0:r, i % 2], xr[0:r, i % 2], lg[0:r], ALU.mult).then_inc(x1_made, 1)
                pool.wait_ge(x1_made, 2 * i + 1)
                nc.gpsimd.tensor_tensor(x1[0:r, i % 2], x1[0:r, i % 2], lb[0:r], ALU.add).then_inc(x1_made, 1)
                pool.wait_ge(x1_made, 2 * i + 2)
                pool.dma_start(scr["x1"][i * P:i * P + r], x1[0:r, i % 2]).then_inc(x1_out[i % 2], 16)
                pool.wait_ge(h2_made, i + 1)
                pool.dma_start(scr["h2"][i * P:i * P + r], h2[0:r, i % 2]).then_inc(h2_out[i % 2], 16)
            pool.wait_ge(x1_out[0], 16 * 5)
            pool.wait_ge(x1_out[1], 16 * 4)
            pool.wait_ge(h2_out[0], 16 * 5)
            pool.wait_ge(h2_out[1], 16 * 4)

        @block.scalar
        def _(act):
            for i in range(NTL + 1):
                if i < NTL:
                    r = rows_of(i)
                    act.wait_ge(x_made, i + 1)
                    if i:
                        act.wait_ge(sq_made, 2 * i)
                    nc.scalar.activation(st[0:r, i, 1:2], st[0:r, i, 0:1], ACT.Copy, scale=-1.0 / D
                                         ).then_inc(sq_made, 1)
                    act.wait_ge(sq_made, 2 * i + 1)
                    nc.scalar.activation(sq[0:r], xr[0:r, i % 2], ACT.Square, bias=st[0:r, i, 1:2],
                                         accum_out=st[0:r, i, 2:3]).then_inc(sq_made, 1)
                if i >= 1:
                    j = i - 1
                    r = rows_of(j)
                    for q in range(2):
                        act.wait_ge(hT_ps, 2 * j + q + 1)
                        nc.scalar.copy(mixT[:, 4 * q:4 * q + 4, cols_of(j)],
                                       psum[:, 4 + q, :].rearrange("p (k c) -> p k c", k=4)[:, :, 0:r]
                                       ).then_inc(hT_act, 1)
                if i < NTL:
                    r = rows_of(i)
                    act.wait_ge(st_clear, i + 1)
                    nc.scalar.activation(st[0:r, i, 3:4], st[0:r, i, 2:3], ACT.Sqrt).then_inc(root, 1)

        @block.vector
        def _(dve):
            def seq(ins):
                dve.wait_ge(chain.sem, chain.did(ins))

            dve.wait_ge(mod_land, 16 * (3 * (1 + NB) + 3))
            seq(nc.vector.tensor_scalar(sc2[:, 0], sc2[:, 0], 1.0, None, ALU.add))
            seq(nc.vector.tensor_scalar(sc2[0:NS, 1], sc2[0:NS, 1], 1.0, None, ALU.add))
            for i in range(NTL):
                r, s = rows_of(i), i // TILES
                xri = xr[0:r, i % 2]
                dve.wait_ge(mixed_ps, i + 1)
                if i >= 2:
                    dve.wait_ge(x1_made, 2 * (i - 1))
                nc.vector.tensor_tensor(xri, psum[0:r, 2 * (i % 2):2 * (i % 2) + 2, :].rearrange("p a b -> p (a b)"),
                                        g1[0:r, s], ALU.mult).then_inc(mixed_read, 1)
                dve.wait_ge(mixed_read, i + 1)
                dve.wait_ge(x_land[i % 2], 16 * (i // 2 + 1))
                nc.vector.scalar_tensor_tensor(xri, xt[0:r, i % 2], ALPHA, xri, ALU.mult, ALU.add,
                                               accum_out=st[0:r, i, 0:1]).then_inc(x_made, 1)
                if i >= 1:
                    scores(dve, i - 1)
                dve.wait_ge(sq_made, 2 * i + 2)
                nc.vector.tensor_scalar(st[0:r, i, 2:3], st[0:r, i, 2:3], 1.0 / D, EPS, ALU.mult, ALU.add
                                        ).then_inc(st_clear, 1)
                dve.wait_ge(root, i + 1)
                seq(nc.vector.reciprocal(st[0:r, i, 3:4], st[0:r, i, 3:4]))
                nc.vector.tensor_scalar(xri, xri, st[0:r, i, 1:2], st[0:r, i, 3:4], ALU.add, ALU.mult
                                        ).then_inc(xhat, 1)
                dve.wait_ge(x1_made, 2 * i + 2)
                if i >= 2:
                    dve.wait_ge(h2_out[i % 2], 16 * (i // 2))
                    dve.wait_ge(hT_ps, 2 * (i - 1))
                seq(nc.vector.tensor_tensor(h2[0:r, i % 2], x1[0:r, i % 2], sc2[0:r, s], ALU.mult))
                nc.vector.tensor_tensor(h2[0:r, i % 2], h2[0:r, i % 2], sh2[0:r, s], ALU.add).then_inc(h2_made, 1)
            scores(dve, NTL - 1)

        @block.tensor
        def _(pe):
            def mixed(i):
                r = rows_of(i)
                if i >= 2:
                    pe.wait_ge(mixed_read, i - 1)
                for n in range(2):
                    for k in range(KD):
                        mm = pe.matmul(psum[0:r, 2 * (i % 2) + n, :], mixT[:, k, cols_of(i)],
                                       wo[:, k, n * 512:(n + 1) * 512], start=(k == 0), stop=(k == KD - 1))
                mm.then_inc(mixed_ps, 1)

            pe.wait_ge(wo_land, 32)
            pe.wait_ge(mod_land, 16 * (3 * (1 + NB) + 3))
            mixed(0)
            for i in range(NTL):
                r = rows_of(i)
                if i + 1 < NTL:
                    mixed(i + 1)
                pe.wait_ge(h2_made, i + 1)
                for q in range(2):
                    if i >= 1:
                        pe.wait_ge(hT_act, 2 * (i - 1) + q + 1)
                    for k in range(4):
                        mm = pe.transpose(psum[:, 4 + q, k * P:k * P + r], h2[0:r, i % 2, 4 * q + k:D:KD],
                                          cst["ident"][0:r, 0:r])
                    mm.then_inc(hT_ps, 1)
                pe.wait_ge(hT_act, 2 * i + 2)
                if i >= 2:
                    pe.wait_ge(aff_made, i - 1)
                for k in range(KD):
                    mm = pe.matmul(psum[0:r, 6 + i % 2, 0:EXPERTS], mixT[:, k, cols_of(i)], wr[:, k],
                                   start=(k == 0), stop=(k == KD - 1))
                mm.then_inc(aff_ps, 1)


def tile_rows(i):
    return P if i < TILES else NS


def tile_cols(i):
    return slice(i, SEQ, LC) if i < TILES else slice(SEQ, TOK)


WBUF = 4
WLEN = KD * 2 * FE + 2 * D
T_EXP, T_BUF, T_FIRST, T_N, T_LEN = 0, P, 2 * P, 2 * P + EXPERTS, 2 * P + EXPERTS + 8


def fetch_expert(sp, a, r, e, s):
    dst = r["wx"][:, s, 0:KD * 2 * FE].rearrange("p (k f) -> p k f", k=KD)
    for j, name in enumerate(("w_e1", "w_e3")):
        sp.dma_start(dst[:, :, j * FE:(j + 1) * FE],
                     a[name][0, bass.ds(e, 1)].rearrange("o (p k) f -> p (o k) f", k=KD)
                     ).then_inc(r["wx_land"][s], 16)
    sp.dma_start(r["wx"][:, s, KD * 2 * FE:].rearrange("p (k n) -> p k n", k=2),
                 a["w_e2"][0, bass.ds(e, 1)].rearrange("o (p k) n -> p (o k) n", k=2)
                 ).then_inc(r["wx_land"][s], 16)


def route_phase(nc, cst, psum, a, scr, mixT, aff, r):
    NTL = TILES + 1
    NE = NTL * EXPERTS
    PART_B = 3
    with ExitStack() as ctx:
        def sb(name, shape, dt=F32):
            return ctx.enter_context(nc.sbuf_tensor(name, shape, dt))

        def sem(name):
            return new_sem(nc, name)

        w13 = sb("ws13", [P, KD, 2 * FE])
        w2 = sb("ws2", [P, 2, D])
        sa, hid, hidT = sb("sa", [P, 2, FE]), sb("hid", [P, 2, FE]), sb("hidT", [P, 2, 2, P])
        ysh = sb("ysh", [P, 2, D])
        br = sb("br", [P, EXPERTS])
        sc, sel, eq, rk, gate, slots, tmp, fresh = (sb(n, [P, NTL, EXPERTS]) for n in (
            "sc", "sel_e", "eq_e", "rk", "gate", "slots", "tmp_e", "fresh"))
        v8 = sb("v8", [P, NTL, 8])
        n1, n2 = sb("n1", [P, NTL]), sb("n2", [P, NTL])
        tot, offs = sb("tot", [P, NTL, EXPERTS]), sb("offs", [P, NTL + 1, EXPERTS])
        nb, inc, exc = (sb(n, [P, EXPERTS]) for n in ("nb", "inc", "exc"))
        one = sb("one_r", [P, EXPERTS])
        choice = sb("choice", [P, 2, TOPE, NTL])
        idx = sb("idx", [P, TOPE, NTL], I32)
        meta = sb("meta", [P, NTL, TOPE, 2])
        tok_i, tok_f = sb("tok_i", [P, NTL], I32), sb("tok_f", [P, NTL])
        dflt_i = sb("dflt_i", [P, NBLK], I32)
        dflt = sb("dflt", [P, NBLK, 2])
        part_i, part_f = sb("part_i", [P, 1], I32), sb("part_f", [P, 1])
        eb, ebi = sb("eb", [P, 1]), sb("ebi", [P, 2], I32)
        firsti = sb("firsti", [1, EXPERTS + 8], I32)
        st = sb("slot_tab", [NBLK, BLK, 2])

        w_land, br_land, iota_made, aff_sig, dflt_made, dflt_out = (sem(n) for n in (
            "ws_land", "br_land", "iota_made", "aff_sig", "dflt_made", "dflt_out"))
        up_ps, silu, hid_made, hT_ps, hT_made, dn_ps, y_read = (sem(n) for n in (
            "sh_up", "sh_silu", "sh_hid", "sh_hT", "sh_hTm", "sh_dn", "sh_y"))
        y_out = [sem(f"sh_out{i}") for i in range(2)]
        sel_made, cnt_ps, tab_made, tab_out, tab_in, meta_made, scattered, st_land, st_ps = (sem(n) for n in (
            "chosen", "cnt_ps", "steer_made", "steer_out", "steer_in", "meta_made", "scattered", "st_land", "st_ps"))
        aff_clear = sem("aff_clear")
        chain = Chain(sem("route_chain"))
        block = ctx.enter_context(nc.Block())

        @block.sync
        def _(sp):
            for j, n in enumerate(("w_s1", "w_s3")):
                sp.dma_start(w13[:, :, j * FE:(j + 1) * FE], a[n][0].rearrange("(p k) f -> p k f", k=KD)
                             ).then_inc(w_land, 16)
            sp.dma_start(w2[:], a["w_s2"][0].rearrange("(p k) n -> p k n", k=2)).then_inc(w_land, 16)
            sp.dma_start(br[:], a["b_router"][0].partition_broadcast(P)).then_inc(br_land, 16)
            for e in range(WBUF):
                fetch_expert(sp, a, r, e, e)
            sp.wait_ge(dflt_made, 1)
            sp.dma_start(scr["slots"].rearrange("(p j) c -> p j c", p=P), dflt[:]).then_inc(dflt_out, 16)
            for i in range(NTL):
                sp.wait_ge(y_read, i + 1)
                sp.dma_start(scr["acc"][i * P:i * P + tile_rows(i)], ysh[0:tile_rows(i), i % 2]
                             ).then_inc(y_out[i % 2], 16)
                if i == PART_B:
                    sp.wait_ge(tab_made, 1)
                    for dst, src in ((T_EXP, ebi[:, 0:1]), (T_BUF, ebi[:, 1:2])):
                        sp.dma_start(scr["tab"][0, dst:dst + P].rearrange("(p o) -> p o", o=1), src,
                                     allow_slow_non_contiguous=True).then_inc(tab_out, 16)
                    sp.dma_start(scr["tab"][:, T_FIRST:T_LEN], firsti[:]).then_inc(tab_out, 16)
                    sp.wait_ge(tab_out, 48)
                    sp.dma_start(r["tab"][:], scr["tab"]).then_inc(tab_in, 16)
            sp.wait_ge(scattered, 16 * TOPE * NTL)
            sp.dma_start(st[:], scr["slots"].rearrange("(b p) c -> b p c", p=BLK)).then_inc(st_land, 16)
            sp.wait_ge(y_out[0], 16 * 5)
            sp.wait_ge(y_out[1], 16 * 4)
            sp.wait_ge(tab_in, 16)

        @block.gpsimd
        def _(pool):
            nc.gpsimd.iota(tok_i[:], pattern=[[P, NTL]], base=0, channel_multiplier=1)
            nc.gpsimd.iota(part_i[:], pattern=[[0, 1]], base=0, channel_multiplier=1)
            nc.gpsimd.iota(dflt_i[:], pattern=[[1, NBLK]], base=0, channel_multiplier=NBLK).then_inc(iota_made, 1)
            pool.wait_ge(dflt_out, 16)
            pool.wait_ge(meta_made, 1)
            for i in range(NTL):
                n = tile_rows(i)
                for k in range(TOPE):
                    nc.gpsimd.indirect_dma_start(
                        out=scr["slots"], out_offset=bass.IndirectOffsetOnAxis(ap=idx[0:n, k, i:i + 1], axis=0),
                        in_=meta[0:n, i, k], in_offset=None).then_inc(scattered, 16)
            pool.wait_ge(scattered, 16 * TOPE * NTL)

        @block.scalar
        def _(act):
            act.wait_ge(aff_clear, 1)
            nc.scalar.activation(aff[:], aff[:], ACT.Sigmoid).then_inc(aff_sig, 1)

            def silu_of(i):
                n = tile_rows(i)
                act.wait_ge(up_ps, i + 1)
                if i >= 2:
                    act.wait_ge(hid_made, i - 1)
                nc.scalar.activation(sa[0:n, i % 2], psum[0:n, i % 2, 0:FE], ACT.Silu).then_inc(silu, 1)

            silu_of(0)
            for i in range(NTL):
                n = tile_rows(i)
                if i + 1 < NTL:
                    silu_of(i + 1)
                act.wait_ge(hT_ps, i + 1)
                if i >= 2:
                    act.wait_ge(dn_ps, i - 1)
                nc.scalar.copy(hidT[:, i % 2, :, 0:n], psum[:, 2, 0:2 * P].rearrange(
                    "p (k c) -> p k c", k=2)[:, :, 0:n]).then_inc(hT_made, 1)
                act.wait_ge(dn_ps, i + 1)
                if i >= 2:
                    act.wait_ge(y_out[i % 2], 16 * (i // 2))
                nc.scalar.copy(ysh[0:n, i % 2], psum[0:n, 4:6, :].rearrange("p a b -> p (a b)")).then_inc(y_read, 1)

        @block.vector
        def _(dve):
            def seq(ins):
                dve.wait_ge(chain.sem, chain.did(ins))

            def hidden(i):
                n = tile_rows(i)
                dve.wait_ge(silu, i + 1)
                if i >= 2:
                    dve.wait_ge(hT_ps, i - 1)
                nc.vector.tensor_tensor(hid[0:n, i % 2], sa[0:n, i % 2], psum[0:n, i % 2, FE:2 * FE], ALU.mult
                                        ).then_inc(hid_made, 1)

            flat = "p t e -> p (t e)"
            all_ = [P, NTL, EXPERTS]
            nc.vector.memset(aff[NS:P, TILES], 0.0).then_inc(aff_clear, 1)
            dve.wait_ge(iota_made, 1)
            seq(nc.vector.tensor_scalar(dflt_i[:], dflt_i[:], BLK - 1, None, ALU.bitwise_and))
            nc.vector.memset(dflt[:], 0.0)
            seq(nc.vector.memset(fresh[:], 1.0))
            nc.vector.tensor_copy(part_f[:], part_i[:])
            nc.vector.tensor_copy(tok_f[:], tok_i[:])
            nc.vector.memset(one[:], 1.0)
            seq(nc.vector.memset(fresh[:, :, 0:1], 0.0))
            nc.vector.tensor_scalar(dflt[:, :, 0], dflt_i[:], float(TRASH), None, ALU.add).then_inc(dflt_made, 1)
            dve.wait_ge(aff_sig, 1)
            dve.wait_ge(br_land, 16)
            seq(nc.vector.tensor_tensor(sc[:], aff[:], br[:].unsqueeze(1).broadcast_to(all_), ALU.add))
            for i in range(NTL):
                last = nc.vector.max(v8[:, i], sc[:, i])
            seq(last)
            least = v8[:, :, TOPE - 1:TOPE].broadcast_to(all_)
            nc.vector.tensor_tensor(eq[:], sc[:], least, ALU.is_equal)
            seq(nc.vector.tensor_tensor(sel[:], sc[:], least, ALU.is_gt))
            seq(nc.vector.tensor_reduce(n1[:], sel[:], AX, ALU.add))
            nc.vector.tensor_scalar(n2[:], n1[:], -1.0, float(TOPE), ALU.mult, ALU.add)
            seq(nc.vector.tensor_tensor_scan(rk[:].rearrange(flat), fresh[:].rearrange(flat),
                                             eq[:].rearrange(flat), 0.0, ALU.mult, ALU.add))
            seq(nc.vector.tensor_tensor(rk[:], rk[:], n2[:].unsqueeze(2).broadcast_to(all_), ALU.is_le))
            seq(nc.vector.tensor_tensor(eq[:], eq[:], rk[:], ALU.mult))
            seq(nc.vector.tensor_tensor(sel[:], sel[:], eq[:], ALU.add))
            nc.vector.memset(sel[NS:P, TILES], 0.0).then_inc(sel_made, 1)
            for i in range(PART_B):
                hidden(i)
            dve.wait_ge(sel_made, 1)
            seq(nc.vector.tensor_tensor(gate[:], aff[:], sel[:], ALU.mult))
            seq(nc.vector.tensor_reduce(n1[:], gate[:], AX, ALU.add))
            seq(nc.vector.tensor_scalar(n1[:], n1[:], 1e-30, None, ALU.max))
            seq(nc.vector.reciprocal(n1[:], n1[:]))
            seq(nc.vector.tensor_tensor(gate[:], gate[:], n1[:].unsqueeze(2).broadcast_to(all_), ALU.mult))
            seq(nc.vector.tensor_scalar(gate[:], gate[:], ROUTED_SCALE, None, ALU.mult))
            dve.wait_ge(cnt_ps, 1)
            nc.vector.tensor_copy(tot[:, 0:TILES].rearrange(flat), psum[:, 7, :])
            nc.vector.memset(offs[:, 0], 0.0)
            seq(nc.vector.tensor_copy(tot[:, TILES], psum[:, 6, EXPERTS:2 * EXPERTS]))
            for i in range(NTL):
                seq(nc.vector.tensor_tensor(offs[:, i + 1], offs[:, i], tot[:, i], ALU.add))
            count = offs[:, NTL]
            seq(nc.vector.tensor_scalar(nb[:], count, 0.0, None, ALU.is_gt))
            for i in range(1, -(-TOK // BLK)):
                seq(nc.vector.scalar_tensor_tensor(nb[:], count, float(i * BLK), nb[:], ALU.is_gt, ALU.add))
            seq(nc.vector.tensor_tensor_scan(inc[:], one[:], nb[:], 0.0, ALU.mult, ALU.add))
            seq(nc.vector.tensor_tensor(exc[:], inc[:], nb[:], ALU.subtract))
            seq(nc.vector.tensor_scalar(nb[:], inc[:], part_f[:], 0.0, ALU.is_le, ALU.add, accum_out=eb[:]))
            seq(nc.vector.tensor_copy(ebi[:, 0:1], eb[:]))
            nc.vector.memset(firsti[:], 0)
            seq(nc.vector.tensor_scalar(ebi[:, 1:2], ebi[:, 0:1], WBUF - 1, None, ALU.bitwise_and))
            seq(nc.vector.tensor_copy(firsti[:, 0:EXPERTS], exc[0:1]))
            nc.vector.tensor_copy(firsti[:, EXPERTS:EXPERTS + 1], inc[0:1, EXPERTS - 1:]).then_inc(tab_made, 1)
            seq(nc.vector.tensor_scalar(exc[:], exc[:], float(BLK), None, ALU.mult))
            seq(nc.vector.tensor_tensor(slots[:], offs[:, 0:NTL], exc[:].unsqueeze(1).broadcast_to(all_), ALU.add))
            seq(nc.vector.tensor_tensor(slots[:, 0:TILES].rearrange(flat), slots[:, 0:TILES].rearrange(flat),
                                        psum[:, 3, :], ALU.add))
            seq(nc.vector.tensor_tensor(slots[:, TILES], slots[:, TILES], psum[:, 6, 0:EXPERTS], ALU.add))
            seq(nc.vector.tensor_tensor(slots[:], slots[:], sel[:], ALU.mult))
            seq(nc.vector.tensor_tensor_scan(rk[:].rearrange(flat), fresh[:].rearrange(flat),
                                             sel[:].rearrange(flat), 0.0, ALU.mult, ALU.add))
            for k in range(TOPE):
                for j, src in enumerate((slots, gate)):
                    out = tmp if j == 0 else sc
                    seq(nc.vector.scalar_tensor_tensor(out[:].rearrange(flat), rk[:].rearrange(flat), float(k + 1),
                                                       src[:].rearrange(flat), ALU.is_equal, ALU.mult))
                    seq(nc.vector.tensor_reduce(choice[:, j, k], out[:], AX, ALU.add))
            nc.vector.tensor_copy(idx[:], choice[:, 0])
            nc.vector.tensor_copy(meta[:, :, :, 0], tok_f[:].unsqueeze(2).broadcast_to([P, NTL, TOPE]))
            nc.vector.tensor_copy(meta[:, :, :, 1], choice[:, 1].rearrange("p k t -> p t k")).then_inc(meta_made, 1)
            for i in range(PART_B, NTL):
                hidden(i)
            nc.vector.memset(r["slot_tok"][:, NBLK:], 0)
            nc.vector.memset(r["slot_gate"][:, NBLK:], 0.0)
            dve.wait_ge(st_ps, 1)
            nc.vector.tensor_copy(r["slot_tok"][:, 0:NBLK], psum[:, 6, 0:NBLK])
            nc.vector.tensor_copy(r["slot_gate"][:, 0:NBLK], psum[:, 6, P:P + NBLK])

        @block.tensor
        def _(pe):
            def up(i):
                n = tile_rows(i)
                if i >= 2:
                    pe.wait_ge(hid_made, i - 1)
                for k in range(KD):
                    mm = pe.matmul(psum[0:n, i % 2, :], mixT[:, k, tile_cols(i)], w13[:, k],
                                   start=(k == 0), stop=(k == KD - 1))
                mm.then_inc(up_ps, 1)

            pe.wait_ge(w_land, 48)
            up(0)
            for i in range(NTL):
                n = tile_rows(i)
                if i + 1 < NTL:
                    up(i + 1)
                if i == PART_B:
                    pe.wait_ge(sel_made, 1)
                    main = sel[:, 0:TILES].rearrange("p t e -> p (t e)")
                    pe.matmul(psum[:, 3, :], cst["before"][:], main, start=True, stop=True)
                    pe.matmul(psum[:, 6, 0:EXPERTS], cst["before"][:], sel[:, TILES], start=True, stop=True)
                    pe.matmul(psum[:, 7, :], cst["ones"][:], main, start=True, stop=True)
                    pe.matmul(psum[:, 6, EXPERTS:2 * EXPERTS], cst["ones"][:], sel[:, TILES],
                              start=True, stop=True).then_inc(cnt_ps, 1)
                pe.wait_ge(hid_made, i + 1)
                if i >= 1:
                    pe.wait_ge(hT_made, i)
                for k in range(2):
                    mm = pe.transpose(psum[:, 2, k * P:k * P + n], hid[0:n, i % 2, k:FE:2], cst["ident"][0:n, 0:n])
                mm.then_inc(hT_ps, 1)
                pe.wait_ge(hT_made, i + 1)
                if i >= 1:
                    pe.wait_ge(y_read, i)
                for c in range(2):
                    for k in range(2):
                        mm = pe.matmul(psum[0:n, 4 + c, :], hidT[:, i % 2, k, 0:n], w2[:, k, c * 512:(c + 1) * 512],
                                       start=(k == 0), stop=(k == 1))
                mm.then_inc(dn_ps, 1)
            pe.wait_ge(st_land, 16)
            pe.wait_ge(meta_made, 1)
            pe.transpose(psum[:, 6, 0:NBLK], st[:, :, 0], cst["ident"][0:NBLK, 0:NBLK])
            pe.transpose(psum[:, 6, P:P + NBLK], st[:, :, 1], cst["ident"][0:NBLK, 0:NBLK]).then_inc(st_ps, 1)


def expert_phase(nc, cst, psum, a, scr, r):
    UNROLL = 4
    with ExitStack() as ctx:
        def sb(name, shape, dt=F32):
            return ctx.enter_context(nc.sbuf_tensor(name, shape, dt))

        def sem(name):
            return new_sem(nc, name)

        wx, w_land = r["wx"], r["wx_land"]
        hg = sb("hg", [P, UNROLL, D])
        hT = sb("hT_x", [P, 2, KD, P])
        sa, hid, hidT = sb("sa_x", [P, 2, FE]), sb("hid_x", [P, FE]), sb("hidT_x", [P, 2, P])
        y = sb("y_x", [P, D])
        gi, si = sb("gather_idx", [P, UNROLL], I32), sb("add_idx", [P, 2], I32)
        spare = sb("spare_x", [P, 2])
        ready = sem("weights_ready")
        hg_land = [sem(f"hg_land{i}") for i in range(UNROLL)]
        idx_put = sem("idx_put")
        hT_ps, hT_dve, hT_act, up_ps, silu, hid_made, hidT_ps, hidT_made, dn_ps, y_dve, y_act, added = (
            sem(n) for n in ("x_hT", "x_hT_dve", "x_hT_act", "x_up", "x_silu", "x_hid", "x_hidT_ps", "x_hidT",
                             "x_dn", "x_y_dve", "x_y_act", "x_added"))
        block = ctx.enter_context(nc.Block())
        tab = r["tab"]

        def load(eng, place, most):
            return eng.value_load(tab[0:1, bass.ds(place, 1)], min_val=0, max_val=most)

        def blocks(eng, body):
            n = load(eng, T_N, NBLK)
            with eng.Fori(0, -(-NBLK // UNROLL)) as turn:
                for j in range(UNROLL):
                    b = UNROLL * turn + j
                    with eng.If(b < n):
                        body(b, j, turn, n)

        @block.sync
        def _(sp):
            for e in range(2):
                sp.wait_ge(w_land[e], 48)
                sp.sem_inc(ready, 1)
            with sp.Fori(1, EXPERTS // WBUF) as turn:
                for s in range(WBUF):
                    e = WBUF * turn + s
                    q = (s + 2) % WBUF
                    sp.wait_ge(w_land[q], 48 * (turn + 1) if s >= 2 else 48 * turn)
                    sp.sem_inc(ready, 1)
                    before = sp.value_load(tab[0:1, bass.ds(T_FIRST + e - WBUF + 1, 1)], min_val=0, max_val=NBLK)
                    sp.wait_ge(dn_ps, before + 1)
                    fetch_expert(sp, a, r, e, s)
            for s in (2, 3):
                sp.wait_ge(w_land[s], 48 * EXPERTS // WBUF)
                sp.sem_inc(ready, 1)

        @block.gpsimd
        def _(pool):
            def gather_index(b, j):
                nc.gpsimd.tensor_copy(gi[:, j:j + 1], r["slot_tok"][:, bass.ds(b, 1)]).then_inc(idx_put, 1)

            def gather(j):
                nc.gpsimd.indirect_dma_start(
                    out=hg[:, j], out_offset=None, in_=scr["h2"],
                    in_offset=bass.IndirectOffsetOnAxis(ap=gi[:, j:j + 1], axis=0)).then_inc(hg_land[j], 16)

            def pause():
                nc.gpsimd.tensor_tensor(spare[:, 1:2], spare[:, 0:1], spare[:, 0:1], ALU.add).then_inc(idx_put, 1)

            pool.dma_start(spare[:], scr["acc"][TRASH:TRASH + P, 0:2]).then_inc(added, 16)
            for j in range(3):
                gather_index(j, j)
            pool.wait_ge(idx_put, 3)
            pool.wait_ge(added, 16)
            for j in range(3):
                gather(j)

            def body(b, j, turn, n):
                ahead = (j + 3) % UNROLL
                pool.wait_ge(hT_ps, b + 1)
                gather_index(b + 3, ahead)
                pool.wait_ge(idx_put, 4 * b + 4)
                pause()
                with pool.If(b + 3 < n):
                    gather(ahead)
                pool.wait_ge(added, 16 * b + 16)
                nc.gpsimd.tensor_copy(si[:, j % 2:j % 2 + 1], r["slot_tok"][:, bass.ds(b, 1)]).then_inc(idx_put, 1)
                pool.wait_ge(idx_put, 4 * b + 6)
                pool.wait_ge(y_dve, b + 2)
                pool.wait_ge(y_act, b + 2)
                pause()
                nc.gpsimd.indirect_dma_start(
                    out=scr["acc"], out_offset=bass.IndirectOffsetOnAxis(ap=si[:, j % 2:j % 2 + 1], axis=0),
                    in_=y[:], in_offset=None, compute_op=ALU.add).then_inc(added, 16)

            blocks(pool, body)
            n = load(pool, T_N, NBLK)
            pool.wait_ge(added, 16 * n + 16)

        def read_hT(eng, copy, half, b_done, par, done):
            eng.wait_ge(hT_ps, b_done + 1)
            copy(hT[:, par, 4 * half:4 * half + 4], psum[:, half, :].rearrange("p (k c) -> p k c", k=4)
                 ).then_inc(done, 1)

        @block.scalar
        def _(act):
            def silu_of(par, done):
                act.wait_ge(up_ps, done)
                nc.scalar.activation(sa[:, par], psum[:, 2 + par, 0:FE], ACT.Silu).then_inc(silu, 1)

            nc.scalar.copy(y[:, 0:1], cst["ones"][:, 0:1]).then_inc(y_act, 1)
            read_hT(act, nc.scalar.copy, 1, 1, 0, hT_act)
            read_hT(act, nc.scalar.copy, 1, 2, 1, hT_act)
            silu_of(0, 1)

            def body(b, j, turn, n):
                par = j % 2
                act.wait_ge(hidT_ps, b + 2)
                nc.scalar.copy(hidT[:].rearrange("p k c -> p (k c)"), psum[:, 4, 0:2 * P]).then_inc(hidT_made, 1)
                with act.If(b + 1 < n):
                    silu_of(1 - par, b + 2)
                with act.If(b + 2 < n):
                    read_hT(act, nc.scalar.copy, 1, b + 3, par, hT_act)
                act.wait_ge(dn_ps, b + 2)
                act.wait_ge(added, 16 * b + 16)
                nc.scalar.activation(y[:, 0:512], psum[:, 5, :], ACT.Copy,
                                     scale=r["slot_gate"][:, bass.ds(b, 1)]).then_inc(y_act, 1)

            blocks(act, body)

        @block.vector
        def _(dve):
            def hidden(par, done):
                dve.wait_ge(silu, done)
                nc.vector.tensor_tensor(hid[:], sa[:, par], psum[:, 2 + par, FE:2 * FE], ALU.mult
                                        ).then_inc(hid_made, 1)

            nc.vector.memset(y[:, 512:D], 0.0).then_inc(y_dve, 1)
            read_hT(dve, nc.vector.tensor_copy, 0, 1, 0, hT_dve)
            read_hT(dve, nc.vector.tensor_copy, 0, 2, 1, hT_dve)
            hidden(0, 1)

            def body(b, j, turn, n):
                par = j % 2
                with dve.If(b + 2 < n):
                    read_hT(dve, nc.vector.tensor_copy, 0, b + 3, par, hT_dve)
                with dve.If(b + 1 < n):
                    dve.wait_ge(hidT_ps, b + 2)
                    hidden(1 - par, b + 2)
                dve.wait_ge(dn_ps, b + 2)
                dve.wait_ge(added, 16 * b + 16)
                nc.vector.tensor_scalar(y[:, 512:D], psum[:, 6, :], r["slot_gate"][:, bass.ds(b, 1)], None,
                                        ALU.mult).then_inc(y_dve, 1)

            blocks(dve, body)

        @block.tensor
        def _(pe):
            def turn_rows(j):
                return [pe.transpose(psum[:, k // 4, k % 4 * P:(k % 4 + 1) * P], hg[:, j, k:D:KD], cst["ident"][:])
                        for k in range(KD)]

            def up(b, par):
                e = pe.value_load(tab[0:1, bass.ds(T_EXP + b, 1)], min_val=0, max_val=EXPERTS - 1)
                s = pe.value_load(tab[0:1, bass.ds(T_BUF + b, 1)], min_val=0, max_val=WBUF - 1)
                pe.wait_ge(ready, e + 1)
                pe.wait_ge(hT_dve, b + 1)
                pe.wait_ge(hT_act, b + 1)
                for k in range(KD):
                    mm = pe.matmul(psum[:, 2 + par, :], hT[:, par, k],
                                   wx[:, bass.ds(s, 1), k * 2 * FE:(k + 1) * 2 * FE].rearrange("p o f -> p (o f)"),
                                   start=(k == 0), stop=(k == KD - 1))
                mm.then_inc(up_ps, 1)

            pe.wait_ge(hg_land[0], 16)
            first = turn_rows(0)
            first[0].then_inc(hidT_ps, 1)
            first[1].then_inc(dn_ps, 1)
            first[-1].then_inc(hT_ps, 2)
            pe.wait_ge(hg_land[1], 16)
            pe.wait_ge(hT_dve, 1)
            pe.wait_ge(hT_act, 1)
            turn_rows(1)[-1].then_inc(hT_ps, 1)
            up(0, 0)

            def body(b, j, turn, n):
                par = j % 2
                with pe.If(b + 1 < n):
                    up(b + 1, 1 - par)
                pe.wait_ge(hid_made, b + 1)
                for k in range(2):
                    mm = pe.transpose(psum[:, 4, k * P:(k + 1) * P], hid[:, k:FE:2], cst["ident"][:])
                mm.then_inc(hidT_ps, 1)
                with pe.If(b + 2 < n):
                    after = (j + 2) % UNROLL
                    pe.wait_ge(hg_land[after], 16 * turn + (32 if after < 2 else 16))
                    turn_rows(after)[-1].then_inc(hT_ps, 1)
                pe.wait_ge(hidT_made, b + 1)
                pe.wait_ge(y_dve, b + 1)
                pe.wait_ge(y_act, b + 1)
                s = pe.value_load(tab[0:1, bass.ds(T_BUF + b, 1)], min_val=0, max_val=WBUF - 1)
                for c in range(2):
                    for k in range(2):
                        at = KD * 2 * FE + k * D + c * 512
                        mm = pe.matmul(psum[:, 5 + c, :], hidT[:, k],
                                       wx[:, bass.ds(s, 1), at:at + 512].rearrange("p o f -> p (o f)"),
                                       start=(k == 0), stop=(k == 1))
                mm.then_inc(dn_ps, 1)

            blocks(pe, body)


def final_phase(nc, cst, a, o, scr):
    NTL = TILES + 1
    XR = 3
    with ExitStack() as ctx:
        def sb(name, shape, dt=F32):
            return ctx.enter_context(nc.sbuf_tensor(name, shape, dt))

        def sem(name):
            return new_sem(nc, name)

        g2 = sb("g2", [P, 2, D])
        lg, lb = sb("lg2", [P, D]), sb("lb2", [P, D])
        x1, f, sq = sb("x1f", [P, XR, D]), sb("f", [P, XR, D]), sb("sq3", [P, D])
        st = sb("st2", [P, NTL, 4])
        mod_land = sem("f_mod")
        x_land = [sem(f"f_in{i}") for i in range(XR)]
        out_done = [sem(f"f_out{i}") for i in range(XR)]
        x_made, sq_made, var_made, root, gain, done = (sem(n) for n in ("f_x", "f_sq", "f_var", "f_root", "f_gain",
                                                                        "f_done"))
        xs = sem("f_xs")
        chain = Chain(sem("f_chain"))
        block = ctx.enter_context(nc.Block())

        @block.sync
        def _(sp):
            for s in range(2):
                load_rows(sp, g2[0:P if s == 0 else NS, s], scr["mod"], G2, s, mod_land)
            sp.dma_start(lg[:], a["ln2_g"][0].partition_broadcast(P)).then_inc(mod_land, 16)
            sp.dma_start(lb[:], a["ln2_b"][0].partition_broadcast(P)).then_inc(mod_land, 16)
            for i in range(NTL):
                n = tile_rows(i)
                if i >= XR:
                    sp.wait_ge(out_done[i % XR], 16 * (i // XR))
                sp.dma_start(x1[0:n, i % XR], scr["x1"][i * P:i * P + n]).then_inc(x_land[i % XR], 16)
                sp.dma_start(f[0:n, i % XR], scr["acc"][i * P:i * P + n]).then_inc(x_land[i % XR], 16)

        @block.gpsimd
        def _(pool):
            for i in range(NTL):
                n = tile_rows(i)
                pool.wait_ge(gain, i + 1)
                nc.gpsimd.tensor_tensor(x1[0:n, i % XR], x1[0:n, i % XR], lb[0:n], ALU.add).then_inc(done, 1)
                pool.wait_ge(done, i + 1)
                dst = o["y_prompt"][0].rearrange("(c s) d -> s c d", s=LC)[i] if i < TILES else \
                    o["y_sample"].rearrange("b t d -> (b t) d")
                pool.dma_start(dst, x1[0:n, i % XR]).then_inc(out_done[i % XR], 16)
            for i in range(XR):
                pool.wait_ge(out_done[i], 16 * 3)

        @block.scalar
        def _(act):
            for i in range(NTL):
                n = tile_rows(i)
                act.wait_ge(x_made, i + 1)
                if i:
                    act.wait_ge(sq_made, 2 * i)
                nc.scalar.activation(st[0:n, i, 1:2], st[0:n, i, 0:1], ACT.Copy, scale=-1.0 / D
                                     ).then_inc(sq_made, 1)
                act.wait_ge(sq_made, 2 * i + 1)
                nc.scalar.activation(sq[0:n], x1[0:n, i % XR], ACT.Square, bias=st[0:n, i, 1:2],
                                     accum_out=st[0:n, i, 2:3]).then_inc(sq_made, 1)
                act.wait_ge(var_made, i + 1)
                nc.scalar.activation(st[0:n, i, 3:4], st[0:n, i, 2:3], ACT.Sqrt).then_inc(root, 1)

        @block.vector
        def _(dve):
            def seq(ins):
                dve.wait_ge(chain.sem, chain.did(ins))

            def front(i):
                n, s = tile_rows(i), i // TILES
                dve.wait_ge(x_land[i % XR], 32 * (i // XR + 1))
                seq(nc.vector.tensor_tensor(f[0:n, i % XR], f[0:n, i % XR], g2[0:n, s], ALU.mult))
                nc.vector.scalar_tensor_tensor(x1[0:n, i % XR], x1[0:n, i % XR], ALPHA, f[0:n, i % XR], ALU.mult,
                                               ALU.add, accum_out=st[0:n, i, 0:1]).then_inc(x_made, 1)

            dve.wait_ge(mod_land, 16 * (1 + NB + 2))
            front(0)
            for i in range(NTL):
                n = tile_rows(i)
                if i + 1 < NTL:
                    front(i + 1)
                dve.wait_ge(sq_made, 2 * i + 2)
                nc.vector.tensor_scalar(st[0:n, i, 2:3], st[0:n, i, 2:3], 1.0 / D, EPS, ALU.mult, ALU.add
                                        ).then_inc(var_made, 1)
                dve.wait_ge(root, i + 1)
                seq(nc.vector.reciprocal(st[0:n, i, 3:4], st[0:n, i, 3:4]))
                seq(nc.vector.tensor_scalar(x1[0:n, i % XR], x1[0:n, i % XR], st[0:n, i, 1:2], st[0:n, i, 3:4],
                                            ALU.add, ALU.mult))
                nc.vector.tensor_tensor(x1[0:n, i % XR], x1[0:n, i % XR], lg[0:n], ALU.mult).then_inc(gain, 1)


def hymba_step(nc, a, o, upto=99):
    scr = {}
    HELD.clear()

    def dram(name, shape, dt=F32):
        scr[name] = nc.dram_tensor("scr_" + name, shape, dt).ap()

    dram("mod", (1 + NB, 6 * D))
    dram("ys", (NS, D_SSM))
    dram("os", (NS, D_SSM))
    dram("x1", (ROWS, D))
    dram("slots", (SLOTS, 2))
    dram("tab", (1, T_LEN), I32)
    dram("h2", (TRASH + P, D))
    dram("acc", (TRASH + P, D))
    with ExitStack() as ctx:
        def sb(name, shape, dt=F32):
            return ctx.enter_context(nc.sbuf_tensor(name, shape, dt))

        psum = ctx.enter_context(nc.psum_tensor("psum", [P, 8, 512], F32))
        cst = {"ident": sb("ident", [P, P]), "ones": sb("ones", [P, P]), "before": sb("before", [P, P])}
        modT = sb("modT", [P, 2, KD, 1 + NB])
        make_constants(nc, cst)
        ada_phase(nc, cst, psum, a, scr, modT)
        with ExitStack() as mixers:
            def sbm(name, shape, dt=F32):
                return mixers.enter_context(nc.sbuf_tensor(name, shape, dt))

            att = sbm("att", [P, TILES + 1, D_SSM])
            t = {"u": sbm("u", [P, GROUPS, LC, GCH]), "us": sbm("us", [NS, D_SSM]),
                 "spare": att[:].rearrange("p t c -> p (t c)")}
            with ExitStack() as projected:
                def sbp(name, shape, dt=F32):
                    return projected.enter_context(nc.sbuf_tensor(name, shape, dt))

                t |= {"qT": sbp("qT", [P, 4, TOK]), "kT": sbp("kT", [P, 2, TOK]), "qiT": sbp("qiT", [P, 2, TOK]),
                      "kiT": sbp("kiT", [P, 1, TOK]), "v": sbp("v", [P, TILES + 1, KVH * HD]),
                      "kiwi": sbp("kiwi", [P, TILES + 1, IDX + IH])}
                project_phase(nc, cst, psum, a, o, modT, t)
                with ExitStack() as ssm:
                    def sbs(name, shape, dt=F32):
                        return ssm.enter_context(nc.sbuf_tensor(name, shape, dt))

                    s = {"toep": sbs("toep", [P, GROUPS, LC, GCH]), "wT": sbs("ssm_wT", [P, 2, PAIRS, P]),
                         "ca": sbs("ssm_ca", [P, 2, PAIRS, LC, GCH]), "rot": sbs("rot", [P, 2, PAIRS, CH]),
                         "r8": sbs("r8", [P, PAIRS]), "a8": sbs("a8", [P, 2, PAIRS]), "spare": t["spare"]}
                    ssm_tables_phase(nc, cst, psum, a, s)
                    s["uc"] = t["spare"][:, 0:GROUPS * CHS].rearrange("p (g c) -> p g c", g=GROUPS)
                    ssm_input_phase(nc, cst, psum, t, s)
                    ssm_scan_phase(nc, cst, psum, a, o, scr, t, s)
                clear_sems(nc)
                x = {"gidx": sbp("gidx", [P, NB], I32),
                     "pbias": sbp("pbias", [P, score_off(TILES)], BF16), "sbias": sbp("sbias", [NS, KEYS], BF16)}
                with ExitStack() as scores:
                    x["psc"] = scores.enter_context(nc.sbuf_tensor("psc", [P, score_off(TILES)], F32))
                    x["ssc"] = scores.enter_context(nc.sbuf_tensor("ssc", [NS, KEYS], F32))
                    index_phase(nc, cst, psum, a, t, x)
                    topk_phase(nc, cst, x)
                prompt_attention_phase(nc, cst, psum, t, x, att)
                sample_attention_phase(nc, cst, psum, a, scr, t, x)
            clear_sems(nc)
            mixT = ctx.enter_context(nc.sbuf_tensor("mixT", [P, KD, TOK], F32, side="right"))
            mix_phase(nc, cst, psum, a, scr, t, att, mixT)
        aff = sb("aff", [P, TILES + 1, EXPERTS])
        out_phase(nc, cst, psum, a, scr, mixT, aff)
        clear_sems(nc)
        r = {"tab": sb("tab", [1, T_LEN], I32), "slot_tok": sb("slot_tok", [P, P], I32),
             "slot_gate": sb("slot_gate", [P, P]), "wx": sb("wx", [P, WBUF, WLEN]),
             "wx_land": [new_sem(nc, f"wx_land{i}") for i in range(WBUF)]}
        route_phase(nc, cst, psum, a, scr, mixT, aff, r)
        expert_phase(nc, cst, psum, a, scr, r)
        final_phase(nc, cst, a, o, scr)
    return scr


_INS = ["x_prompt", "x_sample", "c_prompt", "c_sample", "cache_k", "cache_v", "cache_kidx", "state_ssm_re",
        "state_ssm_im", "page_table", "w_ada", "b_ada", "w_in", "ssm_a_re", "ssm_a_im", "ssm_log_dt",
        "ssm_b_re", "ssm_b_im", "ssm_c_re", "ssm_c_im", "ssm_d", "w_glu", "b_glu", "g_ssm_out", "g_att_out",
        "w_out", "ln1_g", "ln1_b", "w_router", "b_router", "w_e1", "w_e3", "w_e2", "w_s1", "w_s3", "w_s2",
        "ln2_g", "ln2_b"]
_OUTS = [("y_prompt", (1, SEQ, D)), ("y_sample", (NB, NT, D)),
         ("k_prompt", (1, 1, SEQ, KVH, HD)), ("v_prompt", (1, 1, SEQ, KVH, HD)), ("ki_prompt", (1, 1, SEQ, IDX)),
         ("re_prompt", (1, 1, GROUPS, STATES)), ("im_prompt", (1, 1, GROUPS, STATES)),
         ("k_sample", (1, NB, NT, KVH, HD)), ("v_sample", (1, NB, NT, KVH, HD)), ("ki_sample", (1, NB, NT, IDX)),
         ("re_sample", (1, NB, GROUPS, STATES)), ("im_sample", (1, NB, GROUPS, STATES))]


def kernel(**inputs):
    import concourse.bacc as bacc
    from concourse.bass_utils import run_bass_kernel_spmd

    nc = bacc.Bacc("TRN2", target_bir_lowering=False, num_devices=1)
    arrays, a, o = {}, {}, {}
    for name in _INS:
        x = np.ascontiguousarray(inputs[name])
        arrays[f"in_{name}"] = x
        a[name] = nc.dram_tensor(f"in_{name}", x.shape, mybir.dt.from_np(x.dtype), kind="ExternalInput").ap()
    for name, shape in _OUTS:
        o[name] = nc.dram_tensor(f"out_{name}", shape, F32, kind="ExternalOutput").ap()
    hymba_step(nc, a, o)
    r = run_bass_kernel_spmd(nc, [arrays], core_ids=[0])
    return tuple(r.results[0][f"out_{name}"] for name, _ in _OUTS)
```

```python
from contextlib import ExitStack

import numpy as np
import concourse.bass as bass
from concourse import mybir
from concourse.alu_op_type import AluOpType as ALU

ACT = mybir.ActivationFunctionType
F32 = mybir.dt.float32
BF16 = mybir.dt.bfloat16
I32 = mybir.dt.int32
U16 = mybir.dt.uint16
AX = mybir.AxisListType.X

P = 128
D = 1024
KD = D // P
SEQ = 1024
NB, NT = 8, 8
NS = NB * NT
TOK = SEQ + NS
TILES = SEQ // P
D_SSM = 512
GROUPS, GCH, STATES = 32, 16, 64
PAIRS = GROUPS // 2
LC = 8
CH = SEQ // LC
CHS = CH + NB
HEADS, KVH, HD = 8, 4, 64
IH, IDX = 4, 64
TOPK = 256
PAST, PAGE = 2048, 128
PAGES = PAST // PAGE
KEYS = PAST + NT
EXPERTS, TOPE, FE = 64, 6, 256
ROUTED_SCALE = 2.5
ALPHA = 2 ** 0.25
EPS = 1e-5
C_U, C_Q, C_K, C_V, C_QI, C_KI, C_WI, C_END = 0, 512, 1024, 1280, 1536, 1792, 1856, 1860
SH1, SC1, G1, SH2, SC2, G2 = (i * D for i in range(6))
BLK = 128
NBLK = TOK * TOPE // BLK + EXPERTS
SLOTS = NBLK * BLK
ROWS = (TILES + 1) * P
TRASH = ROWS
NEG = -1e30


HELD = []


def new_sem(nc, name):
    HELD.append(nc.alloc_semaphore(name))
    return HELD[-1]


def clear_sems(nc):
    nc.clear_and_free_semaphores(list(HELD))
    nc.all_engine_barrier()
    HELD.clear()


class Chain:

    def __init__(self, sem):
        self.sem, self.n = sem, 0

    def did(self, ins):
        self.n += 1
        ins.then_inc(self.sem, 1)
        return self.n


def make_constants(nc, cst):
    with ExitStack() as ctx:
        made = new_sem(nc, "constants_made")
        block = ctx.enter_context(nc.Block())

        @block.gpsimd
        def _(pool):
            nc.gpsimd.memset(cst["ident"][:], 0.0).then_inc(made, 1)
            nc.gpsimd.memset(cst["ones"][:], 1.0).then_inc(made, 1)
            nc.gpsimd.memset(cst["before"][:], 1.0).then_inc(made, 1)
            pool.wait_ge(made, 3)
            nc.gpsimd.affine_select(out=cst["ident"][:], in_=cst["ident"][:], pattern=[[-1, P]],
                                    compare_op=ALU.not_equal, fill=1.0, base=0,
                                    channel_multiplier=1).then_inc(made, 1)
            nc.gpsimd.affine_select(out=cst["before"][:], in_=cst["before"][:], pattern=[[1, P]],
                                    compare_op=ALU.is_gt, fill=0.0, base=0,
                                    channel_multiplier=-1).then_inc(made, 1)
            pool.wait_ge(made, 5)


def ada_phase(nc, cst, psum, a, scr, modT, cf, w_next, w_land):
    NR = 1 + NB
    NCOL = 6 * D // 512
    RING = 3
    with ExitStack() as ctx:
        def sb(name, shape, dt=F32):
            return ctx.enter_context(nc.sbuf_tensor(name, shape, dt))

        def sem(name):
            return new_sem(nc, name)

        c_rows = sb("c_rows", [NR, D])
        c_sig = sb("c_sig", [NR, D])
        cT = sb("cT", [P, KD, NR])
        wa = sb("wa", [P, RING, KD, 512])
        bada = sb("bada", [NR, 6 * D])
        mod = sb("mod", [NR, 6 * D])
        c_in, silu_done, cT_ps, cT_sb = sem("c_in"), sem("silu_done"), sem("cT_ps"), sem("cT_sb")
        w_in = [sem(f"wa_in{i}") for i in range(RING)]
        b_in, mod_ps, mod_sb = sem("b_in"), sem("mod_ps"), sem("mod_sb")
        mT_ps, mT_sb, mod_out = sem("mT_ps"), sem("mT_sb"), sem("mod_out")
        mod_raw = sem("mod_raw")
        z = ssm_row_buffers(nc, ctx)
        chain = Chain(sem("rows_chain"))
        block = ctx.enter_context(nc.Block())

        @block.sync
        def _(sp):
            sp.dma_start(c_rows[0:1], a["c_prompt"]).then_inc(c_in, 16)
            sp.dma_start(c_rows[1:NR], a["c_sample"]).then_inc(c_in, 16)
            sp.dma_start(z["ar"][:], a["ssm_a_re"][0].rearrange("(m g) p -> m (g p)", g=2)).then_inc(z["landed"], 16)
            sp.dma_start(z["ai"][:], a["ssm_a_im"][0].rearrange("(m g) p -> m (g p)", g=2)).then_inc(z["landed"], 16)
            sp.dma_start(z["ldt"][:], a["ssm_log_dt"][0].rearrange("(m g) -> m g", g=2)).then_inc(z["landed"], 16)
            for n in range(NCOL):
                if n >= RING:
                    sp.wait_ge(mod_ps, n - RING + 1)
                sp.dma_start(wa[:, n % RING],
                             a["w_ada"][0].rearrange("(p k) n -> p k n", k=KD)[:, :, n * 512:(n + 1) * 512]
                             ).then_inc(w_in[n % RING], 16)
                if n == 0:
                    sp.dma_start(bada[:], a["b_ada"][0].partition_broadcast(NR)).then_inc(b_in, 16)
            sp.dma_start(w_next[:], a["w_in"][0].rearrange("(p k) n -> p k n", k=KD)).then_inc(w_land, 16)
            sp.wait_ge(mod_sb, NCOL)
            sp.dma_start(scr["mod"], mod[:]).then_inc(mod_out, 16)
            sp.wait_ge(mod_out, 16)

        @block.scalar
        def _(act):
            act.wait_ge(c_in, 32)
            nc.scalar.activation(c_sig[:], c_rows[:], ACT.Sigmoid).then_inc(silu_done, 1)
            act.wait_ge(z["sin_in"], 1)
            nc.scalar.activation(z["w3"][:], z["w1"][:], ACT.Sin)
            nc.scalar.activation(z["w4"][:], z["w2"][:], ACT.Sin).then_inc(z["sin_out"], 1)
            for n in range(NCOL):
                act.wait_ge(mod_ps, n + 1)
                nc.scalar.copy(mod[:, n * 512:(n + 1) * 512], psum[0:NR, 1 + n % 4, :]).then_inc(mod_raw, 1)

        @block.gpsimd
        def _(pool):
            pool.wait_ge(b_in, 16)
            for n in range(NCOL):
                pool.wait_ge(mod_raw, n + 1)
                cols = slice(n * 512, (n + 1) * 512)
                nc.gpsimd.tensor_tensor(mod[:, cols], mod[:, cols], bada[:, cols], ALU.add).then_inc(mod_sb, 1)

        @block.vector
        def _(dve):
            dve.wait_ge(silu_done, 1)
            nc.vector.tensor_tensor(c_sig[:], c_sig[:], c_rows[:], ALU.mult).then_inc(silu_done, 1)
            dve.wait_ge(cT_ps, 1)
            nc.vector.tensor_copy(cT[:], psum[:, 0, 0:KD * NR].rearrange("p (k r) -> p k r", k=KD)
                                  ).then_inc(cT_sb, 1)
            ssm_rows(nc, dve, chain, z)
            dve.wait_ge(z["ps"], 1)
            nc.vector.tensor_copy(cf[:].rearrange("p q m -> p (q m)"), psum[:, 7, 0:NQ * PAIRS]).then_inc(z["read"], 1)
            dve.wait_ge(mT_ps, 1)
            nc.vector.tensor_copy(modT[:, 0], psum[:, 5, 0:KD * NR].rearrange("p (k r) -> p k r", k=KD))
            nc.vector.tensor_scalar(modT[:, 1], psum[:, 6, 0:KD * NR].rearrange("p (k r) -> p k r", k=KD),
                                    1.0, None, ALU.add).then_inc(mT_sb, 1)

        @block.tensor
        def _(pe):
            pe.wait_ge(silu_done, 2)
            for k in range(KD):
                mm = pe.transpose(psum[:, 0, k * NR:(k + 1) * NR], c_sig[:, k:D:KD],
                                  cst["ident"][0:NR, 0:NR])
            mm.then_inc(cT_ps, 1)
            pe.wait_ge(cT_sb, 1)
            for n in range(NCOL):
                pe.wait_ge(w_in[n % RING], 16 * (n // RING + 1))
                if n >= 4:
                    pe.wait_ge(mod_raw, n - 3)
                for k in range(KD):
                    mm = pe.matmul(psum[0:NR, 1 + n % 4, :], cT[:, k], wa[:, n % RING, k],
                                   start=(k == 0), stop=(k == KD - 1))
                mm.then_inc(mod_ps, 1)
            pe.wait_ge(z["made"], 1)
            for q in range(NQ):
                mm = pe.transpose(psum[:, 7, q * PAIRS:(q + 1) * PAIRS], z["rows"][:, q],
                                  cst["ident"][0:PAIRS, 0:PAIRS])
            mm.then_inc(z["ps"], 1)
            pe.wait_ge(mod_sb, NCOL)
            for part, bank in ((SH1, 5), (SC1, 6)):
                for k in range(KD):
                    mm = pe.transpose(psum[:, bank, k * NR:(k + 1) * NR],
                                      mod[:, part + k:part + D:KD], cst["ident"][0:NR, 0:NR])
            mm.then_inc(mT_ps, 1)


def project_phase(nc, cst, psum, a, o, modT, act_t, w, w_land):
    XR = 2
    with ExitStack() as ctx:
        def sb(name, shape, dt=F32):
            return ctx.enter_context(nc.sbuf_tensor(name, shape, dt))

        def sem(name):
            return new_sem(nc, name)

        wq = sb("wq", [P, KD, 4, P])
        wkk = act_t["spare"][:, 0:KD * P].rearrange("p (k c) -> p k c", k=KD)
        krow = act_t["spare"][:, KD * P:KD * P + (TILES + 1) * KVH * HD].rearrange(
            "p (t c) -> p t c", t=TILES + 1)
        xt = sb("xt", [P, XR, D])
        hT = sb("hT", [P, KD, TOK])
        x_land = [sem(f"x_land{i}") for i in range(XR)]
        wq_made = sem("wq_made")
        ps_full = sem("ps_full")
        dve_read, act_read = sem("dve_read"), sem("act_read")
        rows_out = act_t["rows_out"]
        hs_mid = sem("hs_mid")

        groups = []
        for t in range(TILES):
            groups += [("x", t, 0), ("x", t, 1)]
        groups += [("xs", 0, 0)]
        for s in range(LC):
            groups += [("u", s, 0)]
        groups += [("us", 0, 0)]
        cuts = [(0, 384), (384, 736), (736, TOK)]
        for name, n in (("q", 4), ("k", 2), ("qi", 2), ("ki", 1)):
            for b in range(n):
                for c in cuts:
                    groups.append((name, b, c))
        for t in range(TILES + 1):
            groups += [("v", t, 0), ("kiwi", t, 0), ("krow", t, 0)]
        last_even = max(g for g in range(len(groups)) if g % 2 == 0)
        X_GROUPS = 2 * TILES + 1

        def tokens(t):
            return (t * P, P) if t < TILES else (SEQ, NS)

        block = ctx.enter_context(nc.Block())

        @block.sync
        def _(sp):
            for t in range(TILES + 1):
                if t >= XR:
                    sp.wait_ge(ps_full, 2 * (t - XR) + 2)
                if t < TILES:
                    sp.dma_start(xt[:, t % XR], a["x_prompt"][0].rearrange("(c s) d -> s c d", s=LC)[t]
                                 ).then_inc(x_land[t % XR], 16)
                else:
                    sp.dma_start(xt[0:NS, t % XR], a["x_sample"].rearrange("b t d -> (b t) d")
                                 ).then_inc(x_land[t % XR], 16)
            sp.wait_ge(dve_read, last_even // 2 + 1)
            sp.wait_ge(act_read, len(groups) // 2)
            v, kiwi = act_t["v"], act_t["kiwi"]
            outs = [(o["k_prompt"], krow, 256), (o["v_prompt"], v, 256), (o["ki_prompt"], kiwi, IDX)]
            for dst, src, n in outs:
                flat = dst.rearrange("l b s h d -> (l b s) (h d)") if n == 256 else \
                    dst.rearrange("l b s d -> (l b s) d")
                sp.dma_start(flat.rearrange("(t p) n -> p t n", p=P), src[:, 0:TILES, 0:n]
                             ).then_inc(rows_out, 16)
            outs = [(o["k_sample"], krow, 256), (o["v_sample"], v, 256), (o["ki_sample"], kiwi, IDX)]
            for dst, src, n in outs:
                flat = dst.rearrange("l b s h d -> (l b s) (h d)") if n == 256 else \
                    dst.rearrange("l b s d -> (l b s) d")
                sp.dma_start(flat, src[0:NS, TILES, 0:n]).then_inc(rows_out, 16)

        def evacuate(eng, g):
            kind, i, c = groups[g]
            bank = psum[:, g % 8]
            done = dve_read if g % 2 == 0 else act_read
            copy = nc.vector.tensor_copy if g % 2 == 0 else nc.scalar.copy
            if kind == "x":
                for j in range(4):
                    k = 4 * c + j
                    out, src = hT[:, k, i:SEQ:LC], bank[:, j * P:(j + 1) * P]
                    if g % 2 == 0:
                        ins = nc.vector.tensor_scalar(out, src, modT[:, 1, k, 0:1], modT[:, 0, k, 0:1],
                                                      ALU.mult, ALU.add)
                    else:
                        ins = nc.scalar.activation(out, src, ACT.Identity, bias=modT[:, 0, k, 0:1],
                                                   scale=modT[:, 1, k, 0:1])
                return ins.then_inc(done, 1)
            if kind == "xs":
                out = hT[:, :, SEQ:TOK].rearrange("p k (b t) -> p k b t", b=NB)
                src = bank.rearrange("p (k b t) -> p k b t", k=KD, b=NB)
                shape = [P, KD, NB, NT]
                nc.vector.tensor_tensor(out, src, modT[:, 1, :, 1:].unsqueeze(3).broadcast_to(shape),
                                        ALU.mult).then_inc(hs_mid, 1)
                eng.wait_ge(hs_mid, 1)
                return nc.vector.tensor_tensor(out, out, modT[:, 0, :, 1:].unsqueeze(3).broadcast_to(shape),
                                               ALU.add).then_inc(done, 1)
            if kind == "u":
                out = act_t["u"][:, :, i, :]
                return copy(out, bank.rearrange("p (g j) -> p g j", g=GROUPS)).then_inc(done, 1)
            if kind == "us":
                return copy(act_t["us"][0:NS, :], bank[0:NS, :]).then_inc(done, 1)
            if kind in ("q", "k", "qi", "ki"):
                dst = act_t[kind + "T"]
                out = dst[:, i, c[0]:c[1]]
                return copy(out, bank[:, 0:c[1] - c[0]]).then_inc(done, 1)
            n = tokens(i)[1]
            dst, width = {"v": (act_t["v"], 256), "kiwi": (act_t["kiwi"], IDX + IH),
                          "krow": (krow, 256)}[kind]
            return copy(dst[0:n, i, :], bank[0:n, 0:width]).then_inc(done, 1)

        @block.vector
        def _(dve):
            for g in range(0, len(groups), 2):
                dve.wait_ge(ps_full, g + 1)
                evacuate(dve, g)
                if g == 2 * TILES + 2:
                    dve.wait_ge(w_land, 16)
                    nc.vector.tensor_copy(
                        wq[:].rearrange("p k (m a) (n d) -> p k m a n d", m=2, n=2)[:, :, 0],
                        w[:, :, C_Q:C_Q + 256].rearrange("p k (n a d) -> p k a n d", n=2, a=2))
                    nc.vector.tensor_copy(
                        wq[:].rearrange("p k (m a) (n d) -> p k m a n d", m=2, n=2)[:, :, 1],
                        w[:, :, C_Q + 256:C_K].rearrange("p k (n a d) -> p k a n d", n=2, a=2))
                    for half in range(2):
                        ins = nc.vector.tensor_copy(wkk[:, :, half * IDX:(half + 1) * IDX],
                                                    w[:, :, C_KI:C_WI])
                    ins.then_inc(wq_made, 1)

        @block.scalar
        def _(act):
            for g in range(1, len(groups), 2):
                act.wait_ge(ps_full, g + 1)
                evacuate(act, g)

        @block.tensor
        def _(pe):
            for g, (kind, i, c) in enumerate(groups):
                bank = psum[:, g % 8]
                if g >= 8:
                    if g % 2 == 0:
                        pe.wait_ge(dve_read, (g - 8) // 2 + 1)
                    else:
                        pe.wait_ge(act_read, (g - 8) // 2 + 1)
                if kind in ("x", "xs"):
                    t = i if kind == "x" else TILES
                    pe.wait_ge(x_land[t % XR], 16 * (t // XR + 1))
                    if kind == "x":
                        for j in range(4):
                            mm = pe.transpose(bank[:, j * P:(j + 1) * P], xt[:, t % XR, 4 * c + j:D:KD],
                                              cst["ident"][:])
                        mm.then_inc(ps_full, 1)
                    else:
                        for k in range(KD):
                            mm = pe.transpose(bank[:, k * NS:(k + 1) * NS], xt[0:NS, t % XR, k:D:KD],
                                              cst["ident"][0:NS, 0:NS])
                        mm.then_inc(ps_full, 1)
                    continue
                if g == X_GROUPS:
                    pe.wait_ge(dve_read, X_GROUPS // 2 + 1)
                    pe.wait_ge(act_read, X_GROUPS // 2)
                    pe.wait_ge(w_land, 16)
                if kind == "q" and i == 0 and c[0] == 0:
                    pe.wait_ge(wq_made, 1)
                if kind == "krow":
                    first, n = tokens(i)
                    if i == 0:
                        kg = max(j for j, x in enumerate(groups) if x[0] == "k")
                        pe.wait_ge(dve_read, kg // 2 + 1)
                        pe.wait_ge(act_read, (kg + 1) // 2)
                    for b in range(2):
                        mm = pe.transpose(bank[0:n, b * P:(b + 1) * P], act_t["kT"][:, b, first:first + n],
                                          cst["ident"][:])
                    mm.then_inc(ps_full, 1)
                    continue
                for k in range(KD):
                    flags = dict(start=(k == 0), stop=(k == KD - 1))
                    if kind == "u":
                        mm = pe.matmul(bank, hT[:, k, i:SEQ:LC], w[:, k, C_U:C_Q], **flags)
                    elif kind == "us":
                        mm = pe.matmul(bank[0:NS], hT[:, k, SEQ:TOK], w[:, k, C_U:C_Q], **flags)
                    elif kind in ("q", "k", "qi", "ki"):
                        lhs = {"q": lambda: wq[:, k, i, :], "k": lambda: w[:, k, C_K + i * P:C_K + (i + 1) * P],
                               "qi": lambda: w[:, k, C_QI + i * P:C_QI + (i + 1) * P],
                               "ki": lambda: wkk[:, k, :]}[kind]()
                        mm = pe.matmul(bank[:, 0:c[1] - c[0]], lhs, hT[:, k, c[0]:c[1]], **flags)
                    else:
                        first, n = tokens(i)
                        cols = (C_V, C_QI) if kind == "v" else (C_KI, C_END)
                        mm = pe.matmul(bank[0:n, 0:cols[1] - cols[0]], hT[:, k, first:first + n],
                                       w[:, k, cols[0]:cols[1]], **flags)
                mm.then_inc(ps_full, 1)


NQ = 2 * (LC + 1) + 5
ROW_AT = 0, LC + 1, 2 * LC + 2, 2 * LC + 3, 2 * LC + 4, 2 * LC + 5, 2 * LC + 6


def ssm_row_buffers(nc, ctx):
    def sb(name, shape, dt=F32):
        return ctx.enter_context(nc.sbuf_tensor(name, shape, dt))

    M = PAIRS
    z = {"ldt": sb("ldt", [M, 2]), "dt": sb("dt", [M, 2]), "rows": sb("rows", [M, NQ, P]),
         "ei": sb("ei", [M, P], I32)}
    z |= {n: sb(n, [M, P]) for n in ("ar", "ai", "mag", "ang", "w1", "w2", "w3", "w4", "e1", "e2", "e3")}
    z |= {n: new_sem(nc, "rows_" + n) for n in ("landed", "sin_in", "sin_out", "made", "ps", "read")}
    return z


def ssm_rows(nc, dve, chain, z):
    M = PAIRS
    PR, PI, FR, FI, R8, C8, S8 = ROW_AT
    ar, ai, ldt, dt, mag, ang, rows, ei, w1, w2, w3, w4, e1, e2, e3 = (z[n] for n in (
        "ar", "ai", "ldt", "dt", "mag", "ang", "rows", "ei", "w1", "w2", "w3", "w4", "e1", "e2", "e3"))

    def seq(ins):
        dve.wait_ge(chain.sem, chain.did(ins))

    def tt(out, x, y, op):
        seq(nc.vector.tensor_tensor(out, x, y, op))

    def ts(out, x, s1, s2, op0, op1=ALU.bypass):
        if s2 is None:
            seq(nc.vector.tensor_scalar(out, x, s1, None, op0))
        else:
            seq(nc.vector.tensor_scalar(out, x, s1, s2, op0, op1))

    def exp(out, x, n):
        magic, ln_hi = 12582912.0, 0.693145751953125
        ln_lo = float(np.log(2.0) - ln_hi)
        r, kk, acc, ki = e1[:, 0:n], e2[:, 0:n], e3[:, 0:n], ei[:, 0:n]
        ts(kk, x, float(1 / np.log(2.0)), magic, ALU.mult, ALU.add)
        ts(kk, kk, magic, -126.0, ALU.subtract, ALU.max)
        seq(nc.vector.scalar_tensor_tensor(r, kk, -ln_hi, x, ALU.mult, ALU.add))
        seq(nc.vector.scalar_tensor_tensor(r, kk, -ln_lo, r, ALU.mult, ALU.add))
        ts(acc, r, 1 / 40320.0, 1 / 5040.0, ALU.mult, ALU.add)
        for c in (720.0, 120.0, 24.0, 6.0, 2.0, 1.0, 1.0):
            tt(acc, acc, r, ALU.mult)
            ts(acc, acc, 1 / c, None, ALU.add)
        ts(ki, kk, 127.0, 8388608.0, ALU.add, ALU.mult)
        tt(out, acc, ki.bitcast(F32), ALU.mult)

    def cmul(orr, oi, xr, xi, yr, yi, t1):
        tt(orr, xr, yr, ALU.mult)
        tt(t1, xi, yi, ALU.mult)
        tt(orr, orr, t1, ALU.subtract)
        tt(oi, xr, yi, ALU.mult)
        tt(t1, xi, yr, ALU.mult)
        tt(oi, oi, t1, ALU.add)

    dve.wait_ge(z["landed"], 3 * 16)
    exp(dt[:], ldt[:], 2)
    dtb = dt[:].unsqueeze(2).broadcast_to([M, 2, STATES])
    tt(mag[:].rearrange("m (g p) -> m g p", g=2), ar[:].rearrange("m (g p) -> m g p", g=2), dtb, ALU.mult)
    tt(ang[:].rearrange("m (g p) -> m g p", g=2), ai[:].rearrange("m (g p) -> m g p", g=2), dtb, ALU.mult)
    turn = 2 * np.pi
    t_hi = 6.28125
    t_mid = float(np.float32(int((turn - t_hi) * 2 ** 20)) / 2 ** 20)
    t_lo = float(turn - t_hi - t_mid)
    pi_in = 3.1415925
    ts(w1[:], ang[:], 1 / turn, 12582912.0, ALU.mult, ALU.add)
    ts(w2[:], w1[:], 12582912.0, None, ALU.subtract)
    seq(nc.vector.scalar_tensor_tensor(w1[:], w2[:], -t_hi, ang[:], ALU.mult, ALU.add))
    seq(nc.vector.scalar_tensor_tensor(w1[:], w2[:], -t_mid, w1[:], ALU.mult, ALU.add))
    seq(nc.vector.scalar_tensor_tensor(w1[:], w2[:], -t_lo, w1[:], ALU.mult, ALU.add))
    ts(w1[:], w1[:], pi_in, -pi_in, ALU.min, ALU.max)
    ts(w2[:], w1[:], -1.0, None, ALU.mult)
    tt(w2[:], w2[:], w1[:], ALU.min)
    nc.vector.tensor_scalar(w2[:], w2[:], float(np.pi / 2), None, ALU.add).then_inc(z["sin_in"], 1)
    ts(ang[:], mag[:], float(LC), None, ALU.mult)
    exp(rows[:, R8], ang[:], P)
    exp(ang[:], mag[:], P)
    dve.wait_ge(z["sin_out"], 1)
    nc.vector.tensor_copy(rows[:, C8], w4[:])
    seq(nc.vector.tensor_copy(rows[:, S8], w3[:]))
    for _ in range(3):
        cmul(e1[:], e2[:], rows[:, C8], rows[:, S8], rows[:, C8], rows[:, S8], e3[:])
        nc.vector.tensor_copy(rows[:, C8], e1[:])
        seq(nc.vector.tensor_copy(rows[:, S8], e2[:]))
    nc.vector.memset(rows[:, PR], 1.0)
    nc.vector.memset(rows[:, PI], 0.0)
    tt(rows[:, PR + 1], ang[:], w4[:], ALU.mult)
    tt(rows[:, PI + 1], ang[:], w3[:], ALU.mult)
    for n in range(2, LC + 1):
        h = n // 2
        cmul(rows[:, PR + n], rows[:, PI + n], rows[:, PR + h], rows[:, PI + h],
             rows[:, PR + n - h], rows[:, PI + n - h], e1[:])
    tt(e1[:], ar[:], ar[:], ALU.mult)
    tt(e2[:], ai[:], ai[:], ALU.mult)
    tt(e1[:], e1[:], e2[:], ALU.add)
    seq(nc.vector.reciprocal(e3[:], e1[:]))
    ts(w1[:], rows[:, PR + 1], -1.0, None, ALU.add)
    ni = rows[:, PI + 1]
    tt(e1[:], w1[:], ar[:], ALU.mult)
    tt(e2[:], ni, ai[:], ALU.mult)
    tt(e1[:], e1[:], e2[:], ALU.add)
    tt(rows[:, FR], e1[:], e3[:], ALU.mult)
    tt(e1[:], ni, ar[:], ALU.mult)
    tt(e2[:], w1[:], ai[:], ALU.mult)
    tt(e1[:], e1[:], e2[:], ALU.subtract)
    nc.vector.tensor_tensor(rows[:, FI], e1[:], e3[:], ALU.mult).then_inc(z["made"], 1)


def ssm_tables_phase(nc, cst, psum, a, s):
    M = PAIRS
    with ExitStack() as ctx:
        def sb(name, shape, dt=F32):
            return ctx.enter_context(nc.sbuf_tensor(name, shape, dt))

        def sem(name):
            return new_sem(nc, name)

        cf = s["cf"]
        prev = sb("prev", [P, 2, M, LC + 1])
        b_raw = sb("b_raw", [P, 2, M, GCH])
        bbar = sb("bbar", [P, 2, M, GCH])
        wz = sb("wz", [P, 2, M, LC, GCH])
        free = s["wT"][:].rearrange("p i m x -> p (i m x)")
        tmp = free[:, 0:M * LC * GCH].rearrange("p (m s j) -> p m s j", m=M, s=LC)
        c_nat = sb("c_nat", [P, 2, 4, STATES])
        cT = sb("c_T", [P, 2, M, GCH])
        cb = sb("c_b", [P, 2, M, 2, GCH])
        dmat = sb("dmat", [P, GROUPS, GCH])
        kmat = sb("kmat", [P, GROUPS, GCH])
        shift = sb("shift", [P, P + (LC - 1) * GCH])
        rsq = sb("rsq", [P, 2, 2, M])
        rt = free[:, M * P:2 * M * P].rearrange("p (i m c) -> p i m c", i=2, m=M)
        tmp2 = s["toep"][:].rearrange("p g t i -> p (g t i)")[:, 0:M * LC * GCH].rearrange(
            "p (m s j) -> p m s j", m=M, s=LC)
        tmp_ca = s["toep"][:].rearrange("p g t i -> p (g t i)")[:, M * LC * GCH:].rearrange(
            "p (m s j) -> p m s j", m=M, s=LC)
        in_land, d_land, c_land = sem("in_land"), sem("d_land"), sem("c_land")
        ct_ps, ct_read = sem("ct_ps"), sem("ct_read")
        wz_made, k_ps, k_made, shift_made, dmat_made = (sem(n) for n in ("wz_made", "k_ps", "k_made",
                                                                         "shift_made", "dmat_made"))
        cT_made = sem("cT_made")
        ca_chain = Chain(sem("ca_chain"))
        t_ps, t_read, wt_ps, wt_read = sem("t_ps"), sem("t_read"), sem("wt_ps"), sem("wt_read")
        chain = Chain(sem("ssm_chain"))
        block = ctx.enter_context(nc.Block())

        @block.sync
        def _(sp):
            for i, n in enumerate(("ssm_c_re", "ssm_c_im")):
                sp.dma_start(c_nat[:, i], a[n][0].rearrange("(q g) i p -> (g i) q p", g=8)).then_inc(c_land, 16)
            sp.dma_start(dmat[:].rearrange("p g i -> p (g i)"), a["ssm_d"][0].partition_broadcast(P)
                         ).then_inc(d_land, 16)
            for i, n in enumerate(("ssm_b_re", "ssm_b_im")):
                sp.dma_start(b_raw[:, i], a[n][0].rearrange("(m g) p j -> (g p) m j", g=2)
                             ).then_inc(in_land, 16)
            sp.wait_ge(s["rows_out"], 96)

        @block.gpsimd
        def _(pool):
            nc.gpsimd.memset(shift[:], 0.0).then_inc(shift_made, 1)
            pool.wait_ge(shift_made, 1)
            nc.gpsimd.affine_select(out=shift[:], in_=shift[:], pattern=[[-1, shift.shape[1]]],
                                    compare_op=ALU.not_equal, fill=1.0, base=0,
                                    channel_multiplier=1).then_inc(shift_made, 1)
            pool.wait_ge(d_land, 16)
            nc.gpsimd.affine_select(out=dmat[:], in_=dmat[:], pattern=[[0, GROUPS], [-1, GCH]],
                                    compare_op=ALU.is_equal, fill=0.0, base=-(LC - 1) * GCH,
                                    channel_multiplier=1).then_inc(dmat_made, 1)

            def ptt(out, x, y, op):
                pool.wait_ge(ca_chain.sem, ca_chain.did(nc.gpsimd.tensor_tensor(out, x, y, op)))

            pool.wait_ge(cT_made, 1)
            full = [P, M, LC, GCH]
            fwd = [cf[:, ROW_AT[0] + 1:ROW_AT[0] + LC + 1].rearrange("p t m -> p m t").unsqueeze(3).broadcast_to(full),
                   cf[:, ROW_AT[1] + 1:ROW_AT[1] + LC + 1].rearrange("p t m -> p m t").unsqueeze(3).broadcast_to(full)]
            cc = [cT[:, i].unsqueeze(2).broadcast_to(full) for i in range(2)]
            ptt(s["ca"][:, 0], fwd[0], cc[0], ALU.mult)
            ptt(tmp_ca, fwd[1], cc[1], ALU.mult)
            ptt(s["ca"][:, 0], s["ca"][:, 0], tmp_ca, ALU.add)
            ptt(s["ca"][:, 1], fwd[0], cc[1], ALU.mult)
            ptt(tmp_ca, fwd[1], cc[0], ALU.mult)
            ptt(s["ca"][:, 1], s["ca"][:, 1], tmp_ca, ALU.subtract)

        @block.scalar
        def _(act):
            act.wait_ge(ct_ps, 1)
            nc.scalar.copy(cT[:, 0], psum[:, 1, 0:M * GCH].rearrange("p (m i) -> p m i", m=M))
            nc.scalar.activation(cT[:, 1], psum[:, 2, 0:M * GCH].rearrange("p (m i) -> p m i", m=M), ACT.Copy,
                                 scale=-1.0).then_inc(cT_made, 1)
            for i in range(2):
                for q in range(4):
                    act.wait_ge(wt_ps, 4 * i + q + 1)
                    nc.scalar.copy(s["wT"][:, i, 4 * q:4 * q + 4],
                                   psum[:, 4 + q, :].rearrange("p (m x) -> p m x", m=4)).then_inc(wt_read, 1)
            act.wait_ge(ca_chain.sem, 6)
            for t in range(LC):
                act.wait_ge(t_ps, t + 1)
                nc.scalar.copy(s["toep"][:, :, t], psum[:, t % 4, :].rearrange("p (g i) -> p g i", i=GCH)
                               ).then_inc(t_read, 1)

        @block.vector
        def _(dve):
            def seq(ins):
                dve.wait_ge(chain.sem, chain.did(ins))

            def tt(out, x, y, op):
                seq(nc.vector.tensor_tensor(out, x, y, op))

            def cmul(*products):
                for orr, oi, xr, xi, yr, yi, t1, t2 in products:
                    nc.vector.tensor_tensor(orr, xr, yr, ALU.mult)
                    nc.vector.tensor_tensor(t1, xi, yi, ALU.mult)
                    nc.vector.tensor_tensor(oi, xr, yi, ALU.mult)
                    last = nc.vector.tensor_tensor(t2, xi, yr, ALU.mult)
                seq(last)
                for orr, oi, _, _, _, _, t1, t2 in products:
                    nc.vector.tensor_tensor(orr, orr, t1, ALU.subtract)
                    last = nc.vector.tensor_tensor(oi, oi, t2, ALU.add)
                seq(last)

            PR, PI, FR, FI, R8, C8, S8 = ROW_AT
            rot = s["rot"]
            nc.vector.memset(rot[:, 0, :, 0], 1.0)
            nc.vector.memset(rot[:, 1, :, 0], 0.0)
            nc.vector.tensor_copy(rsq[:, 0, 0], cf[:, C8])
            seq(nc.vector.tensor_copy(rsq[:, 0, 1], cf[:, S8]))
            n, cur = 1, 0
            while n < CH:
                nar = [P, M, n]
                er, ei_ = (rsq[:, cur, i].unsqueeze(2).broadcast_to(nar) for i in range(2))
                products = [(rot[:, 0, :, n:2 * n], rot[:, 1, :, n:2 * n], rot[:, 0, :, 0:n], rot[:, 1, :, 0:n],
                             er, ei_, rt[:, 0, :, 0:n], rt[:, 1, :, 0:n])]
                n *= 2
                if n < CH:
                    products.append((rsq[:, 1 - cur, 0], rsq[:, 1 - cur, 1], rsq[:, cur, 0], rsq[:, cur, 1],
                                     rsq[:, cur, 0], rsq[:, cur, 1], rt[:, 0, :, CH // 2 - 1], rt[:, 1, :, CH // 2 - 1]))
                cmul(*products)
                cur = 1 - cur
            seq(nc.vector.memset(cb[:], 0.0))
            dve.wait_ge(cT_made, 1)
            for g in range(2):
                half = slice(g * 64, g * 64 + 64)
                seq(nc.vector.tensor_copy(cb[half, :, :, g], cT[half]))
            for n in range(LC + 1):
                nc.vector.tensor_copy(prev[:, 0, :, LC - n], cf[:, PR + n])
                last = nc.vector.tensor_copy(prev[:, 1, :, LC - n], cf[:, PI + n])
            seq(last)
            wide = [P, M, GCH]
            dve.wait_ge(in_land, 32)
            cmul((bbar[:, 0], bbar[:, 1], cf[:, FR].unsqueeze(2).broadcast_to(wide),
                  cf[:, FI].unsqueeze(2).broadcast_to(wide), b_raw[:, 0], b_raw[:, 1], tmp[:, :, 0, :],
                  tmp[:, :, 1, :]))
            full = [P, M, LC, GCH]
            cmul((wz[:, 0], wz[:, 1], prev[:, 0, :, 1:].unsqueeze(3).broadcast_to(full),
                  prev[:, 1, :, 1:].unsqueeze(3).broadcast_to(full),
                  bbar[:, 0].unsqueeze(2).broadcast_to(full), bbar[:, 1].unsqueeze(2).broadcast_to(full), tmp,
                  tmp2))
            nc.vector.tensor_copy(s["r8"][:], cf[:, R8]).then_inc(wz_made, 1)
            nc.vector.tensor_copy(s["a8"][:, 0], cf[:, PR + LC])
            seq(nc.vector.tensor_copy(s["a8"][:, 1], cf[:, PI + LC]))
            dve.wait_ge(k_ps, 1)
            dve.wait_ge(dmat_made, 1)
            nc.vector.tensor_tensor(kmat[:].rearrange("p g i -> p (g i)"), psum[:, 3, :],
                                    dmat[:].rearrange("p g i -> p (g i)"), ALU.add).then_inc(k_made, 1)

        @block.tensor
        def _(pe):
            ident = cst["ident"]
            pe.wait_ge(c_land, 32)
            for i in range(2):
                for q in range(4):
                    for g in range(2):
                        sel = ident[:].rearrange("p (m g i) -> p m g i", g=2, i=GCH)[:, :, g]
                        mm = pe.matmul(psum[64 * g:64 * g + 64, 1 + i, q * 64:(q + 1) * 64].rearrange(
                            "p (m i) -> p m i", m=4), c_nat[:, i, q], sel, start=True, stop=True)
            mm.then_inc(ct_ps, 1)
            pe.wait_ge(wz_made, 1)
            for m in range(M):
                for i in range(2):
                    mm = pe.matmul(psum[:, 3, m * 32:(m + 1) * 32],
                                   wz[:, i, m].rearrange("p s j -> p (s j)"),
                                   cb[:, i, m].rearrange("p g i -> p (g i)"), start=(i == 0), stop=(i == 1))
            mm.then_inc(k_ps, 1)
            for i in range(2):
                for q in range(4):
                    if i:
                        pe.wait_ge(wt_read, q + 1)
                    for m in range(4):
                        mm = pe.transpose(psum[:, 4 + q, m * P:(m + 1) * P],
                                          wz[:, i, 4 * q + m].rearrange("p s j -> p (s j)"), ident[:])
                    mm.then_inc(wt_ps, 1)
            pe.wait_ge(k_made, 1)
            pe.wait_ge(shift_made, 2)
            for t in range(LC):
                if t >= 4:
                    pe.wait_ge(t_read, t - 3)
                off = GCH * (LC - 1 - t)
                mm = pe.matmul(psum[:, t % 4, :], shift[:, off:off + P], kmat[:].rearrange("p g i -> p (g i)"),
                               start=True, stop=True)
                mm.then_inc(t_ps, 1)


def ssm_input_phase(nc, cst, psum, t, s):
    with ExitStack() as ctx:
        def sb(name, shape, dt=F32):
            return ctx.enter_context(nc.sbuf_tensor(name, shape, dt))

        def sem(name):
            return new_sem(nc, name)

        us_b = sb("us_b", [NB, NT, D_SSM])
        us_g = sb("us_g", [NB, GROUPS, NT, GCH])
        us_land, us_made, ps_full, dve_read, act_read = (sem(n) for n in (
            "us_land", "us_made", "uc_ps", "uc_dve_read", "uc_act_read"))
        block = ctx.enter_context(nc.Block())
        uc = s["uc"]

        @block.sync
        def _(sp):
            for b in range(NB):
                sp.dma_start(us_b[b:b + 1], t["us"][b * NT:(b + 1) * NT]).then_inc(us_land, 16)

        @block.vector
        def _(dve):
            dve.wait_ge(us_land, 16 * NB)
            nc.vector.tensor_copy(us_g[:], us_b[:].rearrange("b s (g j) -> b g s j", j=GCH)).then_inc(us_made, 1)
            for q in range(0, 8, 2):
                dve.wait_ge(ps_full, q + 1)
                nc.vector.tensor_copy(uc[:, 4 * q:4 * q + 4, 0:CH],
                                      psum[:, q, :].rearrange("p (g c) -> p g c", g=4)).then_inc(dve_read, 1)
            dve.wait_ge(ps_full, 9)
            nc.vector.tensor_copy(uc[:, :, CH:CHS], psum[:, 0, 0:GROUPS * NB].rearrange(
                "p (g c) -> p g c", g=GROUPS)).then_inc(dve_read, 1)

        @block.scalar
        def _(act):
            for q in range(1, 8, 2):
                act.wait_ge(ps_full, q + 1)
                nc.scalar.copy(uc[:, 4 * q:4 * q + 4, 0:CH],
                               psum[:, q, :].rearrange("p (g c) -> p g c", g=4)).then_inc(act_read, 1)

        @block.tensor
        def _(pe):
            for q in range(8):
                for g in range(4):
                    mm = pe.transpose(psum[:, q, g * P:(g + 1) * P],
                                      t["u"][:, 4 * q + g].rearrange("p s j -> p (s j)"), cst["ident"][:])
                mm.then_inc(ps_full, 1)
            pe.wait_ge(us_made, 1)
            pe.wait_ge(dve_read, 1)
            for g in range(GROUPS):
                mm = pe.transpose(psum[:, 0, g * NB:(g + 1) * NB], us_g[:, g].rearrange("p s j -> p (s j)"),
                                  cst["ident"][0:NB, 0:NB])
            mm.then_inc(ps_full, 1)


def ssm_scan_phase(nc, cst, psum, a, o, scr, t, s):
    M, QM = PAIRS, 4
    with ExitStack() as ctx:
        def sb(name, shape, dt=F32):
            return ctx.enter_context(nc.sbuf_tensor(name, shape, dt))

        def sem(name):
            return new_sem(nc, name)

        hx = sb("hx", [P, 2, M, 1 + CH + NB])
        g_sb = sb("g_sb", [P, 2, M, CHS])
        q1, q2 = sb("q1", [P, QM, CH]), sb("q2", [P, QM, CH])
        sr, si = sb("sr", [P, QM, CH]), sb("si", [P, QM, CH])
        decay = sb("decay", [P, M, CH])
        h0 = sb("h0", [P, 2, P])
        hf = sb("hf", [P, 2, NB, M])
        hf_t = sb("hf_t", [P, 2, P])
        hp_t = sb("hp_t", [M, 2, P])
        ys = s["wT"][0:NB].rearrange("p i m c -> p (i m c)").rearrange("p (t x) -> p t x", t=NT)
        h0_land, h0_ps, h0_put, g_ps, g_read = (sem(n) for n in ("h0_land", "h0_ps", "h0_put", "g_ps", "g_read"))
        states_made, y_ps, y_dve, y_act = (sem(n) for n in ("states_made", "y_ps", "y_dve", "y_act"))
        ys_ps, ys_read, fin_ps, fin_read, fin_out = (sem(n) for n in ("ys_ps", "ys_read", "fin_ps", "fin_read",
                                                                      "fin_out"))
        chain = Chain(sem("scan_chain"))
        block = ctx.enter_context(nc.Block())
        y = t["u"][:].rearrange("p g s j -> p (g s j)").rearrange("p (t x) -> p t x", t=LC)

        @block.sync
        def _(sp):
            for i, n in enumerate(("state_ssm_re", "state_ssm_im")):
                sp.dma_start(h0[:, i], a[n][0].rearrange("b (m g) p -> (b m) (g p)", g=2)).then_inc(h0_land, 16)
            sp.wait_ge(fin_read, 1)
            for i, n in enumerate(("re", "im")):
                sp.dma_start(o[n + "_prompt"][0, 0].rearrange("(m g) p -> m (g p)", g=2), hp_t[:, i]
                             ).then_inc(fin_out, 16)
                sp.dma_start(o[n + "_sample"][0].rearrange("b (m g) p -> (b m) (g p)", g=2), hf_t[:, i]
                             ).then_inc(fin_out, 16)
            sp.wait_ge(ys_read, 8)
            sp.dma_start(scr["ys"].rearrange("(b t) c -> b t c", t=NT), ys).then_inc(fin_out, 16)
            sp.wait_ge(fin_out, 80)

        @block.vector
        def _(dve):
            def seq(ins):
                dve.wait_ge(chain.sem, chain.did(ins))

            def tt(out, x, z, op):
                seq(nc.vector.tensor_tensor(out, x, z, op))

            nc.vector.tensor_copy(decay[:], s["r8"][:].unsqueeze(2).broadcast_to([P, M, CH]))
            seq(nc.vector.memset(hx[:, :, :, 0], 0.0))
            seq(nc.vector.memset(decay[:, :, 0:1], 0.0))
            dve.wait_ge(h0_ps, 1)
            for i in range(2):
                last = nc.vector.tensor_copy(hx[:, i, :, 1 + CH:], psum[:, i, 0:P].rearrange(
                    "p (b m) -> p m b", b=NB))
            last.then_inc(h0_put, 1)
            rot = s["rot"]
            for q in range(M // QM):
                ms = slice(q * QM, (q + 1) * QM)
                dve.wait_ge(g_read, 2 * (q + 1) * QM)
                gr, gi = g_sb[:, 0, ms, 0:CH], g_sb[:, 1, ms, 0:CH]
                cr, ci = rot[:, 0, ms], rot[:, 1, ms]
                tt(sr[:], gr, cr, ALU.mult)
                tt(q1[:], gi, ci, ALU.mult)
                tt(sr[:], sr[:], q1[:], ALU.add)
                tt(si[:], gi, cr, ALU.mult)
                tt(q2[:], gr, ci, ALU.mult)
                tt(si[:], si[:], q2[:], ALU.subtract)
                flat = "p m c -> p (m c)"
                dec = decay[:, ms].rearrange(flat)
                seq(nc.vector.tensor_tensor_scan(q1[:].rearrange(flat), dec, sr[:].rearrange(flat), 0.0,
                                                 ALU.mult, ALU.add))
                seq(nc.vector.tensor_tensor_scan(q2[:].rearrange(flat), dec, si[:].rearrange(flat), 0.0,
                                                 ALU.mult, ALU.add))
                hr, hi = hx[:, 0, ms, 1:1 + CH], hx[:, 1, ms, 1:1 + CH]
                tt(hr, q1[:], cr, ALU.mult)
                tt(sr[:], q2[:], ci, ALU.mult)
                tt(hr, hr, sr[:], ALU.subtract)
                tt(hi, q1[:], ci, ALU.mult)
                tt(si[:], q2[:], cr, ALU.mult)
                nc.vector.tensor_tensor(hi, hi, si[:], ALU.add).then_inc(states_made, 1)
            b0 = [h0_ for h0_ in (hx[:, 0, :, 1 + CH:].rearrange("p m b -> p b m"),
                                  hx[:, 1, :, 1 + CH:].rearrange("p m b -> p b m"))]
            a8 = [s["a8"][:, i].unsqueeze(1).broadcast_to([P, NB, M]) for i in range(2)]
            tmp = q1[:].rearrange("p m c -> p (m c)")[:, 0:P].rearrange("p (b m) -> p b m", b=NB)
            dve.wait_ge(states_made, 4)
            dve.wait_ge(h0_put, 1)
            gs = [g_sb[:, i, :, CH:].rearrange("p m b -> p b m") for i in range(2)]
            tt(hf[:, 0], b0[0], a8[0], ALU.mult)
            tt(tmp, b0[1], a8[1], ALU.mult)
            tt(hf[:, 0], hf[:, 0], tmp, ALU.subtract)
            tt(hf[:, 0], hf[:, 0], gs[0], ALU.add)
            tt(hf[:, 1], b0[0], a8[1], ALU.mult)
            tt(tmp, b0[1], a8[0], ALU.mult)
            tt(hf[:, 1], hf[:, 1], tmp, ALU.add)
            nc.vector.tensor_tensor(hf[:, 1], hf[:, 1], gs[1], ALU.add).then_inc(states_made, 1)
            for q in range(0, 8, 2):
                dve.wait_ge(y_ps, q + 1)
                out = y.rearrange("p t (m g i) -> p g m t i", g=2, i=GCH)[:, q % 2, 4 * (q // 2):4 * (q // 2) + 4]
                nc.vector.tensor_copy(out, psum[:, 2 + q % 4, :].rearrange("p (g t i) -> p g t i", g=4, t=LC)
                                      ).then_inc(y_dve, 1)
            dve.wait_ge(fin_ps, 1)
            nc.vector.tensor_copy(hp_t[:], psum[0:M, 0, 0:2 * P].rearrange("p (i x) -> p i x", i=2))
            nc.vector.tensor_copy(hf_t[:], psum[:, 1, 0:2 * P].rearrange("p (i x) -> p i x", i=2)
                                  ).then_inc(fin_read, 1)

        @block.scalar
        def _(act):
            for n in range(2 * M):
                m, i = divmod(n, 2)
                act.wait_ge(g_ps, n + 1)
                nc.scalar.copy(g_sb[:, i, m], psum[:, 2 + n % 6, 0:CHS]).then_inc(g_read, 1)
            for q in range(8):
                act.wait_ge(ys_ps, q + 1)
                for j in range(4):
                    out = ys.rearrange("p t (m g i) -> p g m t i", g=2, i=GCH)[:, q % 2, 4 * (q // 2) + j]
                    last = nc.scalar.copy(out, psum[0:NB, q % 2, j * P:(j + 1) * P].rearrange(
                        "p (t i) -> p t i", t=LC))
                last.then_inc(ys_read, 1)
            for q in range(1, 8, 2):
                act.wait_ge(y_ps, q + 1)
                for j in range(4):
                    out = y.rearrange("p t (m g i) -> p g m t i", g=2, i=GCH)[:, 1, 4 * (q // 2) + j]
                    last = nc.scalar.copy(out, psum[:, 2 + q % 4, j * P:(j + 1) * P].rearrange(
                        "p (t i) -> p t i", t=LC))
                last.then_inc(y_act, 1)

        @block.tensor
        def _(pe):
            uc = s["uc"]
            pe.wait_ge(h0_land, 32)
            for i in range(2):
                mm = pe.transpose(psum[:, i, 0:P], h0[:, i], cst["ident"][:])
            mm.then_inc(h0_ps, 1)
            for m in range(M):
                for i in range(2):
                    n = 2 * m + i
                    if n >= 6:
                        pe.wait_ge(g_read, n - 5)
                    for g in range(2):
                        mm = pe.matmul(psum[64 * g:64 * g + 64, 2 + n % 6, 0:CHS],
                                       s["wT"][:, i, m, 64 * g:64 * g + 64], uc[:, 2 * m + g],
                                       start=True, stop=True)
                    mm.then_inc(g_ps, 1)
            pe.wait_ge(h0_put, 1)
            for q in range(8):
                if q >= 2:
                    pe.wait_ge(ys_read, q - 1)
                rows = slice(64 * (q % 2), 64 * (q % 2) + 64)
                for j in range(4):
                    m = 4 * (q // 2) + j
                    g = 2 * m + q % 2
                    out = psum[0:NB, q % 2, j * P:(j + 1) * P]
                    pe.matmul(out, uc[:, g, CH:CHS], s["toep"][:, g].rearrange("p t i -> p (t i)"),
                              start=True, stop=False)
                    pe.matmul(out, hx[rows, 0, m, 1 + CH:], s["ca"][rows, 0, m].rearrange("p t i -> p (t i)"),
                              start=False, stop=False)
                    mm = pe.matmul(out, hx[rows, 1, m, 1 + CH:], s["ca"][rows, 1, m].rearrange("p t i -> p (t i)"),
                                   start=False, stop=True)
                mm.then_inc(ys_ps, 1)
            pe.wait_ge(g_read, 2 * M)
            for q in range(8):
                pe.wait_ge(states_made, q // 2 + 1)
                if q >= 4:
                    if q % 2 == 0:
                        pe.wait_ge(y_dve, (q - 4) // 2 + 1)
                    else:
                        pe.wait_ge(y_act, (q - 4) // 2 + 1)
                rows = slice(64 * (q % 2), 64 * (q % 2) + 64)
                for j in range(4):
                    m = 4 * (q // 2) + j
                    g = 2 * m + q % 2
                    out = psum[:, 2 + q % 4, j * P:(j + 1) * P]
                    pe.matmul(out, uc[:, g, 0:CH], s["toep"][:, g].rearrange("p t i -> p (t i)"),
                              start=True, stop=False)
                    pe.matmul(out, hx[rows, 0, m, 0:CH], s["ca"][rows, 0, m].rearrange("p t i -> p (t i)"),
                              start=False, stop=False)
                    mm = pe.matmul(out, hx[rows, 1, m, 0:CH], s["ca"][rows, 1, m].rearrange("p t i -> p (t i)"),
                                   start=False, stop=True)
                mm.then_inc(y_ps, 1)
            pe.wait_ge(states_made, 5)
            pe.wait_ge(ys_read, 8)
            for i in range(2):
                pe.transpose(psum[0:M, 0, i * P:(i + 1) * P], hx[:, i, :, CH], cst["ident"][:])
                mm = pe.transpose(psum[:, 1, i * P:(i + 1) * P], hf[:, i].rearrange("p b m -> p (b m)"),
                                  cst["ident"][:])
            mm.then_inc(fin_ps, 1)


def score_off(i):
    return P * i * (i + 1) // 2


EARLY, LATE = (2, 3, 4, 5), (6, 7)


def index_phase(nc, cst, psum, a, t, x):
    NCUT = PAGES * PAGE // 512
    with ExitStack() as ctx:
        def sb(name, shape, dt=F32):
            return ctx.enter_context(nc.sbuf_tensor(name, shape, dt))

        def sem(name):
            return new_sem(nc, name)

        KR = 3
        psc, ssc, gidx = x["psc"], x["ssc"], x["gidx"]
        relu = sb("relu", [P, 4, 512])
        wis = sb("wis", [P, TILES, IH])
        pt = sb("pt", [P, NB], I32)
        sub = sb("sub", [P, 1], I32)
        subf = sb("subf", [P, 1])
        kx = sb("kx", [P, KR, PAGES, IDX])
        kxT = sb("kxT", [P, 2, PAGES // 2, P])
        qib = sb("qib", [P, IH, NS])
        qz = sb("qz", [P, 2, 2, 2, P])
        qi2 = sb("qi2", [P, 2, NB, IH, NT])
        wT = sb("wT", [IH, NS])
        expand = sb("expand", [IH, IH * NT])
        same_t = sb("same_t", [IH * NT, NB, NT])
        rowi = sb("rowi", [P, NT], I32)
        coli = sb("coli", [P, NT], I32)
        wm = sb("wm", [IH * NT, NS])
        w8 = sb("w8", [IH * NT, NB, NS])
        rs = sb("rs", [IH * NT, 2, 512])
        tail = sb("tail", [NS, NT])
        pt_land, sub_made, idx_made, qib_land = (sem(n) for n in ("pt_land", "sub_made", "idx_made", "qib_land"))
        kx_land = [sem(f"kx_land{i}") for i in range(KR)]
        wis_made, d_ps, r_made, r_used = (sem(n) for n in ("wis_made", "d_ps", "r_made", "r_used"))
        masked, tab_made = sem("masked"), sem("tab_made")
        small_ps, w_put, kxT_ps, kxT_read = (sem(n) for n in ("small_ps", "w_put", "kxT_ps", "kxT_read"))
        sd_ps, sr_made, ws_ps = sem("sd_ps"), sem("sr_made"), sem("ws_ps")
        bias01, q_put, qi2_clear = sem("bias01"), sem("q_put"), sem("qi2_clear")
        chain = Chain(sem("index_chain"))
        groups = [(i, c, min(c + 512, (i + 1) * P), h) for i in range(TILES)
                  for c in range(0, (i + 1) * P, 512) for h in range(IH)]
        block = ctx.enter_context(nc.Block())

        @block.sync
        def _(sp):
            for r in range(8):
                sp.dma_start(pt[r:P:8], a["page_table"].rearrange("b j -> j b"),
                             allow_slow_non_contiguous=True).then_inc(pt_land, 16)
            for h in range(IH):
                for half in range(2):
                    sp.dma_start(qib[64 * half:64 * half + 64, h],
                                 t["qiT"][64 * (h % 2):64 * (h % 2) + 64, h // 2, SEQ:TOK]).then_inc(qib_land, 16)

        @block.gpsimd
        def _(pool):
            nc.gpsimd.iota(sub[:], pattern=[[0, 1]], base=0, channel_multiplier=1).then_inc(sub_made, 1)
            nc.gpsimd.iota(rowi[:], pattern=[[0, NT]], base=0, channel_multiplier=1)
            nc.gpsimd.iota(coli[:], pattern=[[1, NT]], base=0, channel_multiplier=0).then_inc(sub_made, 1)
            nc.gpsimd.memset(qz[:], 0.0).then_inc(q_put, 1)
            nc.gpsimd.memset(qi2[:], 0.0).then_inc(qi2_clear, 1)
            nc.gpsimd.memset(expand[:], 1.0).then_inc(tab_made, 1)
            nc.gpsimd.memset(same_t[:], 0.0).then_inc(tab_made, 1)
            nc.gpsimd.memset(w8[:], 0.0).then_inc(tab_made, 1)
            pool.wait_ge(tab_made, 3)
            nc.gpsimd.affine_select(out=expand[:].rearrange("q (h t) -> q h t", h=IH),
                                    in_=expand[:].rearrange("q (h t) -> q h t", h=IH),
                                    pattern=[[-1, IH], [0, NT]], compare_op=ALU.is_equal, fill=0.0, base=0,
                                    channel_multiplier=1).then_inc(tab_made, 1)
            for h in range(IH):
                pool.wait_ge(tab_made, 4 + h)
                nc.gpsimd.affine_select(out=same_t[:], in_=same_t[:], pattern=[[0, NB], [-1, NT]],
                                        compare_op=ALU.not_equal, fill=1.0, base=-NT * h,
                                        channel_multiplier=1).then_inc(tab_made, 1)
            pool.wait_ge(idx_made, 1)

            def gather_keys(b):
                nc.gpsimd.indirect_dma_start(
                    out=kx[:, b % KR].rearrange("p k d -> p (k d)"), out_offset=None,
                    in_=a["cache_kidx"][0].rearrange("n (r k) d -> (n r) (k d)", r=8),
                    in_offset=bass.IndirectOffsetOnAxis(ap=gidx[:, b:b + 1], axis=0)).then_inc(kx_land[b % KR], 16)

            for b in range(KR):
                gather_keys(b)
            nc.gpsimd.memset(x["pbias"][:, 0:score_off(2)], 0.0).then_inc(bias01, 1)
            for i in range(2):
                diag = x["pbias"][:, score_off(i) + i * P:score_off(i) + (i + 1) * P]
                pool.wait_ge(bias01, 1)
                nc.gpsimd.affine_select(out=diag, in_=diag, pattern=[[-1, P]], compare_op=ALU.is_ge,
                                        fill=NEG, base=0, channel_multiplier=1).then_inc(bias01, 1)
            for i in range(TILES):
                pool.wait_ge(r_used, sum(1 for g in groups if g[0] <= i))
                diag = psc[:, score_off(i) + i * P:score_off(i) + (i + 1) * P]
                nc.gpsimd.affine_select(out=diag, in_=diag, pattern=[[-1, P]], compare_op=ALU.is_ge,
                                        fill=-3e38, base=0, channel_multiplier=1).then_inc(masked, 1)
            for b in range(KR, NB):
                pool.wait_ge(kxT_ps, 2 * (b - KR) + 2)
                gather_keys(b)
            pool.wait_ge(masked, TILES)
            pool.wait_ge(bias01, 3)

        @block.scalar
        def _(act):
            def put_queries(i):
                if i >= 2:
                    act.wait_ge(d_ps, sum(1 for g in groups if g[0] <= i - 2))
                for half in range(2):
                    rows = slice(64 * half, 64 * half + 64)
                    nc.scalar.copy(qz[rows, i % 2, :, half], t["qiT"][rows, :, i * P:(i + 1) * P]).then_inc(q_put, 1)

            act.wait_ge(q_put, 1)
            put_queries(0)
            put_queries(1)
            for n, (i, c0, c1, h) in enumerate(groups):
                if c0 == 0 and h == 0 and 1 <= i < TILES - 1:
                    put_queries(i + 1)
                act.wait_ge(d_ps, n + 1)
                if n >= 4:
                    act.wait_ge(r_used, n - 3)
                nc.scalar.activation(relu[:, n % 4, 0:c1 - c0], psum[:, n % 4, 0:c1 - c0], ACT.Relu
                                     ).then_inc(r_made, 1)

            def read_keys(g):
                b, q = divmod(g, 2)
                act.wait_ge(kxT_ps, g + 1)
                if b >= 2:
                    act.wait_ge(sd_ps, 5 * (b - 2) + 4)
                nc.scalar.copy(kxT[:, b % 2, 4 * q:4 * q + 4],
                               psum[:, 7, :].rearrange("p (j k) -> p j k", j=4)).then_inc(kxT_read, 1)

            read_keys(0)
            read_keys(1)
            for n in range(5 * NB):
                w = 512 if n % 5 < 4 else NT
                act.wait_ge(sd_ps, n + 1)
                if n >= 2:
                    act.wait_ge(ws_ps, n - 1)
                nc.scalar.activation(rs[:, n % 2, 0:w], psum[0:IH * NT, 5 + n % 2, 0:w], ACT.Relu
                                     ).then_inc(sr_made, 1)
                if n // 5 + 1 < NB and n % 5 in (2, 4):
                    read_keys(2 * (n // 5 + 1) + n % 5 // 4)

        @block.vector
        def _(dve):
            def seq(ins):
                dve.wait_ge(chain.sem, chain.did(ins))

            find = key_search(nc, dve, chain, x, EARLY)
            nc.vector.memset(x["find"]["one"][:], 1.0)
            scale = float(IDX) ** -0.5 * float(IH) ** -0.5
            nc.vector.tensor_scalar(wis[:], t["kiwi"][:, 0:TILES, IDX:], scale, None, ALU.mult
                                    ).then_inc(wis_made, 1)
            dve.wait_ge(wis_made, 1)
            for n, (i, c0, c1, h) in enumerate(groups):
                if (i, c0, h) == (2, 0, 0):
                    dve.wait_ge(sub_made, 2)
                    dve.wait_ge(pt_land, 16 * 8)
                    seq(nc.vector.tensor_scalar(sub[:], sub[:], 7, None, ALU.bitwise_and))
                    seq(nc.vector.tensor_copy(subf[:], sub[:]))
                    nc.vector.tensor_scalar(gidx[:], pt[:], 8.0, subf[:], ALU.mult, ALU.add).then_inc(idx_made, 1)
                    seq(nc.vector.tensor_scalar(rowi[:], rowi[:], 7, None, ALU.bitwise_and))
                    seq(nc.vector.tensor_tensor(tail[:], rowi[0:NS], coli[0:NS], ALU.is_ge))
                    seq(nc.vector.tensor_scalar(tail[:], tail[:], -1.0, 3e38, ALU.add, ALU.mult))
                dve.wait_ge(r_made, n + 1)
                acc = psc[:, score_off(i) + c0:score_off(i) + c1]
                if h == 0:
                    ins = nc.vector.tensor_scalar(acc, relu[:, n % 4, 0:c1 - c0], wis[:, i, 0:1], None, ALU.mult)
                else:
                    dve.wait_ge(r_used, n)
                    ins = nc.vector.scalar_tensor_tensor(acc, relu[:, n % 4, 0:c1 - c0], wis[:, i, h:h + 1], acc,
                                                         ALU.mult, ALU.add)
                ins.then_inc(r_used, 1)
                if h == IH - 1 and c1 == (i + 1) * P and i - 2 in EARLY:
                    dve.wait_ge(masked, i - 1)
                    find.prepare(EARLY.index(i - 2))
            dve.wait_ge(qib_land, 16 * 8)
            dve.wait_ge(qi2_clear, 1)
            for half in range(2):
                rows = slice(64 * half, 64 * half + 64)
                last = nc.vector.tensor_copy(qi2[rows, half].rearrange("p b h t -> p h b t"),
                                             qib[rows].rearrange("p h (b t) -> p h b t", b=NB))
            last.then_inc(w_put, 1)
            dve.wait_ge(small_ps, 1)
            nc.vector.tensor_copy(wT[:], psum[0:IH, 7, 0:NS]).then_inc(w_put, 1)
            dve.wait_ge(small_ps, 2)
            dve.wait_ge(tab_made, 8)
            seq(nc.vector.scalar_tensor_tensor(wm[:], psum[0:IH * NT, 7, 0:NS], scale,
                                               same_t[:].rearrange("q b t -> q (b t)"), ALU.mult, ALU.mult))
            for b in range(NB):
                last = nc.vector.tensor_copy(w8[:, b, b * NT:(b + 1) * NT], wm[:, b * NT:(b + 1) * NT])
            last.then_inc(w_put, 1)
            for at in range(32):
                if at == 16:
                    find.narrow()
                find.bit(at)
            for at in range(len(EARLY)):
                find.mark(at)
            dve.wait_ge(ws_ps, 5 * NB)
            nat = ssc[:, 0:PAST].rearrange("r (k j e) -> r e j k", j=PAGES // 2, e=2)
            for c in range(4):
                e, q = divmod(c, 2)
                nc.vector.tensor_copy(nat[:, e, 4 * q:4 * q + 4],
                                      psum[0:NS, c, :].rearrange("r (j k) -> r j k", j=4))
            nc.vector.tensor_tensor(ssc[:, PAST:], psum[0:NS, 4, 0:NT], tail[:], ALU.add)

        @block.tensor
        def _(pe):
            for n, (i, c0, c1, h) in enumerate(groups):
                if n >= 4:
                    pe.wait_ge(r_made, n - 3)
                pe.wait_ge(q_put, 1 + 2 * (i + 1))
                pe.matmul(psum[:, n % 4, 0:c1 - c0], qz[:, i % 2, h // 2, h % 2],
                          t["kiT"][:, 0, c0:c1], start=True, stop=True).then_inc(d_ps, 1)
            pe.transpose(psum[0:IH, 7, 0:NS], t["kiwi"][0:NS, TILES, IDX:], cst["ident"][0:NS, 0:NS]
                         ).then_inc(small_ps, 1)
            pe.wait_ge(w_put, 2)
            pe.wait_ge(tab_made, 4)
            pe.matmul(psum[0:IH * NT, 7, 0:NS], expand[:], wT[:], start=True, stop=True).then_inc(small_ps, 1)
            pe.wait_ge(r_made, len(groups))
            pe.wait_ge(w_put, 3)

            def turn_keys(b, q):
                pe.wait_ge(kx_land[b % KR], 16 * (b // KR + 1))
                if 2 * b + q >= 1:
                    pe.wait_ge(kxT_read, 2 * b + q)
                for j in range(4):
                    mm = pe.transpose(psum[:, 7, j * P:(j + 1) * P],
                                      kx[:, b % KR, 8 * q + 2 * j:8 * q + 2 * j + 2].rearrange("p k d -> p (k d)"),
                                      cst["ident"][:])
                mm.then_inc(kxT_ps, 1)

            turn_keys(0, 0)
            turn_keys(0, 1)
            for b in range(NB):
                pe.wait_ge(kxT_read, 2 * b + 2)
                for c in range(6):
                    if c < 5:
                        n = 5 * b + c
                        if n >= 2:
                            pe.wait_ge(sr_made, n - 1)
                        e, q = divmod(c, 2)
                        rhs = kxT[:, b % 2, 4 * q:4 * q + 4].rearrange("p j k -> p (j k)") if c < 4 else \
                            t["kiT"][:, 0, SEQ + b * NT:SEQ + (b + 1) * NT]
                        w = 512 if c < 4 else NT
                        pe.matmul(psum[0:IH * NT, 5 + n % 2, 0:w], qi2[:, e % 2, b].rearrange("p h t -> p (h t)"),
                                  rhs, start=True, stop=True).then_inc(sd_ps, 1)
                    if c >= 1:
                        n = 5 * b + c - 1
                        w = 512 if c - 1 < 4 else NT
                        pe.wait_ge(sr_made, n + 1)
                        pe.matmul(psum[0:NS, c - 1, 0:w], w8[:, b], rs[:, n % 2, 0:w],
                                  start=(b == 0), stop=(b == NB - 1)).then_inc(ws_ps, 1)
                    if b + 1 < NB and c in (2, 4):
                        turn_keys(b + 1, c // 4)


class KeySearch:

    def __init__(self, nc, dve, chain, k, regions):
        self.nc, self.dve, self.chain, self.k, self.regions = nc, dve, chain, k, regions
        self.g = len(regions)

    def seq(self, ins):
        self.dve.wait_ge(self.chain.sem, self.chain.did(ins))

    def prepare(self, r):
        nc, k = self.nc, self.k
        rows, src, first, n, _ = self.regions[r]
        key, si = k["key"][0:rows, 0:n], src.bitcast(I32)
        self.seq(nc.vector.tensor_scalar(src, src, 0.0, None, ALU.add))
        self.seq(nc.vector.tensor_scalar(key, si, 31, 0x7FFFFFFF, ALU.arith_shift_right, ALU.bitwise_and))
        self.seq(nc.vector.tensor_tensor(key, key, si, ALU.bitwise_xor))
        halves = key.bitcast(U16).rearrange("p (n e) -> p n e", e=2)
        nc.vector.tensor_scalar(k["hi"][0:rows, first:first + n], halves[:, :, 1], 0x8000, None, ALU.bitwise_xor)
        self.seq(nc.vector.tensor_copy(k["lo"][0:rows, first:first + n], halves[:, :, 0]))

    def bit(self, b):
        nc, k, g = self.nc, self.k, self.g
        half = k["hi"] if b < 16 else k["lo"]
        value = float(1 << (15 - b % 16))
        cand, cnt, want, ge, less = (k[n][:, 0:g] for n in ("cand", "cnt", "want", "ge", "less"))
        if b == 0:
            nc.vector.memset(cnt, 0.0)
            nc.vector.memset(want, float(TOPK))
        if b % 16 == 0:
            self.seq(nc.vector.memset(cand, value))
        for r, (rows, _, first, n, _) in enumerate(self.regions):
            last = nc.vector.tensor_scalar(k["junk"][0:rows, first:first + n], half[0:rows, first:first + n],
                                           k["cand"][0:rows, r:r + 1], 0.0, ALU.is_ge, ALU.add,
                                           accum_out=k["cnt"][0:rows, r:r + 1])
        counted = self.chain.did(last)
        step = value / 2 if b % 16 < 15 else value
        nc.vector.tensor_scalar(less, cand, -step, None, ALU.add)
        self.dve.wait_ge(self.chain.sem, counted)
        self.seq(nc.vector.tensor_tensor(ge, cnt, want, ALU.is_ge))
        out = cand if b % 16 < 15 else (k["thr"] if b < 16 else k["tlo"])[:, 0:g]
        self.seq(nc.vector.scalar_tensor_tensor(out, ge, value, less, ALU.mult, ALU.add))

    def narrow(self):
        nc, k, g = self.nc, self.k, self.g
        for r, (rows, _, first, n, _) in enumerate(self.regions):
            h, l, th = k["hi"][0:rows, first:first + n], k["lo"][0:rows, first:first + n], k["thr"][0:rows, r:r + 1]
            nc.vector.tensor_scalar(k["junk"][0:rows, first:first + n], h, th, 0.0, ALU.is_gt, ALU.add,
                                    accum_out=k["cnt"][0:rows, r:r + 1])
            self.seq(nc.vector.scalar_tensor_tensor(l, h, th, l, ALU.is_equal, ALU.mult))
        self.seq(nc.vector.tensor_tensor(k["want"][:, 0:g], k["want"][:, 0:g], k["cnt"][:, 0:g], ALU.subtract))

    def mark(self, r):
        nc, k, seq = self.nc, self.k, self.seq
        rows, _, first, n, out = self.regions[r]
        h, l = k["hi"][0:rows, first:first + n], k["lo"][0:rows, first:first + n]
        th, tl = k["thr"][0:rows, r:r + 1], k["tlo"][0:rows, r:r + 1]
        cnt, left = k["cnt"][0:rows, r:r + 1], k["ge"][0:rows, r:r + 1]
        s_, e_, m_, k_ = (k[name][0:rows, 0:n] for name in ("sel", "eq", "eh", "rank"))
        nc.vector.tensor_scalar(s_, h, th, None, ALU.is_gt)
        seq(nc.vector.tensor_scalar(m_, h, th, None, ALU.is_equal))
        nc.vector.scalar_tensor_tensor(e_, l, tl, m_, ALU.is_equal, ALU.mult)
        seq(nc.vector.scalar_tensor_tensor(s_, l, tl, s_, ALU.is_gt, ALU.add, accum_out=cnt))
        seq(nc.vector.tensor_tensor_scan(k_, k["one"][0:rows].broadcast_to([rows, n]), e_, 0.0, ALU.mult, ALU.add))
        seq(nc.vector.tensor_scalar(left, cnt, -1.0, float(TOPK), ALU.mult, ALU.add))
        seq(nc.vector.scalar_tensor_tensor(e_, k_, left, e_, ALU.is_le, ALU.mult))
        seq(nc.vector.tensor_tensor(s_, s_, e_, ALU.add))
        seq(nc.vector.tensor_scalar(out, s_, -1.0, -NEG, ALU.add, ALU.mult))


def key_search(nc, dve, chain, x, tiles):
    if tiles is None:
        return KeySearch(nc, dve, chain, x["find"], [(NS, x["ssc"][:], 0, KEYS, x["sbias"][:])])
    regions, at = [], 0
    for i in tiles:
        n = (i + 1) * P
        cols = slice(score_off(i), score_off(i) + n)
        regions.append((P, x["psc"][:, cols], at, n, x["pbias"][:, cols]))
        at += n
    return KeySearch(nc, dve, chain, x["find"], regions)


def search_buffers(nc, ctx):
    def sb(name, shape, dt=F32):
        return ctx.enter_context(nc.sbuf_tensor(name, shape, dt))

    W = max(KEYS, *(sum((i + 1) * P for i in tiles) for tiles in (EARLY, LATE)))
    k = {"hi": sb("hi", [P, W], U16), "lo": sb("lo", [P, W], U16), "junk": sb("junk", [P, W], BF16),
         "key": sb("key", [P, KEYS], I32), "one": sb("one", [P, 1]), "rank": sb("rank", [P, KEYS], U16)}
    k |= {n: sb(n, [P, KEYS], BF16) for n in ("sel", "eq", "eh")}
    k |= {n: sb(n, [P, 4]) for n in ("cand", "cnt", "want", "ge", "less", "thr", "tlo")}
    return k


def prompt_attention_phase(nc, cst, psum, t, x, att):
    scale = float(HD) ** -0.5
    steps = [(i, h) for i in range(TILES) for h in range(HEADS)]
    parts = [(n, c, min(c + 4, i + 1)) for n, (i, h) in enumerate(steps) for c in range(0, i + 1, 4)]
    first_part = [min(g for g, p in enumerate(parts) if p[0] == n) for n in range(len(steps))] + [len(parts)]
    with ExitStack() as ctx:
        def sb(name, shape, dt=F32):
            return ctx.enter_context(nc.sbuf_tensor(name, shape, dt))

        def sem(name):
            return new_sem(nc, name)

        sm = sb("sm", [P, 2, SEQ])
        pT = sb("pT", [P, 2, TILES, P])
        qz = sb("qz_att", [P, 2, 2, 2, 2, P])
        mx, nmx = sb("mx", [P, HEADS * TILES]), sb("nmx", [P, HEADS * TILES])
        rsum, rinv = sb("rsum", [P, HEADS * TILES]), sb("rinv", [P, HEADS * TILES])
        s_ps, sm_made, max_made, p_made = (sem(n) for n in ("s_ps", "sm_made", "max_made", "p_made"))
        pt_ps, pt_read, o_ps, inv_made, o_read = (sem(n) for n in ("pt_ps", "pt_read", "o_ps", "inv_made", "o_read"))
        q_put = sem("q_put_att")
        chain = Chain(sem("search_chain"))
        block = ctx.enter_context(nc.Block())

        @block.gpsimd
        def _(pool):
            nc.gpsimd.memset(qz[:], 0.0).then_inc(q_put, 1)

        def read_part(act, g):
            n, c0, c1 = parts[g]
            act.wait_ge(pt_ps, g + 1)
            if n >= 2:
                act.wait_ge(o_ps, n - 1)
            nc.scalar.copy(pT[:, n % 2, c0:c1], psum[:, 4 + g % 2, 0:(c1 - c0) * P].rearrange(
                "p (c q) -> p c q", q=P)).then_inc(pt_read, 1)

        @block.vector
        def _(dve):
            def largest(n):
                i, h = steps[n]
                w = (i + 1) * P
                dve.wait_ge(s_ps, n + 1)
                if n >= 2:
                    dve.wait_ge(pt_ps, first_part[n - 1])
                bank = 2 * (n % 2)
                nc.vector.tensor_tensor_reduce(
                    sm[:, n % 2, 0:w], psum[:, bank:bank + 2, :].rearrange("p a b -> p (a b)")[:, 0:w],
                    x["pbias"][:, score_off(i):score_off(i) + w], scale, -3e38, ALU.add, ALU.max,
                    mx[:, n:n + 1]).then_inc(sm_made, 1)
                dve.wait_ge(sm_made, n + 1)
                nc.vector.tensor_scalar(nmx[:, n:n + 1], mx[:, n:n + 1], -1.0, None, ALU.mult).then_inc(max_made, 1)

            def finish(i):
                cols = slice(i * HEADS, (i + 1) * HEADS)
                dve.wait_ge(p_made, (i + 1) * HEADS)
                nc.vector.reciprocal(rinv[:, cols], rsum[:, cols]).then_inc(inv_made, 1)
                dve.wait_ge(inv_made, i + 1)
                dve.wait_ge(o_ps, (i + 1) * HEADS)
                nc.vector.tensor_tensor(att[:, i].rearrange("p (h d) -> p h d", h=HEADS),
                                        psum[:, 6 + i % 2, :].rearrange("p (h d) -> p h d", h=HEADS),
                                        rinv[:, cols].unsqueeze(2).broadcast_to([P, HEADS, HD]), ALU.mult
                                        ).then_inc(o_read, 1)

            late, sample = key_search(nc, dve, chain, x, LATE), key_search(nc, dve, chain, x, None)
            FIRST = len(LATE)
            MARK = FIRST + 32
            S_FIRST, S_MARK = MARK + len(LATE) + 1, len(steps) - 3

            def search(n):
                if n < FIRST:
                    late.prepare(n)
                elif n < FIRST + 32:
                    late.bit(n - FIRST)
                    if n - FIRST == 15:
                        late.narrow()
                elif MARK <= n < MARK + len(LATE):
                    late.mark(n - MARK)
                if n == S_FIRST - 1:
                    sample.prepare(0)
                if n >= S_FIRST:
                    for b in range((n - S_FIRST) * 3 // 2, min((n - S_FIRST + 1) * 3 // 2, 32)):
                        sample.bit(b)
                        if b == 15:
                            sample.narrow()
                if n == S_MARK:
                    sample.mark(0)

            largest(0)
            for n in range(len(steps)):
                if n + 1 < len(steps):
                    largest(n + 1)
                search(n)
                if n % HEADS == 1 and n > HEADS:
                    finish(n // HEADS - 1)
            finish(TILES - 1)

        @block.scalar
        def _(act):
            def exps(n):
                w = (steps[n][0] + 1) * P
                act.wait_ge(max_made, n + 1)
                nc.scalar.activation(sm[:, n % 2, 0:w], sm[:, n % 2, 0:w], ACT.Exp, bias=nmx[:, n:n + 1],
                                     accum_out=rsum[:, n:n + 1]).then_inc(p_made, 1)

            def put_queries(i):
                if i >= 2:
                    act.wait_ge(s_ps, (i - 1) * HEADS)
                for half in range(2):
                    rows = slice(64 * half, 64 * half + 64)
                    nc.scalar.copy(qz[rows, i % 2, :, half],
                                   t["qT"][rows, :, i * P:(i + 1) * P].rearrange("p (m a) q -> p m a q", m=2)
                                   ).then_inc(q_put, 1)

            act.wait_ge(q_put, 1)
            put_queries(0)
            put_queries(1)
            exps(0)
            for n in range(len(steps)):
                if n + 1 < len(steps):
                    exps(n + 1)
                if n % HEADS == 0 and HEADS <= n < (TILES - 1) * HEADS:
                    put_queries(n // HEADS + 1)
                for g in range(first_part[n], first_part[n + 1]):
                    read_part(act, g)

        @block.tensor
        def _(pe):
            def scores(n):
                i, h = steps[n]
                m, half, which = h // 4, h // 2 % 2, h % 2
                pe.wait_ge(q_put, 1 + 2 * (i + 1))
                if n >= 2:
                    pe.wait_ge(sm_made, n - 1)
                for c in range(0, (i + 1) * P, 512):
                    w = min(512, (i + 1) * P - c)
                    mm = pe.matmul(psum[:, 2 * (n % 2) + c // 512, 0:w], qz[:, i % 2, m, half, which],
                                   t["kT"][:, m, c:c + w], start=True, stop=True)
                mm.then_inc(s_ps, 1)

            def transposes(n):
                pe.wait_ge(p_made, n + 1)
                for g in range(first_part[n], first_part[n + 1]):
                    _, c0, c1 = parts[g]
                    if g >= 2:
                        pe.wait_ge(pt_read, g - 1)
                    for c in range(c0, c1):
                        mm = pe.transpose(psum[:, 4 + g % 2, (c - c0) * P:(c - c0 + 1) * P],
                                          sm[:, n % 2, c * P:(c + 1) * P], cst["ident"][:])
                    mm.then_inc(pt_ps, 1)

            def values(n):
                i, h = steps[n]
                pe.wait_ge(pt_read, first_part[n + 1])
                if h == 0 and i >= 2:
                    pe.wait_ge(o_read, i - 1)
                for c in range(i + 1):
                    mm = pe.matmul(psum[:, 6 + i % 2, h * HD:(h + 1) * HD], pT[:, n % 2, c],
                                   t["v"][:, c, (h // 2) * HD:(h // 2 + 1) * HD], start=(c == 0), stop=(c == i))
                mm.then_inc(o_ps, 1)

            scores(0)
            for n in range(len(steps)):
                if n + 1 < len(steps):
                    scores(n + 1)
                transposes(n)
                if n >= 1:
                    values(n - 1)
            values(len(steps) - 1)


def sample_attention_phase(nc, cst, psum, a, scr, t, x):
    scale = float(HD) ** -0.5
    HT = HEADS * NT
    BANKS = (5, 6, 0, 1)
    groups = []

    def add_k(b):
        groups.extend(("k", b, j) for j in range(PAGES // 2))

    add_k(0)
    for b in range(NB):
        if b + 1 < NB:
            add_k(b + 1)
        groups.extend(("p", b, j) for j in range(3))
    num = {g: n for n, g in enumerate(groups)}

    with ExitStack() as ctx:
        def sb(name, shape, dt=F32):
            return ctx.enter_context(nc.sbuf_tensor(name, shape, dt))

        def sem(name):
            return new_sem(nc, name)

        kc = sb("kc", [P, 2, PAGES, KVH * HD])
        vc = sb("vc", [P, 2, PAGES, KVH * HD])
        kcT = sb("kcT", [P, 2, PAGES, P])
        qbd = sb("qbd", [P, 2, NB, HT])
        rep = sb("rep", [NS, NB, HEADS, NT], BF16)
        pr = sb("pr", [HT, KEYS])
        prT = sb("prT", [P, PAGES + 1, HT])
        vn = sb("vn", [NT, NB, KVH * HD])
        own = sb("own", [HT, KVH])
        oe = sb("oe", [HT, KVH, HD])
        os_ = sb("os_sb", [HT, 2, HD])
        m2, m1, s2, s1 = sb("m2", [HT, 2]), sb("m1", [HT, 1]), sb("s2", [HT, 2]), sb("s1", [HT, 1])
        k_land = [sem(f"kc_land{i}") for i in range(2)]
        v_land = [sem(f"vc_land{i}") for i in range(2)]
        vn_land, setup, own_made = sem("vn_land"), sem("setup"), sem("own_made")
        s_ps, m_made, p_made, sum_made = (sem(n) for n in ("ss_ps", "sm2_made", "sp_made", "ssum_made"))
        tr_ps, tr_dve, tr_act, o_ps, o_read, o_made = (sem(n) for n in ("tr_ps", "tr_dve", "tr_act", "so_ps",
                                                                        "so_read", "so_made"))
        o_out = [sem(f"so_out{i}") for i in range(2)]
        chain = Chain(sem("sample_chain"))
        block = ctx.enter_context(nc.Block())

        @block.gpsimd
        def _(pool):
            nc.gpsimd.memset(own[:], 1.0).then_inc(own_made, 1)
            pool.wait_ge(own_made, 1)
            nc.gpsimd.affine_select(out=own[:], in_=own[:], pattern=[[-2 * NT, KVH]], compare_op=ALU.is_ge,
                                    fill=0.0, base=0, channel_multiplier=1).then_inc(own_made, 1)
            pool.wait_ge(own_made, 2)
            nc.gpsimd.affine_select(out=own[:], in_=own[:], pattern=[[2 * NT, KVH]], compare_op=ALU.is_ge,
                                    fill=0.0, base=2 * NT - 1, channel_multiplier=-1).then_inc(own_made, 1)
            for b in range(NB):
                if b >= 2:
                    pool.wait_ge(tr_ps, num[("k", b - 2, 7)] + 1)
                for dst, src, land in ((kc, "cache_k", k_land), (vc, "cache_v", v_land)):
                    if b >= 2 and src == "cache_v":
                        pool.wait_ge(o_ps, b - 1)
                    nc.gpsimd.indirect_dma_start(
                        out=dst[:, b % 2].rearrange("p k d -> p (k d)"), out_offset=None,
                        in_=a[src][0].rearrange("n (r k) h d -> (n r) (k h d)", r=8),
                        in_offset=bass.IndirectOffsetOnAxis(ap=x["gidx"][:, b:b + 1], axis=0)
                    ).then_inc(land[b % 2], 16)

        @block.sync
        def _(sp):
            for b in range(NB):
                sp.dma_start(vn[:, b], t["v"][b * NT:(b + 1) * NT, TILES]).then_inc(vn_land, 16)
            for b in range(NB):
                sp.wait_ge(o_made, b + 1)
                for h in range(HEADS):
                    sp.dma_start(scr["os"][b * NT:(b + 1) * NT, h * HD:(h + 1) * HD],
                                 os_[h * NT:(h + 1) * NT, b % 2]).then_inc(o_out[b % 2], 16)
            for i in range(2):
                sp.wait_ge(o_out[i], 16 * HEADS * NB // 2)

        def read_group(eng, copy, g, done):
            kind, b, j = groups[g]
            eng.wait_ge(tr_ps, g + 1)
            bank = psum[:, BANKS[g % 4], :]
            if kind == "k":
                if b >= 1:
                    eng.wait_ge(s_ps, b)
                copy(kcT[:, :, 2 * j:2 * j + 2].rearrange("p m k q -> p k m q"),
                     bank.rearrange("p (k m q) -> p k m q", k=2, m=2)).then_inc(done, 1)
            else:
                if b >= 1:
                    eng.wait_ge(o_ps, b)
                if j < 2:
                    copy(prT[:, 8 * j:8 * j + 8], bank.rearrange("p (k r) -> p k r", k=8)).then_inc(done, 1)
                else:
                    copy(prT[0:NT, PAGES], bank[0:NT, 0:HT]).then_inc(done, 1)

        def groups_of(b):
            lo = num[("k", b + 1, 0)] if b + 1 < NB else num[("p", b, 0)]
            return range(lo, num[("p", b, 2)] + 1)

        @block.vector
        def _(dve):
            def seq(ins):
                dve.wait_ge(chain.sem, chain.did(ins))

            seq(nc.vector.memset(qbd[:], 0.0))
            for m in range(2):
                for half in range(2):
                    for c in range(2):
                        h = 4 * m + 2 * half + c
                        rows = slice(64 * half, 64 * half + 64)
                        nc.vector.tensor_copy(
                            qbd[rows, m, :, h * NT:(h + 1) * NT],
                            t["qT"][rows, 2 * m + c, SEQ:TOK].rearrange("p (b t) -> p b t", b=NB))
            nc.vector.tensor_copy(rep[:], cst["ident"][0:NS, 0:NS].rearrange("r (b t) -> r b t", b=NB)
                                  .unsqueeze(2).broadcast_to([NS, NB, HEADS, NT])).then_inc(setup, 1)
            for g in range(0, 8, 2):
                read_group(dve, nc.vector.tensor_copy, g, tr_dve)
            dve.wait_ge(own_made, 3)
            for b in range(NB + 1):
                if b >= 1:
                    if b >= 2:
                        dve.wait_ge(o_made, b - 1)
                    dve.wait_ge(p_made, b)
                    seq(nc.vector.tensor_reduce(s1[:], s2[:], AX, ALU.add))
                    nc.vector.reciprocal(s1[:], s1[:]).then_inc(sum_made, 1)
                if b < NB:
                    dve.wait_ge(s_ps, b + 1)
                    nc.vector.tensor_reduce(m2[:, 0:1], psum[0:HT, 0:4, :].rearrange("p a b -> p (a b)"), AX, ALU.max)
                    seq(nc.vector.tensor_reduce(m2[:, 1:2], psum[0:HT, 4, 0:NT], AX, ALU.max))
                    seq(nc.vector.tensor_reduce(m1[:], m2[:], AX, ALU.max))
                    nc.vector.tensor_scalar(m1[:], m1[:], -scale, None, ALU.mult).then_inc(m_made, 1)
                if b >= 1:
                    j = b - 1
                    dve.wait_ge(sum_made, b)
                    dve.wait_ge(o_ps, b)
                    nc.vector.tensor_tensor(oe[:], psum[0:HT, 7, 0:KVH * HD].rearrange("p (k d) -> p k d", k=KVH),
                                            own[:].unsqueeze(2).broadcast_to([HT, KVH, HD]), ALU.mult
                                            ).then_inc(o_read, 1)
                    dve.wait_ge(o_read, b)
                    if j >= 2:
                        dve.wait_ge(o_out[j % 2], 16 * HEADS * (j // 2))
                    seq(nc.vector.tensor_reduce(os_[:, j % 2], oe[:].rearrange("p k d -> p d k"), AX, ALU.add))
                    nc.vector.tensor_scalar(os_[:, j % 2], os_[:, j % 2], s1[:], None, ALU.mult).then_inc(o_made, 1)
                if b < NB:
                    for g in groups_of(b):
                        if g % 2 == 0:
                            read_group(dve, nc.vector.tensor_copy, g, tr_dve)

        @block.scalar
        def _(act):
            for g in range(1, 8, 2):
                read_group(act, nc.scalar.copy, g, tr_act)
            for b in range(NB):
                act.wait_ge(m_made, b + 1)
                if b >= 1:
                    act.wait_ge(tr_ps, num[("p", b - 1, 2)] + 1)
                    act.wait_ge(sum_made, b)
                nc.scalar.activation(pr[:, 0:PAST], psum[0:HT, 0:4, :].rearrange("p a b -> p (a b)"), ACT.Exp,
                                     bias=m1[:], scale=scale, accum_out=s2[:, 0:1])
                nc.scalar.activation(pr[:, PAST:], psum[0:HT, 4, 0:NT], ACT.Exp,
                                     bias=m1[:], scale=scale, accum_out=s2[:, 1:2]).then_inc(p_made, 1)
                for g in groups_of(b):
                    if g % 2 == 1:
                        read_group(act, nc.scalar.copy, g, tr_act)

        @block.tensor
        def _(pe):
            def transposes(g):
                kind, b, j = groups[g]
                if g >= 4:
                    pe.wait_ge(tr_dve if g % 2 == 0 else tr_act, g // 2 - 1)
                if kind == "k":
                    if j == 0:
                        pe.wait_ge(k_land[b % 2], 16 * (b // 2 + 1))
                    for k in range(2):
                        for m in range(2):
                            mm = pe.transpose(psum[:, BANKS[g % 4], (2 * k + m) * P:(2 * k + m + 1) * P],
                                              kc[:, b % 2, 2 * j + k, m * P:(m + 1) * P], cst["ident"][:])
                else:
                    pe.wait_ge(p_made, b + 1)
                    if j < 2:
                        for k in range(8):
                            mm = pe.transpose(psum[:, BANKS[g % 4], k * HT:(k + 1) * HT],
                                              pr[:, (8 * j + k) * P:(8 * j + k + 1) * P], cst["ident"][0:HT, 0:HT])
                    else:
                        mm = pe.transpose(psum[0:NT, BANKS[g % 4], 0:HT], pr[:, PAST:], cst["ident"][0:HT, 0:HT])
                mm.then_inc(tr_ps, 1)

            def all_read(g):
                pe.wait_ge(tr_dve, g // 2 + 1)
                pe.wait_ge(tr_act, (g + 1) // 2)

            def values(b):
                all_read(num[("p", b, 2)])
                pe.wait_ge(v_land[b % 2], 16 * (b // 2 + 1))
                if b >= 1:
                    pe.wait_ge(o_read, b)
                for k in range(PAGES + 1):
                    lhs, rhs = (prT[:, k], vc[:, b % 2, k]) if k < PAGES else (prT[0:NT, k], vn[:, b])
                    mm = pe.matmul(psum[0:HT, 7, 0:KVH * HD], lhs, rhs, start=(k == 0), stop=(k == PAGES))
                mm.then_inc(o_ps, 1)

            for g in range(8):
                transposes(g)
            pe.wait_ge(setup, 1)
            pe.wait_ge(vn_land, 16 * NB)
            for b in range(NB):
                all_read(num[("p", b - 1, 2)] if b >= 1 else num[("k", 0, 7)])
                if b >= 1:
                    pe.wait_ge(p_made, b)
                bias = x["sbias"][:, 0:PAST].rearrange("r (p k) -> r k p", k=PAGES)
                for c in range(5):
                    w = 512 if c < 4 else NT
                    pe.matmul(psum[0:HT, c, 0:w], rep[:, b].rearrange("r h t -> r (h t)"),
                              bias[:, 4 * c:4 * c + 4] if c < 4 else x["sbias"][:, PAST:], start=True, stop=False)
                    for m in range(2):
                        rhs = kcT[:, m, 4 * c:4 * c + 4].rearrange("p k q -> p (k q)") if c < 4 else \
                            t["kT"][:, m, SEQ + b * NT:SEQ + (b + 1) * NT]
                        mm = pe.matmul(psum[0:HT, c, 0:w], qbd[:, m, b], rhs, start=False, stop=(m == 1))
                mm.then_inc(s_ps, 1)
                if b >= 1:
                    values(b - 1)
                pe.wait_ge(p_made, b + 1)
                for g in groups_of(b):
                    transposes(g)
            values(NB - 1)


def load_rows(sp, dst, scr_mod, part, samples, land):
    if samples:
        for b in range(NB):
            sp.dma_start(dst[b * NT:(b + 1) * NT], scr_mod[1 + b, part:part + D].partition_broadcast(NT)
                         ).then_inc(land, 16)
    else:
        sp.dma_start(dst, scr_mod[0, part:part + D].partition_broadcast(P)).then_inc(land, 16)


def out_buffers(nc, ctx):
    def sb(name, shape):
        return ctx.enter_context(nc.sbuf_tensor(name, shape, F32, side="right"))

    w = {"wo": sb("wo", [P, KD, D]), "wr": sb("wr", [P, KD, EXPERTS]), "lg": sb("lg", [P, D]), "lb": sb("lb", [P, D])}
    w |= {n: sb(n, [P, 2, D]) for n in ("g1", "sc2", "sh2")}
    w |= {n: new_sem(nc, n) for n in ("wo_land", "mod_land")}
    return w


def load_out(sp, a, scr, w):
    for half in range(2):
        sp.dma_start(w["wo"][:, 4 * half:4 * half + 4],
                     a["w_out"][0, half * D_SSM:(half + 1) * D_SSM].rearrange("(p k) n -> p k n", k=4)
                     ).then_inc(w["wo_land"], 16)
    for s in range(2):
        for dst, part in (("g1", G1), ("sc2", SC2), ("sh2", SH2)):
            load_rows(sp, w[dst][:, s], scr["mod"], part, s, w["mod_land"])
    sp.dma_start(w["lg"][:], a["ln1_g"][0].partition_broadcast(P)).then_inc(w["mod_land"], 16)
    sp.dma_start(w["lb"][:], a["ln1_b"][0].partition_broadcast(P)).then_inc(w["mod_land"], 16)
    sp.dma_start(w["wr"][:], a["w_router"][0].rearrange("(p k) e -> p k e", k=KD)).then_inc(w["mod_land"], 16)


def mix_phase(nc, cst, psum, a, scr, t, att, mixT, w_next):
    NTL = TILES + 1
    KH = D_SSM // P
    with ExitStack() as ctx:
        def sb(name, shape, dt=F32):
            return ctx.enter_context(nc.sbuf_tensor(name, shape, dt))

        def sem(name):
            return new_sem(nc, name)

        yss = sb("yss", [NS, D_SSM])
        wg = sb("wg", [P, KH, D_SSM])
        bg = sb("bg", [P, D_SSM])
        gcol = sb("gcol", [P, 2, KH])
        gT = sb("gT", [P, 2, KH, P])
        zb = sb("zb", [P, 2, D_SSM])
        sq = sb("sq", [P, D_SSM])
        ss = sb("ss", [P, 2, NTL])
        rstd = sb("rstd", [P, 2, NTL])
        ys_land, os_land, wg_land = sem("ys_land"), sem("os_land"), sem("wg_land")
        ss_clear, gelu, gT_ps, gT_made, z_ps, z_made, sig, glu, sums, root, inv = (sem(n) for n in (
            "ss_clear", "gelu", "gT_ps", "gT_made", "z_ps", "z_made", "sig", "glu", "sums", "root", "inv"))
        scaled, m_ps, m_dve, m_act = (sem(n) for n in ("scaled", "m_ps", "m_dve", "m_act"))
        sq_done = sem("sq_done")
        block = ctx.enter_context(nc.Block())
        y = t["u"][:].rearrange("p g s j -> p (g s j)").rearrange("p (t x) -> p t x", t=LC)

        def ssm_rows(i):
            return y[:, i] if i < TILES else yss[:]

        def att_rows(i):
            return att[:, i] if i < TILES else att[0:NS, TILES]

        def rows_of(i):
            return P if i < TILES else NS

        def sum_squares(act, i):
            r = rows_of(i)
            act.wait_ge(glu, i + 1)
            act.wait_ge(sq_done, NTL + i)
            nc.scalar.activation(sq[0:r], ssm_rows(i), ACT.Square, accum_out=ss[0:r, 0, i:i + 1]
                                 ).then_inc(sq_done, 1)

        def transposed(g, eng):
            i, half = divmod(g, 2)
            r = rows_of(i)
            for k in range(KH):
                if i == TILES:
                    out = mixT[:, KH * half + k, SEQ:TOK]
                elif half == 0:
                    out = mixT[:, k, i:SEQ:LC]
                else:
                    out = mixT[:, KH + k, i * P:(i + 1) * P]
                src = psum[:, 4 + g % 4, k * P:k * P + r]
                if g % 2 == 0:
                    ins = nc.vector.tensor_scalar(out, src, gcol[:, half, k:k + 1], None, ALU.mult)
                else:
                    ins = nc.scalar.activation(out, src, ACT.Copy, scale=gcol[:, half, k:k + 1])
            ins.then_inc(m_dve if g % 2 == 0 else m_act, 1)

        @block.sync
        def _(sp):
            sp.dma_start(yss[:], scr["ys"]).then_inc(ys_land, 16)
            sp.dma_start(att[0:NS, TILES], scr["os"]).then_inc(os_land, 16)
            sp.dma_start(wg[:], a["w_glu"][0].rearrange("(p k) n -> p k n", k=KH)).then_inc(wg_land, 16)
            sp.dma_start(bg[:], a["b_glu"][0].partition_broadcast(P)).then_inc(wg_land, 16)
            sp.dma_start(gcol[:, 0], a["g_ssm_out"][0].rearrange("(p k) -> p k", k=KH)).then_inc(wg_land, 16)
            sp.dma_start(gcol[:, 1], a["g_att_out"][0].rearrange("(p k) -> p k", k=KH)).then_inc(wg_land, 16)
            load_out(sp, a, scr, w_next)

        @block.scalar
        def _(act):
            act.wait_ge(ys_land, 16)
            for i in range(NTL):
                nc.scalar.activation(ssm_rows(i), ssm_rows(i), ACT.Gelu_apprx_tanh).then_inc(gelu, 1)
            act.wait_ge(os_land, 16)
            act.wait_ge(ss_clear, 1)
            for i in range(NTL):
                r = rows_of(i)
                if i:
                    act.wait_ge(sq_done, i)
                nc.scalar.activation(sq[0:r], att_rows(i), ACT.Square, accum_out=ss[0:r, 1, i:i + 1]
                                     ).then_inc(sq_done, 1)
            for i in range(NTL):
                r = rows_of(i)
                act.wait_ge(z_made, i + 1)
                nc.scalar.activation(zb[0:r, i % 2], zb[0:r, i % 2], ACT.Sigmoid).then_inc(sig, 1)
                if i >= 1:
                    sum_squares(act, i - 1)
            sum_squares(act, NTL - 1)
            act.wait_ge(sums, 1)
            nc.scalar.activation(rstd[:], ss[:], ACT.Sqrt).then_inc(root, 1)
            for g in range(1, 2 * NTL, 2):
                act.wait_ge(m_ps, g + 1)
                transposed(g, act)

        @block.vector
        def _(dve):
            nc.vector.memset(ss[:], 1.0).then_inc(ss_clear, 1)
            dve.wait_ge(wg_land, 64)
            for i in range(NTL + 1):
                if i < NTL:
                    r = rows_of(i)
                    dve.wait_ge(gT_ps, i + 1)
                    if i >= 2:
                        dve.wait_ge(z_ps, i - 1)
                    nc.vector.tensor_copy(gT[:, i % 2, :, 0:r], psum[:, i % 2, :].rearrange(
                        "p (k q) -> p k q", k=KH)[:, :, 0:r]).then_inc(gT_made, 1)
                if i >= 1:
                    j, r = i - 1, rows_of(i - 1)
                    dve.wait_ge(z_ps, j + 1)
                    if j >= 2:
                        dve.wait_ge(glu, j - 1)
                    nc.vector.tensor_tensor(zb[0:r, j % 2], psum[0:r, 2 + j % 2, :], bg[0:r], ALU.add
                                            ).then_inc(z_made, 1)
                    dve.wait_ge(sig, j + 1)
                    nc.vector.tensor_tensor(ssm_rows(j), ssm_rows(j), zb[0:r, j % 2], ALU.mult).then_inc(glu, 1)
            dve.wait_ge(sq_done, 2 * NTL)
            nc.vector.tensor_scalar(ss[:], ss[:], 1.0 / D_SSM, EPS, ALU.mult, ALU.add).then_inc(sums, 1)
            dve.wait_ge(root, 1)
            nc.vector.reciprocal(rstd[:], rstd[:]).then_inc(inv, 1)
            dve.wait_ge(inv, 1)
            for i in range(NTL):
                r = rows_of(i)
                nc.vector.tensor_scalar(ssm_rows(i), ssm_rows(i), rstd[0:r, 0, i:i + 1], None, ALU.mult
                                        ).then_inc(scaled, 1)
                nc.vector.tensor_scalar(att_rows(i), att_rows(i), rstd[0:r, 1, i:i + 1], None, ALU.mult
                                        ).then_inc(scaled, 1)
            for g in range(0, 2 * NTL, 2):
                dve.wait_ge(m_ps, g + 1)
                transposed(g, dve)

        @block.tensor
        def _(pe):
            ident = cst["ident"]
            for i in range(NTL + 1):
                if i < NTL:
                    r = rows_of(i)
                    pe.wait_ge(gelu, i + 1)
                    if i >= 2:
                        pe.wait_ge(gT_made, i - 1)
                    for k in range(KH):
                        mm = pe.transpose(psum[:, i % 2, k * P:k * P + r], ssm_rows(i)[:, k:D_SSM:KH],
                                          ident[0:r, 0:r])
                    mm.then_inc(gT_ps, 1)
                if i >= 1:
                    j, r = i - 1, rows_of(i - 1)
                    pe.wait_ge(gT_made, j + 1)
                    pe.wait_ge(wg_land, 64)
                    if j >= 2:
                        pe.wait_ge(z_made, j - 1)
                    for k in range(KH):
                        mm = pe.matmul(psum[0:r, 2 + j % 2, :], gT[:, j % 2, k, 0:r], wg[:, k],
                                       start=(k == 0), stop=(k == KH - 1))
                    mm.then_inc(z_ps, 1)
            for g in range(2 * NTL):
                i, half = divmod(g, 2)
                r = rows_of(i)
                pe.wait_ge(scaled, g + 1)
                if g >= 4:
                    pe.wait_ge(m_dve if g % 2 == 0 else m_act, (g - 4) // 2 + 1)
                src = ssm_rows(i) if half == 0 else att_rows(i)
                for k in range(KH):
                    mm = pe.transpose(psum[:, 4 + g % 4, k * P:k * P + r], src[:, k:D_SSM:KH], ident[0:r, 0:r])
                mm.then_inc(m_ps, 1)


def out_phase(nc, cst, psum, a, scr, mixT, aff, w, w_next):
    NTL = TILES + 1
    with ExitStack() as ctx:
        def sb(name, shape, dt=F32):
            return ctx.enter_context(nc.sbuf_tensor(name, shape, dt))

        def sem(name):
            return new_sem(nc, name)

        wo, wr, g1, sc2, sh2, lg, lb, wo_land, mod_land = (w[n] for n in (
            "wo", "wr", "g1", "sc2", "sh2", "lg", "lb", "wo_land", "mod_land"))
        xt = sb("xt2", [P, 2, D])
        xr = sb("xr", [P, 2, D])
        x1 = sb("x1", [P, 2, D])
        h2 = sb("h2", [P, 2, D])
        sq = sb("sq2", [P, D])
        zero = sb("zero", [P, D])
        st = sb("st", [P, NTL, 4])
        zero_made = sem("zero_made")
        x_land = [sem(f"x2_land{i}") for i in range(2)]
        mixed_ps, mixed_read, x_made, sq_made, root, xhat, x1_made, h2_made = (sem(n) for n in (
            "mixed_ps", "mixed_read", "x_made", "sq_made", "root2", "xhat", "x1_made", "h2_made"))
        st_clear = sem("st_clear")
        hT_ps, hT_act, aff_ps, aff_made = (sem(n) for n in ("hT_ps", "hT_act", "aff_ps", "aff_made"))
        x1_out = [sem(f"x1_out{i}") for i in range(2)]
        h2_out = [sem(f"h2_out{i}") for i in range(2)]
        z_out, shared_land = sem("z_out"), sem("shared_land")
        chain = Chain(sem("out_chain"))
        block = ctx.enter_context(nc.Block())

        def rows_of(i):
            return P if i < TILES else NS

        def cols_of(i):
            return slice(i, SEQ, LC) if i < TILES else slice(SEQ, TOK)

        def scores(dve, i):
            r = rows_of(i)
            dve.wait_ge(aff_ps, i + 1)
            nc.vector.tensor_copy(aff[0:r, i], psum[0:r, 6 + i % 2, 0:EXPERTS]).then_inc(aff_made, 1)

        @block.sync
        def _(sp):
            for i in range(NTL):
                r = rows_of(i)
                if i >= 2:
                    sp.wait_ge(x_made, i - 1)
                src = a["x_prompt"][0].rearrange("(c s) d -> s c d", s=LC)[i] if i < TILES else \
                    a["x_sample"].rearrange("b t d -> (b t) d")
                sp.dma_start(xt[0:r, i % 2], src).then_inc(x_land[i % 2], 16)
            load_shared(sp, a, w_next, shared_land)
            sp.wait_ge(zero_made, 1)
            for name in ("h2", "acc"):
                sp.dma_start(scr[name][SEQ + NS:TRASH], zero[0:NS]).then_inc(z_out, 16)
                sp.dma_start(scr[name][TRASH:], zero[:]).then_inc(z_out, 16)
            sp.wait_ge(z_out, 64)
            sp.wait_ge(shared_land, 64)

        @block.gpsimd
        def _(pool):
            nc.gpsimd.memset(zero[:], 0.0).then_inc(zero_made, 1)
            pool.wait_ge(mod_land, 16 * (3 * (1 + NB) + 3))
            for i in range(NTL):
                r = rows_of(i)
                pool.wait_ge(xhat, i + 1)
                if i >= 2:
                    pool.wait_ge(x1_out[i % 2], 16 * (i // 2))
                nc.gpsimd.tensor_tensor(x1[0:r, i % 2], xr[0:r, i % 2], lg[0:r], ALU.mult).then_inc(x1_made, 1)
                pool.wait_ge(x1_made, 2 * i + 1)
                nc.gpsimd.tensor_tensor(x1[0:r, i % 2], x1[0:r, i % 2], lb[0:r], ALU.add).then_inc(x1_made, 1)
                pool.wait_ge(x1_made, 2 * i + 2)
                pool.dma_start(scr["x1"][i * P:i * P + r], x1[0:r, i % 2]).then_inc(x1_out[i % 2], 16)
                pool.wait_ge(h2_made, i + 1)
                pool.dma_start(scr["h2"][i * P:i * P + r], h2[0:r, i % 2]).then_inc(h2_out[i % 2], 16)
            pool.wait_ge(x1_out[0], 16 * 5)
            pool.wait_ge(x1_out[1], 16 * 4)
            pool.wait_ge(h2_out[0], 16 * 5)
            pool.wait_ge(h2_out[1], 16 * 4)

        @block.scalar
        def _(act):
            for i in range(NTL + 1):
                if i >= 1:
                    j = i - 1
                    r = rows_of(j)
                    for q in range(2):
                        act.wait_ge(hT_ps, 2 * j + q + 1)
                        nc.scalar.copy(mixT[:, 4 * q:4 * q + 4, cols_of(j)],
                                       psum[:, 4 + q, :].rearrange("p (k c) -> p k c", k=4)[:, :, 0:r]
                                       ).then_inc(hT_act, 1)
                if i < NTL:
                    r = rows_of(i)
                    act.wait_ge(x_made, i + 1)
                    nc.scalar.activation(st[0:r, i, 1:2], st[0:r, i, 0:1], ACT.Copy, scale=-1.0 / D
                                         ).then_inc(sq_made, 1)
                    act.wait_ge(sq_made, 2 * i + 1)
                    nc.scalar.activation(sq[0:r], xr[0:r, i % 2], ACT.Square, bias=st[0:r, i, 1:2],
                                         accum_out=st[0:r, i, 2:3]).then_inc(sq_made, 1)
                    act.wait_ge(st_clear, i + 1)
                    nc.scalar.activation(st[0:r, i, 3:4], st[0:r, i, 2:3], ACT.Sqrt).then_inc(root, 1)

        @block.vector
        def _(dve):
            def seq(ins):
                dve.wait_ge(chain.sem, chain.did(ins))

            dve.wait_ge(mod_land, 16 * (3 * (1 + NB) + 3))
            for s, r in ((0, P), (1, NS)):
                seq(nc.vector.tensor_scalar(sc2[0:r, s], sc2[0:r, s], 1.0, None, ALU.add))
                seq(nc.vector.tensor_tensor(h2[0:r, s], sc2[0:r, s], lb[0:r], ALU.mult))
                nc.vector.tensor_tensor(sh2[0:r, s], sh2[0:r, s], h2[0:r, s], ALU.add)
                seq(nc.vector.tensor_tensor(sc2[0:r, s], sc2[0:r, s], lg[0:r], ALU.mult))
            for i in range(NTL):
                r, s = rows_of(i), i // TILES
                xri = xr[0:r, i % 2]
                dve.wait_ge(mixed_ps, i + 1)
                if i >= 2:
                    dve.wait_ge(x1_made, 2 * (i - 1))
                nc.vector.tensor_tensor(xri, psum[0:r, 2 * (i % 2):2 * (i % 2) + 2, :].rearrange("p a b -> p (a b)"),
                                        g1[0:r, s], ALU.mult).then_inc(mixed_read, 1)
                dve.wait_ge(mixed_read, i + 1)
                dve.wait_ge(x_land[i % 2], 16 * (i // 2 + 1))
                nc.vector.scalar_tensor_tensor(xri, xt[0:r, i % 2], ALPHA, xri, ALU.mult, ALU.add,
                                               accum_out=st[0:r, i, 0:1]).then_inc(x_made, 1)
                if i >= 1:
                    scores(dve, i - 1)
                dve.wait_ge(sq_made, 2 * i + 2)
                nc.vector.tensor_scalar(st[0:r, i, 2:3], st[0:r, i, 2:3], 1.0 / D, EPS, ALU.mult, ALU.add
                                        ).then_inc(st_clear, 1)
                dve.wait_ge(root, i + 1)
                seq(nc.vector.reciprocal(st[0:r, i, 3:4], st[0:r, i, 3:4]))
                nc.vector.tensor_scalar(xri, xri, st[0:r, i, 1:2], st[0:r, i, 3:4], ALU.add, ALU.mult
                                        ).then_inc(xhat, 1)
                dve.wait_ge(xhat, i + 1)
                if i >= 2:
                    dve.wait_ge(h2_out[i % 2], 16 * (i // 2))
                    dve.wait_ge(hT_ps, 2 * (i - 1))
                seq(nc.vector.tensor_tensor(h2[0:r, i % 2], xri, sc2[0:r, s], ALU.mult))
                nc.vector.tensor_tensor(h2[0:r, i % 2], h2[0:r, i % 2], sh2[0:r, s], ALU.add).then_inc(h2_made, 1)
            scores(dve, NTL - 1)

        @block.tensor
        def _(pe):
            def mixed(i):
                r = rows_of(i)
                if i >= 2:
                    pe.wait_ge(mixed_read, i - 1)
                for n in range(2):
                    for k in range(KD):
                        mm = pe.matmul(psum[0:r, 2 * (i % 2) + n, :], mixT[:, k, cols_of(i)],
                                       wo[:, k, n * 512:(n + 1) * 512], start=(k == 0), stop=(k == KD - 1))
                mm.then_inc(mixed_ps, 1)

            pe.wait_ge(wo_land, 32)
            pe.wait_ge(mod_land, 16 * (3 * (1 + NB) + 3))
            mixed(0)
            for i in range(NTL):
                r = rows_of(i)
                if i + 1 < NTL:
                    mixed(i + 1)
                pe.wait_ge(h2_made, i + 1)
                for q in range(2):
                    if i >= 1:
                        pe.wait_ge(hT_act, 2 * (i - 1) + q + 1)
                    for k in range(4):
                        mm = pe.transpose(psum[:, 4 + q, k * P:k * P + r], h2[0:r, i % 2, 4 * q + k:D:KD],
                                          cst["ident"][0:r, 0:r])
                    mm.then_inc(hT_ps, 1)
                pe.wait_ge(hT_act, 2 * i + 2)
                if i >= 2:
                    pe.wait_ge(aff_made, i - 1)
                for k in range(KD):
                    mm = pe.matmul(psum[0:r, 6 + i % 2, 0:EXPERTS], mixT[:, k, cols_of(i)], wr[:, k],
                                   start=(k == 0), stop=(k == KD - 1))
                mm.then_inc(aff_ps, 1)


def tile_rows(i):
    return P if i < TILES else NS


def tile_cols(i):
    return slice(i, SEQ, LC) if i < TILES else slice(SEQ, TOK)


WBUF = 4
WLEN = KD * 2 * FE + 2 * D
T_EXP, T_BUF, T_FIRST, T_N, T_LEN = 0, P, 2 * P, 2 * P + EXPERTS, 2 * P + EXPERTS + 8


def fetch_expert(sp, a, r, e, s):
    dst = r["wx"][:, s, 0:KD * 2 * FE].rearrange("p (k f) -> p k f", k=KD)
    for j, name in enumerate(("w_e1", "w_e3")):
        sp.dma_start(dst[:, :, j * FE:(j + 1) * FE],
                     a[name][0, bass.ds(e, 1)].rearrange("o (p k) f -> p (o k) f", k=KD)
                     ).then_inc(r["wx_land"][s], 16)
    sp.dma_start(r["wx"][:, s, KD * 2 * FE:].rearrange("p (k n) -> p k n", k=2),
                 a["w_e2"][0, bass.ds(e, 1)].rearrange("o (p k) n -> p (o k) n", k=2)
                 ).then_inc(r["wx_land"][s], 16)


def shared_buffers(nc, ctx):
    def sb(name, shape):
        return ctx.enter_context(nc.sbuf_tensor(name, shape, F32, side="right"))

    return {"w13": sb("ws13", [P, KD, 2 * FE]), "w2": sb("ws2", [P, 2, D]), "br": sb("br", [P, EXPERTS])}


def load_shared(sp, a, w, land):
    for j, n in enumerate(("w_s1", "w_s3")):
        sp.dma_start(w["w13"][:, :, j * FE:(j + 1) * FE], a[n][0].rearrange("(p k) f -> p k f", k=KD)
                     ).then_inc(land, 16)
    sp.dma_start(w["w2"][:], a["w_s2"][0].rearrange("(p k) n -> p k n", k=2)).then_inc(land, 16)
    sp.dma_start(w["br"][:], a["b_router"][0].partition_broadcast(P)).then_inc(land, 16)


def route_phase(nc, cst, psum, a, scr, mixT, aff, r, w_shared):
    NTL = TILES + 1
    NE = NTL * EXPERTS
    with ExitStack() as ctx:
        def sb(name, shape, dt=F32):
            return ctx.enter_context(nc.sbuf_tensor(name, shape, dt))

        def sem(name):
            return new_sem(nc, name)

        w13, w2, br = w_shared["w13"], w_shared["w2"], w_shared["br"]
        sa, hid, hidT = sb("sa", [P, 2, FE]), sb("hid", [P, 2, FE]), sb("hidT", [P, 2, 2, P])
        ysh = sb("ysh", [P, 2, D])
        sc, sel, eq, rk, gate, slots, tmp, fresh = (sb(n, [P, NTL, EXPERTS]) for n in (
            "sc", "sel_e", "eq_e", "rk", "gate", "slots", "tmp_e", "fresh"))
        v8 = sb("v8", [P, NTL, 8])
        n1, n2 = sb("n1", [P, NTL]), sb("n2", [P, NTL])
        tot, offs = sb("tot", [P, NTL, EXPERTS]), sb("offs", [P, NTL + 1, EXPERTS])
        nb, inc, exc = (sb(n, [P, EXPERTS]) for n in ("nb", "inc", "exc"))
        one = sb("one_r", [P, EXPERTS])
        choice = sb("choice", [P, 2, TOPE, NTL])
        idx = sb("idx", [P, TOPE, NTL], I32)
        meta = sb("meta", [P, NTL, TOPE, 2])
        tok_i, tok_f = sb("tok_i", [P, NTL], I32), sb("tok_f", [P, NTL])
        dflt_i = sb("dflt_i", [P, NBLK], I32)
        dflt = sb("dflt", [P, NBLK, 2])
        part_i, part_f = sb("part_i", [P, 1], I32), sb("part_f", [P, 1])
        eb, ebi = sb("eb", [P, 1]), sb("ebi", [P, 2], I32)
        firsti = sb("firsti", [1, EXPERTS + 8], I32)
        st = sb("slot_tab", [NBLK, BLK, 2])

        iota_made, aff_sig, dflt_made, dflt_out = (sem(n) for n in (
            "iota_made", "aff_sig", "dflt_made", "dflt_out"))
        up_ps, silu, hid_made, hT_ps, hT_made, dn_ps, y_read = (sem(n) for n in (
            "sh_up", "sh_silu", "sh_hid", "sh_hT", "sh_hTm", "sh_dn", "sh_y"))
        y_out = [sem(f"sh_out{i}") for i in range(2)]
        sel_made, cnt_ps, tab_made, tab_out, tab_in, meta_made, scattered, st_land, st_ps = (sem(n) for n in (
            "chosen", "cnt_ps", "steer_made", "steer_out", "steer_in", "meta_made", "scattered", "st_land", "st_ps"))
        aff_clear = sem("aff_clear")
        chain = Chain(sem("route_chain"))
        block = ctx.enter_context(nc.Block())

        @block.sync
        def _(sp):
            for e in range(WBUF):
                fetch_expert(sp, a, r, e, e)
            sp.wait_ge(dflt_made, 1)
            sp.dma_start(scr["slots"].rearrange("(p j) c -> p j c", p=P), dflt[:]).then_inc(dflt_out, 16)
            for i in range(NTL):
                sp.wait_ge(y_read, i + 1)
                sp.dma_start(scr["acc"][i * P:i * P + tile_rows(i)], ysh[0:tile_rows(i), i % 2]
                             ).then_inc(y_out[i % 2], 16)
                if i == 0:
                    sp.wait_ge(tab_made, 1)
                    for dst, src in ((T_EXP, ebi[:, 0:1]), (T_BUF, ebi[:, 1:2])):
                        sp.dma_start(scr["tab"][0, dst:dst + P].rearrange("(p o) -> p o", o=1), src,
                                     allow_slow_non_contiguous=True).then_inc(tab_out, 16)
                    sp.dma_start(scr["tab"][:, T_FIRST:T_LEN], firsti[:]).then_inc(tab_out, 16)
                    sp.wait_ge(tab_out, 48)
                    sp.dma_start(r["tab"][:], scr["tab"]).then_inc(tab_in, 16)
            sp.wait_ge(scattered, 16 * TOPE * NTL)
            sp.dma_start(st[:], scr["slots"].rearrange("(b p) c -> b p c", p=BLK)).then_inc(st_land, 16)
            sp.wait_ge(y_out[0], 16 * 5)
            sp.wait_ge(y_out[1], 16 * 4)
            sp.wait_ge(tab_in, 16)

        @block.gpsimd
        def _(pool):
            nc.gpsimd.iota(tok_i[:], pattern=[[P, NTL]], base=0, channel_multiplier=1)
            nc.gpsimd.iota(part_i[:], pattern=[[0, 1]], base=0, channel_multiplier=1)
            nc.gpsimd.iota(dflt_i[:], pattern=[[1, NBLK]], base=0, channel_multiplier=NBLK).then_inc(iota_made, 1)
            pool.wait_ge(dflt_out, 16)
            pool.wait_ge(meta_made, 1)
            for i in range(NTL):
                n = tile_rows(i)
                for k in range(TOPE):
                    nc.gpsimd.indirect_dma_start(
                        out=scr["slots"], out_offset=bass.IndirectOffsetOnAxis(ap=idx[0:n, k, i:i + 1], axis=0),
                        in_=meta[0:n, i, k], in_offset=None).then_inc(scattered, 16)
            pool.wait_ge(scattered, 16 * TOPE * NTL)

        @block.scalar
        def _(act):
            act.wait_ge(aff_clear, 1)
            nc.scalar.activation(aff[:], aff[:], ACT.Sigmoid).then_inc(aff_sig, 1)

            def silu_of(i):
                n = tile_rows(i)
                act.wait_ge(up_ps, i + 1)
                if i >= 2:
                    act.wait_ge(hid_made, i - 1)
                nc.scalar.activation(sa[0:n, i % 2], psum[0:n, i % 2, 0:FE], ACT.Silu).then_inc(silu, 1)

            silu_of(0)
            for i in range(NTL):
                n = tile_rows(i)
                if i + 1 < NTL:
                    silu_of(i + 1)
                act.wait_ge(hT_ps, i + 1)
                if i >= 2:
                    act.wait_ge(dn_ps, i - 1)
                nc.scalar.copy(hidT[:, i % 2, :, 0:n], psum[:, 2, 0:2 * P].rearrange(
                    "p (k c) -> p k c", k=2)[:, :, 0:n]).then_inc(hT_made, 1)
                act.wait_ge(dn_ps, i + 1)
                if i >= 2:
                    act.wait_ge(y_out[i % 2], 16 * (i // 2))
                nc.scalar.copy(ysh[0:n, i % 2], psum[0:n, 4:6, :].rearrange("p a b -> p (a b)")).then_inc(y_read, 1)

        @block.vector
        def _(dve):
            def seq(ins):
                dve.wait_ge(chain.sem, chain.did(ins))

            def hidden(i):
                n = tile_rows(i)
                dve.wait_ge(silu, i + 1)
                if i >= 2:
                    dve.wait_ge(hT_ps, i - 1)
                nc.vector.tensor_tensor(hid[0:n, i % 2], sa[0:n, i % 2], psum[0:n, i % 2, FE:2 * FE], ALU.mult
                                        ).then_inc(hid_made, 1)

            flat = "p t e -> p (t e)"
            all_ = [P, NTL, EXPERTS]
            nc.vector.memset(aff[NS:P, TILES], 0.0).then_inc(aff_clear, 1)
            dve.wait_ge(iota_made, 1)
            seq(nc.vector.tensor_scalar(dflt_i[:], dflt_i[:], BLK - 1, None, ALU.bitwise_and))
            nc.vector.memset(dflt[:], 0.0)
            seq(nc.vector.memset(fresh[:], 1.0))
            nc.vector.tensor_copy(part_f[:], part_i[:])
            nc.vector.tensor_copy(tok_f[:], tok_i[:])
            nc.vector.memset(one[:], 1.0)
            seq(nc.vector.memset(fresh[:, :, 0:1], 0.0))
            nc.vector.tensor_scalar(dflt[:, :, 0], dflt_i[:], float(TRASH), None, ALU.add).then_inc(dflt_made, 1)
            dve.wait_ge(aff_sig, 1)
            seq(nc.vector.tensor_tensor(sc[:], aff[:], br[:].unsqueeze(1).broadcast_to(all_), ALU.add))
            for i in range(NTL):
                last = nc.vector.max(v8[:, i], sc[:, i])
            seq(last)
            least = v8[:, :, TOPE - 1:TOPE].broadcast_to(all_)
            nc.vector.tensor_tensor(eq[:], sc[:], least, ALU.is_equal)
            seq(nc.vector.tensor_tensor(sel[:], sc[:], least, ALU.is_gt))
            seq(nc.vector.tensor_reduce(n1[:], sel[:], AX, ALU.add))
            nc.vector.tensor_scalar(n2[:], n1[:], -1.0, float(TOPE), ALU.mult, ALU.add)
            seq(nc.vector.tensor_tensor_scan(rk[:].rearrange(flat), fresh[:].rearrange(flat),
                                             eq[:].rearrange(flat), 0.0, ALU.mult, ALU.add))
            seq(nc.vector.tensor_tensor(rk[:], rk[:], n2[:].unsqueeze(2).broadcast_to(all_), ALU.is_le))
            seq(nc.vector.tensor_tensor(eq[:], eq[:], rk[:], ALU.mult))
            seq(nc.vector.tensor_tensor(sel[:], sel[:], eq[:], ALU.add))
            nc.vector.memset(sel[NS:P, TILES], 0.0).then_inc(sel_made, 1)
            hidden(0)
            dve.wait_ge(sel_made, 1)
            seq(nc.vector.tensor_tensor(gate[:], aff[:], sel[:], ALU.mult))
            seq(nc.vector.tensor_reduce(n1[:], gate[:], AX, ALU.add))
            seq(nc.vector.tensor_scalar(n1[:], n1[:], 1e-30, None, ALU.max))
            seq(nc.vector.reciprocal(n1[:], n1[:]))
            seq(nc.vector.tensor_tensor(gate[:], gate[:], n1[:].unsqueeze(2).broadcast_to(all_), ALU.mult))
            seq(nc.vector.tensor_scalar(gate[:], gate[:], ROUTED_SCALE, None, ALU.mult))
            dve.wait_ge(cnt_ps, 1)
            nc.vector.tensor_copy(tot[:, 0:TILES].rearrange(flat), psum[:, 7, :])
            nc.vector.memset(offs[:, 0], 0.0)
            seq(nc.vector.tensor_copy(tot[:, TILES], psum[:, 6, EXPERTS:2 * EXPERTS]))
            for i in range(NTL):
                seq(nc.vector.tensor_tensor(offs[:, i + 1], offs[:, i], tot[:, i], ALU.add))
            hidden(1)
            count = offs[:, NTL]
            seq(nc.vector.tensor_scalar(nb[:], count, 0.0, None, ALU.is_gt))
            for i in range(1, -(-TOK // BLK)):
                seq(nc.vector.scalar_tensor_tensor(nb[:], count, float(i * BLK), nb[:], ALU.is_gt, ALU.add))
            seq(nc.vector.tensor_tensor_scan(inc[:], one[:], nb[:], 0.0, ALU.mult, ALU.add))
            seq(nc.vector.tensor_tensor(exc[:], inc[:], nb[:], ALU.subtract))
            seq(nc.vector.tensor_scalar(nb[:], inc[:], part_f[:], 0.0, ALU.is_le, ALU.add, accum_out=eb[:]))
            seq(nc.vector.tensor_copy(ebi[:, 0:1], eb[:]))
            nc.vector.memset(firsti[:], 0)
            seq(nc.vector.tensor_scalar(ebi[:, 1:2], ebi[:, 0:1], WBUF - 1, None, ALU.bitwise_and))
            seq(nc.vector.tensor_copy(firsti[:, 0:EXPERTS], exc[0:1]))
            nc.vector.tensor_copy(firsti[:, EXPERTS:EXPERTS + 1], inc[0:1, EXPERTS - 1:]).then_inc(tab_made, 1)
            hidden(2)
            seq(nc.vector.tensor_scalar(exc[:], exc[:], float(BLK), None, ALU.mult))
            seq(nc.vector.tensor_tensor(slots[:], offs[:, 0:NTL], exc[:].unsqueeze(1).broadcast_to(all_), ALU.add))
            seq(nc.vector.tensor_tensor(slots[:, 0:TILES].rearrange(flat), slots[:, 0:TILES].rearrange(flat),
                                        psum[:, 3, :], ALU.add))
            seq(nc.vector.tensor_tensor(slots[:, TILES], slots[:, TILES], psum[:, 6, 0:EXPERTS], ALU.add))
            seq(nc.vector.tensor_tensor(slots[:], slots[:], sel[:], ALU.mult))
            seq(nc.vector.tensor_tensor_scan(rk[:].rearrange(flat), fresh[:].rearrange(flat),
                                             sel[:].rearrange(flat), 0.0, ALU.mult, ALU.add))
            for k in range(TOPE):
                for out, src in ((tmp, slots), (sc, gate)):
                    last = nc.vector.scalar_tensor_tensor(out[:].rearrange(flat), rk[:].rearrange(flat), float(k + 1),
                                                          src[:].rearrange(flat), ALU.is_equal, ALU.mult)
                seq(last)
                nc.vector.tensor_reduce(choice[:, 0, k], tmp[:], AX, ALU.add)
                seq(nc.vector.tensor_reduce(choice[:, 1, k], sc[:], AX, ALU.add))
                if k == 2:
                    hidden(3)
            nc.vector.tensor_copy(idx[:], choice[:, 0])
            nc.vector.tensor_copy(meta[:, :, :, 0], tok_f[:].unsqueeze(2).broadcast_to([P, NTL, TOPE]))
            nc.vector.tensor_copy(meta[:, :, :, 1], choice[:, 1].rearrange("p k t -> p t k")).then_inc(meta_made, 1)
            for i in range(4, NTL):
                hidden(i)
            nc.vector.memset(r["slot_tok"][:, NBLK:], 0)
            nc.vector.memset(r["slot_gate"][:, NBLK:], 0.0)
            dve.wait_ge(st_ps, 1)
            nc.vector.tensor_copy(r["slot_tok"][:, 0:NBLK], psum[:, 6, 0:NBLK])
            nc.vector.tensor_copy(r["slot_gate"][:, 0:NBLK], psum[:, 6, P:P + NBLK])

        @block.tensor
        def _(pe):
            def up(i):
                n = tile_rows(i)
                if i >= 2:
                    pe.wait_ge(hid_made, i - 1)
                for k in range(KD):
                    mm = pe.matmul(psum[0:n, i % 2, :], mixT[:, k, tile_cols(i)], w13[:, k],
                                   start=(k == 0), stop=(k == KD - 1))
                mm.then_inc(up_ps, 1)

            up(0)
            for i in range(NTL):
                n = tile_rows(i)
                if i + 1 < NTL:
                    up(i + 1)
                if i == 0:
                    pe.wait_ge(sel_made, 1)
                    main = sel[:, 0:TILES].rearrange("p t e -> p (t e)")
                    pe.matmul(psum[:, 3, :], cst["before"][:], main, start=True, stop=True)
                    pe.matmul(psum[:, 6, 0:EXPERTS], cst["before"][:], sel[:, TILES], start=True, stop=True)
                    pe.matmul(psum[:, 7, :], cst["ones"][:], main, start=True, stop=True)
                    pe.matmul(psum[:, 6, EXPERTS:2 * EXPERTS], cst["ones"][:], sel[:, TILES],
                              start=True, stop=True).then_inc(cnt_ps, 1)
                pe.wait_ge(hid_made, i + 1)
                if i >= 1:
                    pe.wait_ge(hT_made, i)
                for k in range(2):
                    mm = pe.transpose(psum[:, 2, k * P:k * P + n], hid[0:n, i % 2, k:FE:2], cst["ident"][0:n, 0:n])
                mm.then_inc(hT_ps, 1)
                pe.wait_ge(hT_made, i + 1)
                if i >= 1:
                    pe.wait_ge(y_read, i)
                for c in range(2):
                    for k in range(2):
                        mm = pe.matmul(psum[0:n, 4 + c, :], hidT[:, i % 2, k, 0:n], w2[:, k, c * 512:(c + 1) * 512],
                                       start=(k == 0), stop=(k == 1))
                mm.then_inc(dn_ps, 1)
            pe.wait_ge(st_land, 16)
            pe.wait_ge(meta_made, 1)
            pe.transpose(psum[:, 6, 0:NBLK], st[:, :, 0], cst["ident"][0:NBLK, 0:NBLK])
            pe.transpose(psum[:, 6, P:P + NBLK], st[:, :, 1], cst["ident"][0:NBLK, 0:NBLK]).then_inc(st_ps, 1)


def expert_phase(nc, cst, psum, a, scr, r, w_next):
    UNROLL = 4
    with ExitStack() as ctx:
        def sb(name, shape, dt=F32):
            return ctx.enter_context(nc.sbuf_tensor(name, shape, dt))

        def sem(name):
            return new_sem(nc, name)

        wx, w_land = r["wx"], r["wx_land"]
        hg = sb("hg", [P, UNROLL, D])
        hT = sb("hT_x", [P, 2, KD, P])
        sa, hid, hidT = sb("sa_x", [P, 2, FE]), sb("hid_x", [P, FE]), sb("hidT_x", [P, 2, P])
        y = sb("y_x", [P, D])
        gi, si = sb("gather_idx", [P, UNROLL], I32), sb("add_idx", [P, 2], I32)
        spare = sb("spare_x", [P, 2])
        ready = sem("weights_ready")
        hg_land = [sem(f"hg_land{i}") for i in range(UNROLL)]
        idx_put = sem("idx_put")
        hT_ps, hT_dve, hT_act, up_ps, silu, hid_made, hidT_ps, hidT_made, dn_ps, y_dve, y_act, added = (
            sem(n) for n in ("x_hT", "x_hT_dve", "x_hT_act", "x_up", "x_silu", "x_hid", "x_hidT_ps", "x_hidT",
                             "x_dn", "x_y_dve", "x_y_act", "x_added"))
        block = ctx.enter_context(nc.Block())
        tab = r["tab"]

        def load(eng, place, most):
            return eng.value_load(tab[0:1, bass.ds(place, 1)], min_val=0, max_val=most)

        def blocks(eng, body):
            n = load(eng, T_N, NBLK)
            with eng.Fori(0, -(-NBLK // UNROLL)) as turn:
                for j in range(UNROLL):
                    b = UNROLL * turn + j
                    with eng.If(b < n):
                        body(b, j, turn, n)

        @block.sync
        def _(sp):
            for e in range(2):
                sp.wait_ge(w_land[e], 48)
                sp.sem_inc(ready, 1)
            with sp.Fori(1, EXPERTS // WBUF) as turn:
                for s in range(WBUF):
                    e = WBUF * turn + s
                    q = (s + 2) % WBUF
                    sp.wait_ge(w_land[q], 48 * (turn + 1) if s >= 2 else 48 * turn)
                    sp.sem_inc(ready, 1)
                    before = sp.value_load(tab[0:1, bass.ds(T_FIRST + e - WBUF + 1, 1)], min_val=0, max_val=NBLK)
                    sp.wait_ge(dn_ps, before + 1)
                    fetch_expert(sp, a, r, e, s)
            load_final(sp, a, scr, w_next)
            for s in (2, 3):
                sp.wait_ge(w_land[s], 48 * EXPERTS // WBUF)
                sp.sem_inc(ready, 1)

        @block.gpsimd
        def _(pool):
            def gather_index(b, j):
                nc.gpsimd.tensor_copy(gi[:, j:j + 1], r["slot_tok"][:, bass.ds(b, 1)]).then_inc(idx_put, 1)

            def gather(j):
                nc.gpsimd.indirect_dma_start(
                    out=hg[:, j], out_offset=None, in_=scr["h2"],
                    in_offset=bass.IndirectOffsetOnAxis(ap=gi[:, j:j + 1], axis=0)).then_inc(hg_land[j], 16)

            def pause():
                nc.gpsimd.tensor_tensor(spare[:, 1:2], spare[:, 0:1], spare[:, 0:1], ALU.add).then_inc(idx_put, 1)

            pool.dma_start(spare[:], scr["acc"][TRASH:TRASH + P, 0:2]).then_inc(added, 16)
            for j in range(3):
                gather_index(j, j)
            pool.wait_ge(idx_put, 3)
            pool.wait_ge(added, 16)
            for j in range(3):
                gather(j)

            def body(b, j, turn, n):
                ahead = (j + 3) % UNROLL
                pool.wait_ge(hT_ps, b + 1)
                gather_index(b + 3, ahead)
                pool.wait_ge(idx_put, 4 * b + 4)
                pause()
                with pool.If(b + 3 < n):
                    gather(ahead)
                pool.wait_ge(added, 16 * b + 16)
                nc.gpsimd.tensor_copy(si[:, j % 2:j % 2 + 1], r["slot_tok"][:, bass.ds(b, 1)]).then_inc(idx_put, 1)
                pool.wait_ge(idx_put, 4 * b + 6)
                pool.wait_ge(y_dve, b + 2)
                pool.wait_ge(y_act, b + 2)
                pause()
                nc.gpsimd.indirect_dma_start(
                    out=scr["acc"], out_offset=bass.IndirectOffsetOnAxis(ap=si[:, j % 2:j % 2 + 1], axis=0),
                    in_=y[:], in_offset=None, compute_op=ALU.add).then_inc(added, 16)

            blocks(pool, body)
            n = load(pool, T_N, NBLK)
            pool.wait_ge(added, 16 * n + 16)

        def read_hT(eng, copy, half, b_done, par, done):
            eng.wait_ge(hT_ps, b_done + 1)
            copy(hT[:, par, 4 * half:4 * half + 4], psum[:, half, :].rearrange("p (k c) -> p k c", k=4)
                 ).then_inc(done, 1)

        @block.scalar
        def _(act):
            def silu_of(par, done):
                act.wait_ge(up_ps, done)
                nc.scalar.activation(sa[:, par], psum[:, 2 + par, 0:FE], ACT.Silu).then_inc(silu, 1)

            nc.scalar.copy(y[:, 0:1], cst["ones"][:, 0:1]).then_inc(y_act, 1)
            read_hT(act, nc.scalar.copy, 1, 1, 0, hT_act)
            read_hT(act, nc.scalar.copy, 1, 2, 1, hT_act)
            silu_of(0, 1)

            def body(b, j, turn, n):
                par = j % 2
                act.wait_ge(hidT_ps, b + 2)
                nc.scalar.copy(hidT[:].rearrange("p k c -> p (k c)"), psum[:, 4, 0:2 * P]).then_inc(hidT_made, 1)
                with act.If(b + 1 < n):
                    silu_of(1 - par, b + 2)
                with act.If(b + 2 < n):
                    read_hT(act, nc.scalar.copy, 1, b + 3, par, hT_act)
                act.wait_ge(dn_ps, b + 2)
                act.wait_ge(added, 16 * b + 16)
                nc.scalar.activation(y[:, 0:512], psum[:, 5, :], ACT.Copy,
                                     scale=r["slot_gate"][:, bass.ds(b, 1)]).then_inc(y_act, 1)

            blocks(act, body)

        @block.vector
        def _(dve):
            def hidden(par, done):
                dve.wait_ge(silu, done)
                nc.vector.tensor_tensor(hid[:], sa[:, par], psum[:, 2 + par, FE:2 * FE], ALU.mult
                                        ).then_inc(hid_made, 1)

            nc.vector.memset(y[:, 512:D], 0.0).then_inc(y_dve, 1)
            read_hT(dve, nc.vector.tensor_copy, 0, 1, 0, hT_dve)
            read_hT(dve, nc.vector.tensor_copy, 0, 2, 1, hT_dve)
            hidden(0, 1)

            def body(b, j, turn, n):
                par = j % 2
                with dve.If(b + 2 < n):
                    read_hT(dve, nc.vector.tensor_copy, 0, b + 3, par, hT_dve)
                with dve.If(b + 1 < n):
                    dve.wait_ge(hidT_ps, b + 2)
                    hidden(1 - par, b + 2)
                dve.wait_ge(dn_ps, b + 2)
                dve.wait_ge(added, 16 * b + 16)
                nc.vector.tensor_scalar(y[:, 512:D], psum[:, 6, :], r["slot_gate"][:, bass.ds(b, 1)], None,
                                        ALU.mult).then_inc(y_dve, 1)

            blocks(dve, body)

        @block.tensor
        def _(pe):
            def turn_rows(j):
                return [pe.transpose(psum[:, k // 4, k % 4 * P:(k % 4 + 1) * P], hg[:, j, k:D:KD], cst["ident"][:])
                        for k in range(KD)]

            def up(b, par):
                e = pe.value_load(tab[0:1, bass.ds(T_EXP + b, 1)], min_val=0, max_val=EXPERTS - 1)
                s = pe.value_load(tab[0:1, bass.ds(T_BUF + b, 1)], min_val=0, max_val=WBUF - 1)
                pe.wait_ge(ready, e + 1)
                pe.wait_ge(hT_dve, b + 1)
                pe.wait_ge(hT_act, b + 1)
                for k in range(KD):
                    mm = pe.matmul(psum[:, 2 + par, :], hT[:, par, k],
                                   wx[:, bass.ds(s, 1), k * 2 * FE:(k + 1) * 2 * FE].rearrange("p o f -> p (o f)"),
                                   start=(k == 0), stop=(k == KD - 1))
                mm.then_inc(up_ps, 1)

            pe.wait_ge(hg_land[0], 16)
            first = turn_rows(0)
            first[0].then_inc(hidT_ps, 1)
            first[1].then_inc(dn_ps, 1)
            first[-1].then_inc(hT_ps, 2)
            pe.wait_ge(hg_land[1], 16)
            pe.wait_ge(hT_dve, 1)
            pe.wait_ge(hT_act, 1)
            turn_rows(1)[-1].then_inc(hT_ps, 1)
            up(0, 0)

            def body(b, j, turn, n):
                par = j % 2
                s = pe.value_load(tab[0:1, bass.ds(T_BUF + b, 1)], min_val=0, max_val=WBUF - 1)
                with pe.If(b + 1 < n):
                    up(b + 1, 1 - par)
                pe.wait_ge(hid_made, b + 1)
                for k in range(2):
                    mm = pe.transpose(psum[:, 4, k * P:(k + 1) * P], hid[:, k:FE:2], cst["ident"][:])
                mm.then_inc(hidT_ps, 1)
                with pe.If(b + 2 < n):
                    after = (j + 2) % UNROLL
                    pe.wait_ge(hg_land[after], 16 * turn + (32 if after < 2 else 16))
                    turn_rows(after)[-1].then_inc(hT_ps, 1)
                pe.wait_ge(hidT_made, b + 1)
                pe.wait_ge(y_dve, b + 1)
                pe.wait_ge(y_act, b + 1)
                for c in range(2):
                    for k in range(2):
                        at = KD * 2 * FE + k * D + c * 512
                        mm = pe.matmul(psum[:, 5 + c, :], hidT[:, k],
                                       wx[:, bass.ds(s, 1), at:at + 512].rearrange("p o f -> p (o f)"),
                                       start=(k == 0), stop=(k == 1))
                mm.then_inc(dn_ps, 1)

            blocks(pe, body)


def final_buffers(nc, ctx):
    def sb(name, shape):
        return ctx.enter_context(nc.sbuf_tensor(name, shape, F32))

    return {"g2": sb("g2", [P, 2, D]), "lg": sb("lg2", [P, D]), "lb": sb("lb2", [P, D]),
            "x1": sb("x1f", [P, TILES + 1, D]), "land": new_sem(nc, "f_mod")}


F_LOADS = 1 + NB + 2 + 2


def load_final(sp, a, scr, w):
    for s in range(2):
        load_rows(sp, w["g2"][0:P if s == 0 else NS, s], scr["mod"], G2, s, w["land"])
    sp.dma_start(w["lg"][:], a["ln2_g"][0].partition_broadcast(P)).then_inc(w["land"], 16)
    sp.dma_start(w["lb"][:], a["ln2_b"][0].partition_broadcast(P)).then_inc(w["land"], 16)
    sp.dma_start(w["x1"][:, 0:TILES], scr["x1"][0:SEQ].rearrange("(t p) d -> p t d", p=P)).then_inc(w["land"], 16)
    sp.dma_start(w["x1"][0:NS, TILES], scr["x1"][SEQ:TOK]).then_inc(w["land"], 16)


def final_phase(nc, cst, a, o, scr, w):
    NTL = TILES + 1
    with ExitStack() as ctx:
        def sb(name, shape, dt=F32):
            return ctx.enter_context(nc.sbuf_tensor(name, shape, dt))

        def sem(name):
            return new_sem(nc, name)

        g2, lg, lb, x1 = w["g2"], w["lg"], w["lb"], w["x1"]
        f, sq = sb("f", [P, NTL, D]), sb("sq3", [P, D])
        st = sb("st2", [P, NTL, 4])
        f_land = [sem(f"f_in{i}") for i in range(NTL)]
        out_done = sem("f_out")
        x_made, sq_made, var_made, root, gain, done = (sem(n) for n in ("f_x", "f_sq", "f_var", "f_root", "f_gain",
                                                                        "f_done"))
        chain = Chain(sem("f_chain"))
        block = ctx.enter_context(nc.Block())

        @block.sync
        def _(sp):
            for i in range(NTL):
                n = tile_rows(i)
                sp.dma_start(f[0:n, i], scr["acc"][i * P:i * P + n]).then_inc(f_land[i], 16)
            for i in range(NTL):
                n = tile_rows(i)
                sp.wait_ge(done, i + 1)
                dst = o["y_prompt"][0].rearrange("(c s) d -> s c d", s=LC)[i] if i < TILES else \
                    o["y_sample"].rearrange("b t d -> (b t) d")
                sp.dma_start(dst, x1[0:n, i]).then_inc(out_done, 16)
            sp.wait_ge(out_done, 16 * NTL)

        @block.gpsimd
        def _(pool):
            for i in range(NTL):
                n = tile_rows(i)
                pool.wait_ge(gain, i + 1)
                nc.gpsimd.tensor_tensor(x1[0:n, i], x1[0:n, i], lb[0:n], ALU.add).then_inc(done, 1)

        @block.scalar
        def _(act):
            for i in range(NTL):
                n = tile_rows(i)
                act.wait_ge(x_made, i + 1)
                if i:
                    act.wait_ge(sq_made, 2 * i)
                nc.scalar.activation(st[0:n, i, 1:2], st[0:n, i, 0:1], ACT.Copy, scale=-1.0 / D
                                     ).then_inc(sq_made, 1)
                act.wait_ge(sq_made, 2 * i + 1)
                nc.scalar.activation(sq[0:n], x1[0:n, i], ACT.Square, bias=st[0:n, i, 1:2],
                                     accum_out=st[0:n, i, 2:3]).then_inc(sq_made, 1)
                act.wait_ge(var_made, i + 1)
                nc.scalar.activation(st[0:n, i, 3:4], st[0:n, i, 2:3], ACT.Sqrt).then_inc(root, 1)

        @block.vector
        def _(dve):
            def seq(ins):
                dve.wait_ge(chain.sem, chain.did(ins))

            def front(i):
                n, s = tile_rows(i), i // TILES
                dve.wait_ge(f_land[i], 16)
                seq(nc.vector.tensor_tensor(f[0:n, i], f[0:n, i], g2[0:n, s], ALU.mult))
                nc.vector.scalar_tensor_tensor(x1[0:n, i], x1[0:n, i], ALPHA, f[0:n, i], ALU.mult,
                                               ALU.add, accum_out=st[0:n, i, 0:1]).then_inc(x_made, 1)

            dve.wait_ge(w["land"], 16 * F_LOADS)
            front(0)
            for i in range(NTL):
                n = tile_rows(i)
                if i + 1 < NTL:
                    front(i + 1)
                dve.wait_ge(sq_made, 2 * i + 2)
                nc.vector.tensor_scalar(st[0:n, i, 2:3], st[0:n, i, 2:3], 1.0 / D, EPS, ALU.mult, ALU.add
                                        ).then_inc(var_made, 1)
                dve.wait_ge(root, i + 1)
                seq(nc.vector.reciprocal(st[0:n, i, 3:4], st[0:n, i, 3:4]))
                seq(nc.vector.tensor_scalar(x1[0:n, i], x1[0:n, i], st[0:n, i, 1:2], st[0:n, i, 3:4],
                                            ALU.add, ALU.mult))
                nc.vector.tensor_tensor(x1[0:n, i], x1[0:n, i], lg[0:n], ALU.mult).then_inc(gain, 1)


def hymba_step(nc, a, o):
    scr = {}
    HELD.clear()

    def dram(name, shape, dt=F32):
        scr[name] = nc.dram_tensor("scr_" + name, shape, dt).ap()

    dram("mod", (1 + NB, 6 * D))
    dram("ys", (NS, D_SSM))
    dram("os", (NS, D_SSM))
    dram("x1", (ROWS, D))
    dram("slots", (SLOTS, 2))
    dram("tab", (1, T_LEN), I32)
    dram("h2", (TRASH + P, D))
    dram("acc", (TRASH + P, D))
    with ExitStack() as ctx:
        def sb(name, shape, dt=F32):
            return ctx.enter_context(nc.sbuf_tensor(name, shape, dt))

        psum = ctx.enter_context(nc.psum_tensor("psum", [P, 8, 512], F32))
        cst = {"ident": sb("ident", [P, P]), "ones": sb("ones", [P, P]), "before": sb("before", [P, P])}
        modT = sb("modT", [P, 2, KD, 1 + NB])
        make_constants(nc, cst)
        mix_ctx = ctx.enter_context(ExitStack())
        early, out_ctx = ctx.enter_context(ExitStack()), ctx.enter_context(ExitStack())
        cf = early.enter_context(nc.sbuf_tensor("cf", [P, NQ, PAIRS], F32, side="right"))
        w_ctx = ctx.enter_context(ExitStack())
        w_in = w_ctx.enter_context(nc.sbuf_tensor("w", [P, KD, C_END], F32, side="right"))
        w_land = new_sem(nc, "w_land")
        ada_phase(nc, cst, psum, a, scr, modT, cf, w_in, w_land)
        with ExitStack() as mixers:
            def sbm(name, shape, dt=F32):
                return mixers.enter_context(nc.sbuf_tensor(name, shape, dt))

            att = sbm("att", [P, TILES + 1, D_SSM])
            t = {"u": sbm("u", [P, GROUPS, LC, GCH]), "us": sbm("us", [NS, D_SSM]),
                 "spare": att[:].rearrange("p t c -> p (t c)"), "rows_out": new_sem(nc, "rows_out")}
            with ExitStack() as projected:
                def sbp(name, shape, dt=F32):
                    return projected.enter_context(nc.sbuf_tensor(name, shape, dt))

                t |= {"qT": sbp("qT", [P, 4, TOK]), "kT": sbp("kT", [P, 2, TOK]), "qiT": sbp("qiT", [P, 2, TOK]),
                      "kiT": sbp("kiT", [P, 1, TOK]), "v": sbp("v", [P, TILES + 1, KVH * HD]),
                      "kiwi": sbp("kiwi", [P, TILES + 1, IDX + IH])}
                project_phase(nc, cst, psum, a, o, modT, t, w_in, w_land)
                w_ctx.close()
                with ExitStack() as ssm:
                    def sbs(name, shape, dt=F32):
                        return ssm.enter_context(nc.sbuf_tensor(name, shape, dt))

                    s = {"toep": sbs("toep", [P, GROUPS, LC, GCH]), "wT": sbs("ssm_wT", [P, 2, PAIRS, P]),
                         "ca": sbs("ssm_ca", [P, 2, PAIRS, LC, GCH]), "rot": sbs("rot", [P, 2, PAIRS, CH]),
                         "r8": sbs("r8", [P, PAIRS]), "a8": sbs("a8", [P, 2, PAIRS]), "spare": t["spare"], "cf": cf,
                         "rows_out": t["rows_out"]}
                    ssm_tables_phase(nc, cst, psum, a, s)
                    early.close()
                    s["uc"] = t["spare"][:, 0:GROUPS * CHS].rearrange("p (g c) -> p g c", g=GROUPS)
                    ssm_input_phase(nc, cst, psum, t, s)
                    ssm_scan_phase(nc, cst, psum, a, o, scr, t, s)
                clear_sems(nc)
                x = {"gidx": sbp("gidx", [P, NB], I32),
                     "pbias": sbp("pbias", [P, score_off(TILES)], BF16), "sbias": sbp("sbias", [NS, KEYS], BF16)}
                with ExitStack() as scores:
                    x["psc"] = scores.enter_context(nc.sbuf_tensor("psc", [P, score_off(TILES)], F32))
                    x["ssc"] = scores.enter_context(nc.sbuf_tensor("ssc", [NS, KEYS], F32))
                    x["find"] = search_buffers(nc, scores)
                    index_phase(nc, cst, psum, a, t, x)
                    prompt_attention_phase(nc, cst, psum, t, x, att)
                sample_attention_phase(nc, cst, psum, a, scr, t, x)
            clear_sems(nc)
            mixT = mix_ctx.enter_context(nc.sbuf_tensor("mixT", [P, KD, TOK], F32, side="right"))
            w_shared = shared_buffers(nc, mix_ctx)
            w_out = out_buffers(nc, out_ctx)
            mix_phase(nc, cst, psum, a, scr, t, att, mixT, w_out)
        aff = sb("aff", [P, TILES + 1, EXPERTS])
        out_phase(nc, cst, psum, a, scr, mixT, aff, w_out, w_shared)
        out_ctx.close()
        clear_sems(nc)
        r = {"tab": sb("tab", [1, T_LEN], I32), "slot_tok": sb("slot_tok", [P, P], I32),
             "slot_gate": sb("slot_gate", [P, P]), "wx": sb("wx", [P, WBUF, WLEN]),
             "wx_land": [new_sem(nc, f"wx_land{i}") for i in range(WBUF)]}
        route_phase(nc, cst, psum, a, scr, mixT, aff, r, w_shared)
        mix_ctx.close()
        w_final = final_buffers(nc, ctx)
        expert_phase(nc, cst, psum, a, scr, r, w_final)
        final_phase(nc, cst, a, o, scr, w_final)
    return scr


_INS = ["x_prompt", "x_sample", "c_prompt", "c_sample", "cache_k", "cache_v", "cache_kidx", "state_ssm_re",
        "state_ssm_im", "page_table", "w_ada", "b_ada", "w_in", "ssm_a_re", "ssm_a_im", "ssm_log_dt",
        "ssm_b_re", "ssm_b_im", "ssm_c_re", "ssm_c_im", "ssm_d", "w_glu", "b_glu", "g_ssm_out", "g_att_out",
        "w_out", "ln1_g", "ln1_b", "w_router", "b_router", "w_e1", "w_e3", "w_e2", "w_s1", "w_s3", "w_s2",
        "ln2_g", "ln2_b"]
_OUTS = [("y_prompt", (1, SEQ, D)), ("y_sample", (NB, NT, D)),
         ("k_prompt", (1, 1, SEQ, KVH, HD)), ("v_prompt", (1, 1, SEQ, KVH, HD)), ("ki_prompt", (1, 1, SEQ, IDX)),
         ("re_prompt", (1, 1, GROUPS, STATES)), ("im_prompt", (1, 1, GROUPS, STATES)),
         ("k_sample", (1, NB, NT, KVH, HD)), ("v_sample", (1, NB, NT, KVH, HD)), ("ki_sample", (1, NB, NT, IDX)),
         ("re_sample", (1, NB, GROUPS, STATES)), ("im_sample", (1, NB, GROUPS, STATES))]


def kernel(**inputs):
    import concourse.bacc as bacc
    from concourse.bass_utils import run_bass_kernel_spmd

    nc = bacc.Bacc("TRN2", target_bir_lowering=False, num_devices=1)
    arrays, a, o = {}, {}, {}
    for name in _INS:
        x = np.ascontiguousarray(inputs[name])
        arrays[f"in_{name}"] = x
        a[name] = nc.dram_tensor(f"in_{name}", x.shape, mybir.dt.from_np(x.dtype), kind="ExternalInput").ap()
    for name, shape in _OUTS:
        o[name] = nc.dram_tensor(f"out_{name}", shape, F32, kind="ExternalOutput").ap()
    hymba_step(nc, a, o)
    r = run_bass_kernel_spmd(nc, [arrays], core_ids=[0])
    return tuple(r.results[0][f"out_{name}"] for name, _ in _OUTS)
```
